# Optimizing a Trainium2 kernel written in Bass

```python
import math, functools
import jax, jax.numpy as jnp
from jax import lax
import numpy as np

D_MODEL = 1024
BATCH = 1
SEQ = 512
DEPTH = 1
DEC_BATCH = 8
DEC_SEQ = 4
PAST_LEN = 2048
PAGE_SIZE = 128

HEAD_DIM = 64
HEADS_PER_GROUP = 8
DIL_GROUPS = ((128, 1), (512, 4), (2048, 16))
N_DIL = len(DIL_GROUPS)
N_ATTN_HEADS = N_DIL * HEADS_PER_GROUP
ATTN_WIDTH = N_ATTN_HEADS * HEAD_DIM
ATTN_OUT = HEADS_PER_GROUP * HEAD_DIM
ROT_DIM = HEAD_DIM // 4
ROPE_THETA = 500000.0
QUERY_BLOCK = 128
CONV_WIDTH = D_MODEL
CONV_K = 3
N_EXPERT_GROUPS = 4
EXPERTS_PER_GROUP = 4
TOP_K_IN_GROUP = 2
D_EXPERT = 512
RMS_EPS = 1e-6
IN_COLS = 3 * CONV_WIDTH + 3 * ATTN_WIDTH + 2 * D_MODEL

kernel_name = 'hybrid_conv_dilattn_hmoe_step'

def rmsnorm(x, g):
    xf = x.astype(jnp.float32)
    y = xf * lax.rsqrt(jnp.mean(xf * xf, axis=-1, keepdims=True) + RMS_EPS)
    return (y * g.astype(jnp.float32)).astype(x.dtype)

def rope_partial(x, pos):
    half = ROT_DIM // 2
    inv_freq = jnp.power(jnp.float32(ROPE_THETA), -jnp.arange(half, dtype=jnp.float32) / half)
    ang = pos.astype(jnp.float32)[:, None] * inv_freq[None, :]
    cos = jnp.cos(ang)[None, :, None, :]
    sin = jnp.sin(ang)[None, :, None, :]
    xr = x[..., :ROT_DIM].astype(jnp.float32)
    x1, x2 = xr[..., :half], xr[..., half:]
    rot = jnp.concatenate([x1 * cos - x2 * sin, x2 * cos + x1 * sin], axis=-1).astype(x.dtype)
    return jnp.concatenate([rot, x[..., ROT_DIM:]], axis=-1)

def short_conv(u, conv_w, past):
    T = u.shape[1]
    ext = jnp.concatenate([past.astype(u.dtype), u], axis=1)
    y = conv_w[0] * ext[:, 0:T]
    for j in range(1, CONV_K):
        y = y + conv_w[j] * ext[:, j:j + T]
    return y, ext[:, T:]

def dilated_group_attn(q, k_rows, v_rows, q_rows, min_row, window, dilation):
    n_keys = window // dilation + 1
    idx = q_rows[:, None] - dilation * jnp.arange(n_keys, dtype=jnp.int32)[None, :]
    valid = idx >= min_row
    idx = jnp.maximum(idx, 0)
    kg = k_rows[:, idx].astype(jnp.float32)
    vg = v_rows[:, idx].astype(jnp.float32)
    s = jnp.einsum('bqhd,bqjhd->bhqj', q.astype(jnp.float32), kg) * (HEAD_DIM ** -0.5)
    s = jnp.where(valid[None, None], s, -jnp.inf)
    lse = jax.nn.logsumexp(s, axis=-1)
    p = jnp.exp(s - lse[..., None])
    o = jnp.einsum('bhqj,bqjhd->bqhd', p, vg)
    return o, lse

def dilated_mixture(q, ks, vs, rows, mins):
    outs, lses = [], []
    for g, (w, d) in enumerate(DIL_GROUPS):
        o, l = dilated_group_attn(q[:, :, g], ks[g], vs[g], rows[g], mins[g], w, d)
        outs.append(o)
        lses.append(l)
    wts = jax.nn.softmax(jnp.stack(lses), axis=0)
    wts = jnp.transpose(wts, (0, 1, 3, 2))[..., None]
    return jnp.sum(wts * jnp.stack(outs), axis=0)

def prompt_attention(q, k, v):
    B, S = q.shape[0], q.shape[1]
    kps = [jnp.pad(k[:, :, g], ((0, 0), (w, 0), (0, 0), (0, 0))) for g, (w, _) in enumerate(DIL_GROUPS)]
    vps = [jnp.pad(v[:, :, g], ((0, 0), (w, 0), (0, 0), (0, 0))) for g, (w, _) in enumerate(DIL_GROUPS)]
    mins = [w for (w, _) in DIL_GROUPS]

    def block(s0):
        qb = lax.dynamic_slice_in_dim(q, s0, QUERY_BLOCK, axis=1)
        rows = [w + s0 + jnp.arange(QUERY_BLOCK, dtype=jnp.int32) for (w, _) in DIL_GROUPS]
        return dilated_mixture(qb, kps, vps, rows, mins)

    starts = jnp.arange(S // QUERY_BLOCK, dtype=jnp.int32) * QUERY_BLOCK
    ob = lax.map(block, starts)
    o = jnp.moveaxis(ob, 0, 1).reshape(B, S, ATTN_OUT)
    new_kv = []
    for g, (w, _) in enumerate(DIL_GROUPS):
        L = min(w, S)
        new_kv += [k[:, S - L:, g], v[:, S - L:, g]]
    return o, new_kv

def sample_attention(caches, q, k, v):
    B, T = q.shape[0], q.shape[1]
    kcs, vcs, rows, mins, new_kv = [], [], [], [], []
    for g in range(N_DIL):
        kc = jnp.concatenate([caches[2 * g].astype(k.dtype), k[:, :, g]], axis=1)
        vc = jnp.concatenate([caches[2 * g + 1].astype(v.dtype), v[:, :, g]], axis=1)
        L = caches[2 * g].shape[1]
        kcs.append(kc)
        vcs.append(vc)
        rows.append(L + jnp.arange(T, dtype=jnp.int32))
        mins.append(0)
        new_kv += [kc[:, -L:], vc[:, -L:]]
    o = dilated_mixture(q, kcs, vcs, rows, mins)
    return o.reshape(B, T, ATTN_OUT), new_kv

def split_projection(z):
    sizes = (CONV_WIDTH, CONV_WIDTH, CONV_WIDTH, ATTN_WIDTH, ATTN_WIDTH, ATTN_WIDTH, D_MODEL, D_MODEL)
    offs = np.cumsum(sizes)[:-1].tolist()
    return jnp.split(z, offs, axis=-1)

def hier_moe(h, w_rg, b_rg, w_re, b_re, w1, w3, w2):
    B, T, _ = h.shape
    f32 = jnp.float32
    hf = h.astype(f32)
    g_logits = hf @ w_rg.astype(f32) + b_rg.astype(f32)
    g_prob = jax.nn.softmax(g_logits, axis=-1)
    g_onehot = jax.nn.one_hot(jnp.argmax(g_logits, axis=-1), N_EXPERT_GROUPS, dtype=f32)
    g_w = jnp.sum(g_prob * g_onehot, axis=-1, keepdims=True)
    e_logits = (hf @ w_re.astype(f32) + b_re.astype(f32)).reshape(B, T, N_EXPERT_GROUPS, EXPERTS_PER_GROUP)
    e_sel = jnp.sum(e_logits * g_onehot[..., None], axis=2)
    top_v, top_i = lax.top_k(e_sel, TOP_K_IN_GROUP)
    top_w = jax.nn.softmax(top_v, axis=-1) * g_w
    e_w = jnp.sum(jax.nn.one_hot(top_i, EXPERTS_PER_GROUP, dtype=f32) * top_w[..., None], axis=-2)
    comb = (g_onehot[..., None] * e_w[:, :, None, :]).astype(h.dtype)
    out = jnp.zeros_like(h)
    for g in range(N_EXPERT_GROUPS):
        a = jnp.einsum('btd,edf->btef', h, w1[g])
        b = jnp.einsum('btd,edf->btef', h, w3[g])
        hid = jax.nn.silu(a) * b * comb[:, :, g, :, None]
        out = out + jnp.einsum('btef,efd->btd', hid, w2[g])
    return out

def decoder_layer(x, c, pos, conv_past, attn_fn, w_ada, b_ada, norm1_g, norm2_g, w_in, conv_w,
                  w_conv_out, w_attn_out, w_o, w_rg, b_rg, w_re, b_re, w1, w3, w2):
    B, T, _ = x.shape
    mod = (jax.nn.silu(c) @ w_ada + b_ada)[:, None, :]
    sh1, sc1, gt1, sh2, sc2, gt2 = jnp.split(mod, 6, axis=-1)
    h = rmsnorm(x, norm1_g) * (1 + sc1) + sh1
    u_in, gate_c, gate_b, q, k, v, g_conv, g_attn = split_projection(h @ w_in)
    conv_y, conv_state = short_conv(gate_c * u_in, conv_w, conv_past)
    y_conv = (gate_b * conv_y) @ w_conv_out
    q = rope_partial(q.reshape(B, T, N_ATTN_HEADS, HEAD_DIM), pos).reshape(B, T, N_DIL, HEADS_PER_GROUP, HEAD_DIM)
    k = rope_partial(k.reshape(B, T, N_ATTN_HEADS, HEAD_DIM), pos).reshape(B, T, N_DIL, HEADS_PER_GROUP, HEAD_DIM)
    v = v.reshape(B, T, N_DIL, HEADS_PER_GROUP, HEAD_DIM)
    attn_o, kv_state = attn_fn(q, k, v)
    y_attn = attn_o.astype(x.dtype) @ w_attn_out
    mixed = (jax.nn.sigmoid(g_conv) * y_conv + jax.nn.sigmoid(g_attn) * y_attn) @ w_o
    x = x + gt1 * mixed
    h2 = rmsnorm(x, norm2_g) * (1 + sc2) + sh2
    x = x + gt2 * hier_moe(h2, w_rg, b_rg, w_re, b_re, w1, w3, w2)
    return x, kv_state + [conv_state]

def setup_inputs(seed: int = 0) -> dict:
    key = jax.random.key(seed)
    ks = jax.random.split(key, 32)
    f32 = jnp.float32

    def nrm(k, shape, s):
        return jax.random.normal(k, shape, f32) * s

    win = [min(w, PAST_LEN) for (w, _) in DIL_GROUPS]
    G, E = N_EXPERT_GROUPS, EXPERTS_PER_GROUP
    return {
        'x_prompt': nrm(ks[0], (BATCH, SEQ, D_MODEL), 1.0),
        'x_sample': nrm(ks[1], (DEC_BATCH, DEC_SEQ, D_MODEL), 1.0),
        'cache_k1': nrm(ks[2], (DEPTH, DEC_BATCH, win[0], HEADS_PER_GROUP, HEAD_DIM), 1.0),
        'cache_v1': nrm(ks[3], (DEPTH, DEC_BATCH, win[0], HEADS_PER_GROUP, HEAD_DIM), 1.0),
        'cache_k2': nrm(ks[4], (DEPTH, DEC_BATCH, win[1], HEADS_PER_GROUP, HEAD_DIM), 1.0),
        'cache_v2': nrm(ks[5], (DEPTH, DEC_BATCH, win[1], HEADS_PER_GROUP, HEAD_DIM), 1.0),
        'cache_k3': nrm(ks[6], (DEPTH, DEC_BATCH, win[2], HEADS_PER_GROUP, HEAD_DIM), 1.0),
        'cache_v3': nrm(ks[7], (DEPTH, DEC_BATCH, win[2], HEADS_PER_GROUP, HEAD_DIM), 1.0),
        'state_conv': nrm(ks[8], (DEPTH, DEC_BATCH, CONV_K - 1, CONV_WIDTH), 1.0),
        'c_prompt': nrm(ks[9], (BATCH, D_MODEL), 1.0),
        'c_sample': nrm(ks[10], (DEC_BATCH, D_MODEL), 1.0),
        'norm1_g': 1.0 + nrm(ks[11], (DEPTH, D_MODEL), 0.01),
        'norm2_g': 1.0 + nrm(ks[12], (DEPTH, D_MODEL), 0.01),
        'normf_g': 1.0 + nrm(ks[13], (D_MODEL,), 0.01),
        'w_ada': nrm(ks[14], (DEPTH, D_MODEL, 6 * D_MODEL), 0.5 * D_MODEL ** -0.5),
        'b_ada': nrm(ks[15], (DEPTH, 6 * D_MODEL), 0.02),
        'w_in': nrm(ks[16], (DEPTH, D_MODEL, IN_COLS), D_MODEL ** -0.5),
        'conv_w': nrm(ks[17], (DEPTH, CONV_K, CONV_WIDTH), CONV_K ** -0.5),
        'w_conv_out': nrm(ks[18], (DEPTH, CONV_WIDTH, D_MODEL), CONV_WIDTH ** -0.5),
        'w_attn_out': nrm(ks[19], (DEPTH, ATTN_OUT, D_MODEL), ATTN_OUT ** -0.5),
        'w_o': nrm(ks[20], (DEPTH, D_MODEL, D_MODEL), D_MODEL ** -0.5),
        'w_rg': nrm(ks[21], (DEPTH, D_MODEL, G), D_MODEL ** -0.5),
        'b_rg': nrm(ks[22], (DEPTH, G), 0.01),
        'w_re': nrm(ks[23], (DEPTH, D_MODEL, G * E), D_MODEL ** -0.5),
        'b_re': nrm(ks[24], (DEPTH, G * E), 0.01),
        'w1': nrm(ks[25], (DEPTH, G, E, D_MODEL, D_EXPERT), D_MODEL ** -0.5),
        'w3': nrm(ks[26], (DEPTH, G, E, D_MODEL, D_EXPERT), D_MODEL ** -0.5),
        'w2': nrm(ks[27], (DEPTH, G, E, D_EXPERT, D_MODEL), D_EXPERT ** -0.5),
    }

def reference(x_prompt, x_sample, cache_k1, cache_v1, cache_k2, cache_v2, cache_k3, cache_v3, state_conv,
              c_prompt, c_sample, norm1_g, norm2_g, normf_g, w_ada, b_ada, w_in, conv_w, w_conv_out,
              w_attn_out, w_o, w_rg, b_rg, w_re, b_re, w1, w3, w2):
    B, S, _ = x_prompt.shape
    T = x_sample.shape[1]
    pos_p = jnp.arange(S, dtype=jnp.int32)
    pos_s = PAST_LEN + jnp.arange(T, dtype=jnp.int32)
    xp, xs = x_prompt, x_sample
    st_p, st_s = [], []
    for l in range(DEPTH):
        lw = (w_ada[l], b_ada[l], norm1_g[l], norm2_g[l], w_in[l], conv_w[l], w_conv_out[l], w_attn_out[l],
              w_o[l], w_rg[l], b_rg[l], w_re[l], b_re[l], w1[l], w3[l], w2[l])
        conv_zero = jnp.zeros((B, CONV_K - 1, CONV_WIDTH), xp.dtype)
        xp, new_p = decoder_layer(xp, c_prompt, pos_p, conv_zero, prompt_attention, *lw)
        caches_l = (cache_k1[l], cache_v1[l], cache_k2[l], cache_v2[l], cache_k3[l], cache_v3[l])
        xs, new_s = decoder_layer(xs, c_sample, pos_s, state_conv[l],
                                  functools.partial(sample_attention, caches_l), *lw)
        st_p.append(new_p)
        st_s.append(new_s)
    y_prompt = rmsnorm(xp, normf_g)
    y_sample = rmsnorm(xs, normf_g)
    k1_p, v1_p, k2_p, v2_p, k3_p, v3_p, conv_p = [jnp.stack([s[i] for s in st_p]) for i in range(7)]
    k1_s, v1_s, k2_s, v2_s, k3_s, v3_s, conv_s = [jnp.stack([s[i] for s in st_s]) for i in range(7)]
    return (y_prompt, y_sample, k1_p, v1_p, k2_p, v2_p, k3_p, v3_p, conv_p,
            k1_s, v1_s, k2_s, v2_s, k3_s, v3_s, conv_s)


_drawn_inputs = setup_inputs


def setup_inputs(seed=0):
    import zlib

    import numpy as np

    out = dict(_drawn_inputs(seed))
    spreads = {}
    factors = {'norm1_g': 4.199, 'norm2_g': 7.524, 'normf_g': 29.766, 'b_rg': 6.119, 'b_re': 44.604}
    for name, (base, spread) in spreads.items():
        noise = np.random.default_rng([zlib.crc32(name.encode()), seed]).standard_normal(out[name].shape)
        drawn = base * np.exp(spread * noise) if base else spread * noise
        out[name] = __import__('jax').numpy.asarray(drawn.astype(out[name].dtype))
    for name, factor in factors.items():
        out[name] = (out[name] * factor).astype(out[name].dtype)
    return out
```

```python
from contextlib import ExitStack

import concourse.bass as bass
from concourse import mybir

F32 = mybir.dt.float32
F32R = mybir.dt.float32r
BF16 = mybir.dt.bfloat16
U16 = mybir.dt.uint16
I32 = mybir.dt.int32
ALU = mybir.AluOpType
ACT = mybir.ActivationFunctionType
AX = mybir.AxisListType

P = 128
D = 1024
KC = D // P
SEQ = 512
DEC_B, DEC_T = 8, 4
NS = DEC_B * DEC_T
NT = SEQ + NS
HALF = NT // 2
TILES = SEQ // P
HD = 64
HEADS = 8
GROUPS = 3
AC = HEADS * HD // P
WINDOWS = (128, 512, 2048)
SCALE = HD ** -0.5
EPS = 1e-6
NEG = -3.0e38
NE, DE = 16, 512
FC = DE // P
TS = 96
MAX_TILES = (2 * NT + NE * (TS - 1)) // TS
MAX_PAIRS = (MAX_TILES + 1) // 2
XTILES = 2 * MAX_PAIRS + 1
TABLE = 32
COUNT_STEPS = -(-NT // TS)

COL_Q = 3 * D
COL_GC = COL_Q + 3 * GROUPS * AC * P
COL_GA = COL_GC + D

B_P = 9 * AC
A_P = 3 * KC
C_P = 4 * KC
D_P = KC
A0, C0 = B_P, B_P + A_P
D0 = C0 + C_P
N_P = D0 + D_P
RING = 4
LEAD = 3
ADA_FIRST = 2 * KC
ADA_ALL = 6 * KC
SLOTS_B = 2 * 9
STEPS = 9
UNITS = 2 * TILES
KEYS_P = SEQ + 2 * P
KEYS_S = 2 * SEQ + P + GROUPS * NS
ROT = 8


def _build(nc, x_prompt, x_sample, cache_k1, cache_v1, cache_k2, cache_v2, cache_k3, cache_v3,
           state_conv, c_prompt, c_sample, norm1_g, norm2_g, normf_g, w_ada, b_ada, w_in, conv_w,
           w_conv_out, w_attn_out, w_o, w_rg, b_rg, w_re, b_re, w1, w3, w2,
           k_ident, k_tri, k_small, k_ropec, k_ropes, k_maskp, k_masks,
           y_prompt, y_sample, k1_p, v1_p, k2_p, v2_p, k3_p, v3_p, conv_p,
           k1_s, v1_s, k2_s, v2_s, k3_s, v3_s, conv_s):
    caches = ((cache_k1, cache_v1), (cache_k2, cache_v2), (cache_k3, cache_v3))
    prompt_kv = ((k1_p, v1_p), (k2_p, v2_p), (k3_p, v3_p))
    sample_kv = ((k1_s, v1_s), (k2_s, v2_s), (k3_s, v3_s))

    x_rows = nc.dram_tensor("x_rows", [XTILES * TS, D], F32, kind="Internal").ap()
    y_rows = x_rows

    base = -(-nc.sbuf_base // 64) * 64
    top = nc.sbuf_top

    class Region:
        def __init__(self, at):
            self.at = at

        def __call__(self, name, shape, dt=F32):
            n = 2 if dt in (BF16, U16) else 4
            for s in shape[1:]:
                n *= s
            t = nc.alloc_sbuf_tensor_at(name, shape, dt, offset=self.at)
            self.at += -(-n // 32) * 32
            assert self.at <= top, (name, self.at, top)
            return t

    keep = Region(base)
    ident = keep("ident", [P, P])
    small = keep("small", [P, 96])
    cT = keep("cT", [P, KC, 9])
    stT = keep("stT", [P, KC, 2 * DEC_B])
    modT = keep("modT", [P, ADA_ALL, 9])
    A1 = keep("A1", [P, KC, 9])
    A2 = keep("A2", [P, KC, 9])
    last2 = keep("last2", [P, KC, 2 + 2 * DEC_B])
    stat = keep("stat", [P, 8])
    rstd = keep("rstd", [P, 8])
    oT_at = keep.at
    oT = keep("oT", [P, AC, NT])
    yb_at = keep.at
    adar = Region(yb_at)("adar", [P, RING, KC, P])
    yb = keep("yb", [P, KC, NT])
    hHi = keep("hHi", [P, KC, NT], F32R)
    hLo = keep("hLo", [P, KC, NT], F32R)
    wraw = keep("wraw", [P, RING, KC, P])
    whi = keep("whi", [P, RING, KC, P], F32R)
    wlo = keep("wlo", [P, RING, KC, P], F32R)
    c_region = keep.at
    QB = keep("QB", [P, GROUPS, AC, DEC_B, NS])
    kTn = keep("kTn", [P, GROUPS, AC, NS])
    Vn = keep("Vn", [NS, GROUPS, AC, P])

    r = Region(keep.at)
    xt = r("xt", [P, TILES + 1, D])
    hraw = r("hraw", [P, 2, KC, P])
    junk = r("junk", [P, D])
    ctok = r("ctok", [9, D])
    sttok = r("sttok", [2 * DEC_B, D])
    rows = r("rows", [88, P])

    r = Region(keep.at)
    ropec = r("ropec", [P, NT])
    ropes = r("ropes", [P, NT])
    maskp = r("maskp", [P, TILES, KEYS_P], U16)
    qT = r("qT", [P, 2, GROUPS, NT])
    kT = r("kT", [P, 2, GROUPS, NT])
    Vt = r("Vt", [P, 2, TILES, GROUPS, P])
    Kst = r("Kst", [P, 2, TILES, P])
    Kns = r("Kns", [NS, 2, P])
    vf = r("vf", [P, NT])
    pr = r("pr", [P, 2, KEYS_P])
    pTa = r("pTa", [P, 3 * P])
    pTb = r("pTb", [P, 3 * P])
    otok = r("otok", [P, P])
    nmx = r("nmx", [P, 2])
    nb = r("nb", [P, 2])
    rs = r("rs", [P, 2])
    ri = r("ri", [P, 2])
    rope_at = r.at
    rb = r("rb", [P, 2, HALF])
    shb = r("shb", [P, 2, HALF])
    t1 = r("t1", [P, 2, HALF])
    r = Region(rope_at)
    u_sb = r("u_sb", [P, 2, HALF])
    cu = r("cu", [P, NT])
    yv = r("yv", [P, NT])
    ext = r("ext", [P, DEC_B, 6])

    r = Region(keep.at)
    kvr = r("kvr", [P, RING, 4 * HEADS * HD])
    kTs = r("kTs", [P, RING, 4 * P])
    ps_ = r("ps_", [P, KEYS_S])
    pTs = r("pTs", [P, 9, P])
    pTn = r("pTn", [NS, GROUPS, P])
    masks = r("masks", [P, 2, KEYS_S], U16)
    zer = r("zer", [P, P])
    sst = r("sst", [P, 8])
    ltok = r("ltok", [2 + 2 * DEC_B, D])

    r = Region(c_region)
    zrow = Region(top - 2048 - 64)("zrow", [P, 512])
    ybHi = r("ybHi", [P, KC, NT], F32R)
    ybLo = r("ybLo", [P, KC, NT], F32R)
    oHi = r("oHi", [P, AC, NT], F32R)
    oLo = r("oLo", [P, AC, NT], F32R)
    mixHi = r("mixHi", [P, KC, NT], F32R)
    gyc = r("gyc", [P, 2, HALF])
    gsg = r("gsg", [P, 2, HALF])
    gm1 = r("gm1", [P, 2, HALF])
    gmx = r("gmx", [P, 2, HALF])
    mixLo = Region(yb_at)("mixLo", [P, KC, NT], F32R)

    r = Region(c_region)
    op = r("op", [P, KC, NT])
    x2 = r("x2", [P, TILES + 1, D])
    tokt = r("tokt", [P, 3, D])
    toks = r("toks", [NS, 3, D])
    wr = r("wr", [P, KC, 20])
    tri = r("tri", [P, P])
    ones = r("ones", [P, P])
    br = r("br", [P, 20])
    cst = r("cst", [P, 96])
    lg = r("lg", [P, 5, 20])
    rt = r("rt", [P, 24, 5, 4])
    rs1 = r("rs1", [P, 12, 5])
    onehot = r("onehot", [P, 4, 5, NE])
    cmp6 = r("cmp6", [P, NE, COUNT_STEPS])
    ends = r("ends", [P, 6, NE])
    cmpt = r("cmpt", [1, TABLE, NE])
    eidf = r("eidf", [1, TABLE + 16])
    tab = r("tab", [1, TABLE + 4], I32)
    slotf = r("slotf", [P, 2, 5])
    sloti = r("sloti", [P, 2, 5], I32)
    cw = r("cw", [P, 2, 5])
    r = Region(oT_at)
    h2 = r("h2", [P, TILES + 1, D])
    junk2 = r("junk2", [P, D])
    bcp = r("bcp", [P, KC, P])
    bcs = r("bcs", [P, KC, NS])
    h2T = r("h2T", [P, 2, KC, P])
    assert r.at <= c_region

    r = Region(oT_at)
    e1 = r("e1", [P, 2, KC, DE])
    e3 = r("e3", [P, 2, KC, DE])
    e2 = r("e2", [P, 2, FC, D])
    xg = r("xg", [TS, 2, D])
    xgT = r("xgT", [P, 2, KC, TS])
    sil = r("sil", [P, 2, FC, TS])
    hid = r("hid", [P, 2, FC, TS])
    yev = r("yev", [TS, 2, D])
    assert r.at <= c_region + KC * NT * 4
    r = Region(oT_at)
    ya = r("ya", [P, 2, D])
    yb2 = r("yb2", [P, 2, D])
    junk3 = r("junk3", [P, D])

    psum = nc.alloc_psum_tensor("psum", [P, 8, 512], F32)
    BANK_S, BANK_PT, BANK_O, BANK_KV, BANK_MISC = 2, 4, 5, 6, 7
    score = psum[:, BANK_S:BANK_S + 2, :].rearrange("p b n -> p (b n)")
    score_s = psum[:, 2:5, :].rearrange("p b n -> p (b n)")

    win = w_in[0].rearrange("(k p) n -> p k n", p=P)
    wada = w_ada[0].rearrange("(k p) n -> p k n", p=P)
    wco = w_conv_out[0].rearrange("(k p) n -> p k n", p=P)
    wao = w_attn_out[0].rearrange("(k p) n -> p k n", p=P)
    wo = w_o[0].rearrange("(k p) n -> p k n", p=P)
    w1_v = w1[0].rearrange("g e (k p) f -> (g e) p k f", p=P)
    w3_v = w3[0].rearrange("g e (k p) f -> (g e) p k f", p=P)
    w2_v = w2[0].rearrange("g e (k p) f -> (g e) p k f", p=P)
    xp_v = x_prompt[0].rearrange("(n b a) d -> a b n d", b=4, a=TILES)
    yp_v = y_prompt[0].rearrange("(n b a) d -> a b n d", b=4, a=TILES)
    xs_v = x_sample.rearrange("b q d -> (b q) d")
    ys_v = y_sample.rearrange("b q d -> (b q) d")

    def piece_source(m):
        if m < A0:
            c, j = divmod(m, 9)
            g, kv = divmod(j, 3)
            col = COL_Q + GROUPS * AC * P * kv + AC * P * g + P * c
            return win[:, :, col:col + P]
        if m < C0:
            f, j = divmod(m - A0, 3)
            return win[:, :, D * j + P * f:D * j + P * f + P]
        assert m >= D0
        return wo[:, :, P * (m - D0):P * (m - D0) + P]

    kn_rows = nc.dram_tensor("kn_rows", [GROUPS, NS, AC * P], F32, kind="Internal").ap()
    vn_rows = nc.dram_tensor("vn_rows", [GROUPS, NS, AC * P], F32, kind="Internal").ap()

    SHIFTS = []
    for g in (2, 1):
        rows_g = WINDOWS[g] - DEC_T
        parts = 4 if g == 2 else 1
        n = rows_g // parts
        for b in range(DEC_B):
            for kv in range(1 if g == 2 else 2):
                for i in range(parts):
                    src = caches[g][kv][0, b, DEC_T + i * n:DEC_T + (i + 1) * n].rearrange("r h d -> (r h d)")
                    dst = sample_kv[g][kv][0, b, i * n:(i + 1) * n].rearrange("r h d -> (r h d)")
                    SHIFTS.append((dst.rearrange("(x y) -> x y", x=64), src.rearrange("(x y) -> x y", x=64)))
    for kv in range(2):
        src = caches[0][kv][0, :, DEC_T:].rearrange("b r h d -> b (r h d)")
        dst = sample_kv[0][kv][0, :, 0:WINDOWS[0] - DEC_T].rearrange("b r h d -> b (r h d)")
        SHIFTS.append((dst.rearrange("b (x y) -> b x y", x=4), src.rearrange("b (x y) -> b x y", x=4)))

    SHIFTS_AB = len(SHIFTS)
    assert SHIFTS_AB <= C0

    kv_units = [(half, kv, j, g) for half in range(2) for kv in range(2) for j in range(4) for g in (1, 2, 0)]
    K_COL = {1: 0, 2: 4 * P, 0: 8 * P}
    K_TILE = {1: 0, 2: 4, 0: 8}
    NEW_COL = 9 * P

    def cache_source(w):
        half, kv, j, g = kv_units[w]
        v = caches[g][kv][0, 4 * half + j]
        if g == 0:
            return v.rearrange("n h d -> n (h d)")
        if g == 1:
            return v.rearrange("(n r) h d -> n (r h d)", r=4)
        return v.rearrange("(n r) h d -> n r (h d)", r=16)[:, 0:DEC_T, :]

    def kv_tiles(g):
        return 1 if g == 0 else 4

    def kind(m):
        if m < A0:
            return "qkv"[m % 3]
        return ("u", "c", "b")[(m - A0) % 3]

    def unit_at(step):
        if not 0 <= step < STEPS * AC or step % STEPS == STEPS - 1:
            return None
        c, k = divmod(step, STEPS)
        return c * UNITS + k, c, k // 2, k % 2

    def step_of(G):
        return (G - SLOTS_B) // 2 if G >= SLOTS_B else -9

    def unit_cols(a, h):
        return slice(P * a, P * a + P)

    with ExitStack() as ctx:
        def sem(name):
            return ctx.enter_context(nc.semaphore(name))

        cst_in = sem("cst_in")
        x_in = sem("x_in")
        rope_in = sem("rope_in")
        ada_in = [sem(f"ada_in{k}") for k in range(RING)]
        raw_in = [sem(f"raw_in{k}") for k in range(RING)]
        silu_done = sem("silu_done")
        first_T = sem("first_T")
        first_ev = sem("first_ev")
        ada_pe = sem("ada_pe")
        ada_ev = sem("ada_ev")
        sq_done = sem("sq_done")
        ms_done = sem("ms_done")
        sqrt_done = sem("sqrt_done")
        xn_done = sem("xn_done")
        xT_pe = sem("xT_pe")
        hraw_done = sem("hraw_done")
        hhi_done = sem("hhi_done")
        hlo_done = sem("hlo_done")
        dve_local = sem("dve_local")
        hi_done = sem("hi_done")
        lo_done = sem("lo_done")
        grp = sem("grp")
        bank_free = [sem("bank_free0"), sem("bank_free1")]
        shuf_done = sem("shuf_done")
        rot_done = sem("rot_done")
        rope_done = sem("rope_done")
        qb_zero = sem("qb_zero")
        qb_done = sem("qb_done")
        kt_pe = sem("kt_pe")
        kt_ev = sem("kt_ev")
        vt_pe = sem("vt_pe")
        vt_ev = sem("vt_ev")
        k_out = [sem("k_out0"), sem("k_out1")]
        v_out = [sem("v_out0"), sem("v_out1")]
        misc_pe = sem("misc_pe")
        misc_ev = sem("misc_ev")
        s_pe = sem("s_pe")
        s_mx = sem("s_mx")
        s_nb = sem("s_nb")
        s_exp = sem("s_exp")
        pta_pe = sem("pta_pe")
        pta_ev = sem("pta_ev")
        pva_pe = sem("pva_pe")
        ptb_pe = sem("ptb_pe")
        ptb_ev = sem("ptb_ev")
        pvb_pe = sem("pvb_pe")
        rec_done = sem("rec_done")
        o_ev = sem("o_ev")
        cu_done = sem("cu_done")
        shift_out = sem("shift_out")
        conv_out = sem("conv_out")
        mask_in = sem("mask_in")
        kv_in = [sem(f"kv_in{k}") for k in range(RING)]
        zer_done = sem("zer_done")
        ktr_pe = sem("ktr_pe")
        ktr_act = sem("ktr_act")
        ktr_dve = sem("ktr_dve")
        ss_pe = sem("ss_pe")
        ssn_pe = sem("ssn_pe")
        ss_mx = sem("ss_mx")
        ss_nb = sem("ss_nb")
        ss_exp = sem("ss_exp")
        ss_p = sem("ss_p")
        spt_pe = sem("spt_pe")
        spt_ev = sem("spt_ev")
        spv_pe = sem("spv_pe")
        so_pe = sem("so_pe")
        so_ev = sem("so_ev")
        lt_pe = sem("lt_pe")
        lt_ev = sem("lt_ev")
        yo_hi = sem("yo_hi")
        yo_lo = sem("yo_lo")
        g_m1 = sem("g_m1")
        g_m2 = sem("g_m2")
        g_mx = sem("g_mx")
        g_hi = sem("g_hi")
        g_lo = sem("g_lo")
        xr_in = sem("xr_in")
        late_in = sem("late_in")
        opT_pe = sem("opT_pe")
        x2_done = sem("x2_done")
        bc_done = sem("bc_done")
        bcT_pe = sem("bcT_pe")
        bcT_ev = sem("bcT_ev")
        ss2_done = sem("ss2_done")
        ms2_done = sem("ms2_done")
        sqrt2_done = sem("sqrt2_done")
        h2_done = sem("h2_done")
        h2T_pe = sem("h2T_pe")
        h2T_ev = sem("h2T_ev")
        lg_pe = sem("lg_pe")
        rt_dve = sem("rt_dve")
        rt_act = sem("rt_act")
        oh_done = sem("oh_done")
        pos_pe = sem("pos_pe")
        slot_done = sem("slot_done")
        tab_done = sem("tab_done")
        zrow_done = sem("zrow_done")
        xz_out = sem("xz_out")
        disp_out = sem("disp_out")
        xg_in = [sem("xg_in0"), sem("xg_in1")]
        e13_in = [sem("e13_in0"), sem("e13_in1")]
        e2_in = [sem("e2_in0"), sem("e2_in1")]
        xgT_pe = sem("xgT_pe")
        xgT_ev = sem("xgT_ev")
        ab_pe = sem("ab_pe")
        sil_done = sem("sil_done")
        hid_done = sem("hid_done")
        ye_pe = sem("ye_pe")
        ye_ev0 = sem("ye_ev0")
        ye_ev1 = sem("ye_ev1")
        ye_out = [sem("ye_out0"), sem("ye_out1")]
        yg_in = [sem("yg_in0"), sem("yg_in1")]
        nf_in = sem("nf_in")
        f_mix = sem("f_mix")
        f_sq = sem("f_sq")
        f_ms = sem("f_ms")
        f_sqrt = sem("f_sqrt")
        f_y = sem("f_y")
        y_out = sem("y_out")
        otr_pe = sem("otr_pe")
        kn_pe = sem("kn_pe")
        kn_ev = sem("kn_ev")
        kn_out = sem("kn_out")
        stat_init = sem("stat_init")
        tail_out = sem("tail_out")
        all_stored = sem("all_stored")
        shiftc = sem("shiftc")
        vn_out = sem("vn_out")

        block = ctx.enter_context(nc.Block())

        def misc_before(G, part):
            n = 0
            for g in range(G + 1):
                for q in range(3):
                    if (g, q) >= (G, part):
                        return n
                    n += misc_use(g, q)
            return n

        def misc_use(G, part):
            m = G // 2
            if part == 0:
                return G % 2 == 0 and 2 <= m < B_P + 2 and kind(m - 2) in "kv"
            if part == 1:
                u = unit_at(step_of(G) - 2)
                return G % 2 == 1 and u is not None and u[3] == 1
            return G % 2 == 1 and m < ADA_ALL - ADA_FIRST

        MISC = {(G, q): misc_before(G, q) for G in range(2 * C0) for q in range(3) if misc_use(G, q)}
        MISC_ALL = len(MISC)

        @block.sync
        def _(sp):
            sp.dma_start(ident[:, :], k_ident).then_inc(cst_in, 16)
            sp.dma_start(ctok[0:1, :], c_prompt).then_inc(cst_in, 16)
            sp.dma_start(ctok[1:9, :], c_sample).then_inc(cst_in, 16)
            sp.dma_start(rows[0:48, :], b_ada[0].rearrange("(c p) -> c p", p=P)).then_inc(cst_in, 16)
            sp.dma_start(rows[48:56, :], norm1_g[0].rearrange("(c p) -> c p", p=P)).then_inc(cst_in, 16)
            sp.dma_start(rows[56:64, :], norm2_g[0].rearrange("(c p) -> c p", p=P)).then_inc(cst_in, 16)
            sp.dma_start(rows[64:88, :], conv_w[0].rearrange("j (c p) -> (j c) p", p=P)).then_inc(cst_in, 16)
            sp.dma_start(sttok[:, :], state_conv[0].rearrange("b r d -> (b r) d")).then_inc(cst_in, 16)
            for k in range(RING):
                sp.dma_start(adar[:, k], wada[:, :, P * k:P * k + P]).then_inc(ada_in[k], 16)
            for a in range(TILES):
                for b in range(4):
                    sp.dma_start(xt[32 * b:32 * b + 32, a, :], xp_v[a, b]).then_inc(x_in, 16)
            sp.dma_start(xt[0:NS, TILES, :], xs_v).then_inc(x_in, 16)
            with sp.Fori(1, ADA_FIRST // RING) as i:
                for k in range(RING):
                    sp.wait_ge(ada_pe, 4 * i + (k - 3))
                    sp.dma_start(adar[:, k], wada[:, :, bass.ds((4 * i + k) * P, P)]).then_inc(ada_in[k], 16)
            for m in range(C0):
                if m == RING:
                    sp.wait_ge(hlo_done, TILES + 1)
                    sp.wait_ge(first_ev, 3)
                    sp.dma_start(ropec[:, :], k_ropec).then_inc(rope_in, 16)
                    sp.dma_start(ropes[:, :], k_ropes).then_inc(rope_in, 16)
                    sp.dma_start(maskp[:, :, :], k_maskp).then_inc(rope_in, 16)
                if m >= RING:
                    sp.wait_ge(lo_done, m - RING + 1)
                sp.dma_start(wraw[:, m % RING], piece_source(m)).then_inc(raw_in[m % RING], 16)
                if m < ADA_ALL - ADA_FIRST:
                    n = ADA_FIRST + m
                    sp.wait_ge(ada_pe, n - RING + 1)
                    sp.dma_start(adar[:, n % RING], wada[:, :, P * n:P * n + P]).then_inc(ada_in[n % RING], 16)
                if m < SHIFTS_AB:
                    dst, src = SHIFTS[m]
                    sp.dma_start(dst, src).then_inc(shift_out, 16)
            sp.wait_ge(o_ev, UNITS * AC)
            sp.wait_ge(otr_pe, TILES * AC)
            for k in range(2):
                sp.wait_ge(k_out[k], 64 * (GROUPS * AC // 2))
                sp.wait_ge(v_out[k], 64 * GROUPS * (AC // 2))
            sp.dma_start(masks[:, :, :], k_masks).then_inc(mask_in, 16)
            for w, (half, kv, j, g) in enumerate(kv_units):
                if w >= RING:
                    h0, kv0, j0, g0 = kv_units[w - RING]
                    done = 12 * h0 + 3 * j0 + (1, 2, 0).index(g0) + 1
                    if kv0 == 0:
                        sp.wait_ge(ktr_pe, AC * done)
                    else:
                        sp.wait_ge(spv_pe, done)
                src = cache_source(w)
                dst = kvr[:, w % RING, 0:kv_tiles(g) * 512]
                if g == 2:
                    dst = dst.rearrange("p (r n) -> p r n", n=512)
                sp.dma_start(dst, src).then_inc(kv_in[w % RING], 16)
            sp.wait_ge(zrow_done, 1)
            zsrc = zrow[:, :].rearrange("p (o n) -> p o n", o=1)
            zdst = x_rows.rearrange("(p r) (o n) -> p (r o) n", p=TS, n=512)
            sp.dma_start(zdst, zsrc[0:TS].to_broadcast([TS, XTILES * 2, 512])).then_inc(xz_out, 16)
            with sp.Fori(0, KC) as f:
                for j in range(RING):
                    sp.wait_ge(lo_done, 4 * f + (C0 + j - RING + 1))
                    if j == 2:
                        src, dst = wao[:, :, bass.ds(f * P, P)], wraw[:, j, 0:AC]
                    elif j == 0:
                        src, dst = wco[:, :, bass.ds(f * P, P)], wraw[:, j]
                    else:
                        src, dst = win[:, :, bass.ds(f * P + (COL_GC if j == 1 else COL_GA), P)], wraw[:, j]
                    sp.dma_start(dst, src).then_inc(raw_in[j], 16)
                    n = (WINDOWS[2] - DEC_T) // 4
                    src = cache_v3[0, bass.ds(f, 1), DEC_T + j * n:DEC_T + (j + 1) * n].rearrange("b r h d -> (b r h d)")
                    dst = v3_s[0, bass.ds(f, 1), j * n:(j + 1) * n].rearrange("b r h d -> (b r h d)")
                    sp.dma_start(dst.rearrange("(x y) -> x y", x=64), src.rearrange("(x y) -> x y", x=64))\
                        .then_inc(shiftc, 16)
            for m in range(D0, N_P):
                sp.wait_ge(lo_done, m - RING + 1)
                if m == D0 + RING:
                    sp.wait_ge(grp, 2 * D0)
                    for a in range(TILES):
                        for b in range(4):
                            sp.dma_start(x2[32 * b:32 * b + 32, a, :], xp_v[a, b]).then_inc(xr_in, 16)
                    sp.dma_start(x2[0:NS, TILES, :], xs_v).then_inc(xr_in, 16)
                sp.dma_start(wraw[:, m % RING], piece_source(m)).then_inc(raw_in[m % RING], 16)
            sp.wait_ge(grp, 2 * N_P)
            sp.dma_start(tri[:, :], k_tri).then_inc(late_in, 16)
            sp.dma_start(cst[:, :], k_small).then_inc(late_in, 16)
            sp.dma_start(wr[:, :, 0:4], w_rg[0].rearrange("(k p) n -> p k n", p=P)).then_inc(late_in, 16)
            sp.dma_start(wr[:, :, 4:20], w_re[0].rearrange("(k p) n -> p k n", p=P)).then_inc(late_in, 16)
            sp.dma_start(br[:, 0:4], b_rg.to_broadcast([P, 4])).then_inc(late_in, 16)
            sp.dma_start(br[:, 4:20], b_re.to_broadcast([P, 16])).then_inc(late_in, 16)
            sp.wait_ge(h2_done, TILES + 1)
            sp.dma_start(tokt[:, 0, :], normf_g.rearrange("(a n) -> a n", a=1).to_broadcast([P, D])).then_inc(nf_in, 16)
            sp.wait_ge(tab_done, 1)
            sp.wait_ge(disp_out, 160)
            pairs = sp.value_load(tab[0:1, TABLE:TABLE + 1], min_val=1, max_val=MAX_PAIRS)
            sp.dma_start(xg[:, 0, :], x_rows[0:TS, :]).then_inc(xg_in[0], 16)
            with sp.Fori(0, pairs) as jp:
                for q in range(2):
                    e = sp.value_load(tab[0:1, bass.ds(2 * jp + q, 1)], min_val=0, max_val=NE - 1)
                    sp.wait_ge(ab_pe, 2 * jp + (q + 1))
                    sp.dma_start(e1[:, q], w1_v[bass.ds(e, 1)].rearrange("e p k f -> (e p) k f")).then_inc(e13_in[q], 16)
                    sp.dma_start(e3[:, q], w3_v[bass.ds(e, 1)].rearrange("e p k f -> (e p) k f")).then_inc(e13_in[q], 16)
                    sp.wait_ge(xgT_pe, 2 * jp + (q + 1))
                    sp.dma_start(xg[:, 1 - q, :], x_rows[bass.ds((2 * jp + (q + 1)) * TS, TS), :])\
                        .then_inc(xg_in[1 - q], 16)
                    sp.wait_ge(ye_pe, 4 * jp + (2 * q + 2))
                    sp.dma_start(e2[:, q], w2_v[bass.ds(e, 1)].rearrange("e p k f -> (e p) k f")).then_inc(e2_in[q], 16)
            for tt in range(TILES + 1):
                sp.wait_ge(f_y, tt + 1)
                if tt < TILES:
                    for b in range(4):
                        sp.dma_start(yp_v[tt, b], x2[32 * b:32 * b + 32, tt, :]).then_inc(y_out, 16)
                else:
                    sp.dma_start(ys_v, x2[0:NS, tt, :]).then_inc(y_out, 16)
            sp.wait_ge(y_out, 16 * (4 * TILES + 1))
            sp.wait_ge(shift_out, 16 * SHIFTS_AB)
            sp.wait_ge(shiftc, 16 * 4 * KC)
            sp.wait_ge(conv_out, 32)
            sp.wait_ge(kn_out, 16 * GROUPS * AC)
            sp.wait_ge(vn_out, 16 * GROUPS)
            sp.wait_ge(tail_out, 16 * 2 * GROUPS)

        @block.tensor
        def _(pe):
            pe.wait_ge(cst_in, 128)
            pe.transpose(psum[:, 0, 0:88], rows[:, :], ident[0:88, 0:88]).then_inc(first_T, 1)
            pe.wait_ge(silu_done, 1)
            for k in range(KC):
                mm = pe.transpose(psum[:, 1, 16 * k:16 * k + 9], ctok[:, P * k:P * k + P], ident[0:9, 0:9])
            mm.then_inc(first_T, 1)
            for k in range(KC):
                mm = pe.transpose(psum[:, 2, 16 * k:16 * k + 16], sttok[:, P * k:P * k + P], ident[0:16, 0:16])
            mm.then_inc(first_T, 1)

            def modulation(slot, out):
                for k in range(KC):
                    mm = pe.matmul(out, adar[:, slot, k, :], cT[:, k, :], start=(k == 0), stop=(k == KC - 1))
                mm.then_inc(ada_pe, 1)

            pe.wait_ge(first_ev, 3)
            with pe.Fori(0, ADA_FIRST // RING) as i:
                for k in range(RING):
                    pe.wait_ge(ada_in[k], 16 * i + 16)
                    if k % 2 == 0:
                        pe.wait_ge(ada_ev, 2 * i + (k // 2 + 1))
                    modulation(k, psum[:, 3 + k // 2, 16 * (k % 2):16 * (k % 2) + 9])

            pe.wait_ge(ada_ev, 2 + ADA_FIRST // 2)
            for tt in range(TILES + 1):
                n = P if tt < TILES else NS
                pe.wait_ge(xn_done, tt + 1)
                if tt >= 2:
                    pe.wait_ge(hraw_done, 2 * tt - 2)
                for k in range(KC):
                    mm = pe.transpose(psum[:, 2 * (tt % 2) + k // 4, P * (k % 4):P * (k % 4) + n],
                                      xt[0:n, tt, P * k:P * k + P], ident[0:n, 0:n])
                mm.then_inc(xT_pe, 1)
            pe.wait_ge(hlo_done, TILES + 1)

            def project(m, slot, xhi, xlo, t, k_n=KC, free=None):
                if free is not None:
                    pe.wait_ge(bank_free[t], free)
                cols = slice(HALF * t, HALF * t + HALF)
                for k in range(k_n):
                    for n, (w, x) in enumerate(((whi, xhi), (wlo, xhi), (whi, xlo))):
                        mm = pe.matmul(psum[:, t, 0:HALF], w[:, slot, k, :], x[:, k, cols],
                                       start=(k == 0 and n == 0), stop=(k == k_n - 1 and n == 2))
                mm.then_inc(grp, 1)

            def keys_values_T(G):
                m = G // 2 - 2
                c, j = divmod(m, 9)
                g, kv = divmod(j, 3)
                n = GROUPS * c + g
                if kind(m) == "k":
                    pe.wait_ge(rope_done, 4 * n + 4)
                    if n >= 1:
                        pe.wait_ge(vt_ev, n)
                    src = kT[:, c % 2, g, :]
                else:
                    pe.wait_ge(bank_free[0], m + 1)
                    pe.wait_ge(bank_free[1], m + 1)
                    pe.wait_ge(kt_ev, n + 1)
                    src = vf[:, :]
                for a in range(TILES):
                    mm = pe.transpose(psum[:, BANK_KV, P * a:P * a + P], src[:, P * a:P * a + P], ident[:, :])
                mm.then_inc(kt_pe if kind(m) == "k" else vt_pe, 1)
                if MISC[G, 0] > 0:
                    pe.wait_ge(misc_ev, MISC[G, 0])
                pe.transpose(psum[0:NS, BANK_MISC, 0:P], src[:, SEQ:NT], ident[:, :]).then_inc(kn_pe, 1)

            def values_part(u, second):
                _, c, a, h = u
                for i in range(3):
                    n = 3 * second + i
                    g, tile_ = (0, n) if n < TILES else (n - TILES + 1, a)
                    mm = pe.matmul(psum[:, BANK_O, 0:HD], (pTb if second else pTa)[:, P * i:P * i + P],
                                   Vt[:, c % 2, tile_, g, HD * h:HD * h + HD], start=(n == 0), stop=(n == 5))
                return mm

            def probs_T(u, second):
                for i in range(3):
                    n = 3 * second + i
                    mm = pe.transpose(psum[:, BANK_PT, P * i:P * i + P], pr[:, u[0] % 2, P * n:P * n + P],
                                      ident[:, :])
                return mm

            def attend(G):
                step = step_of(G)
                if G % 2 == 0:
                    u = unit_at(step - 2)
                    if u:
                        pe.wait_ge(ptb_ev, u[0] + 1)
                        values_part(u, 1).then_inc(pvb_pe, 1)
                    u = unit_at(step)
                    if u:
                        n, c, a, h = u
                        pe.wait_ge(rope_done, 12 * (c + 1))
                        if n >= 1:
                            pe.wait_ge(s_mx, n)
                        rows_h = slice(HD * h, HD * h + HD)
                        q = [qT[rows_h, c % 2, g, P * a:P * a + P] for g in range(GROUPS)]
                        pe.matmul(score[:, 0:SEQ], q[0], kT[rows_h, c % 2, 0, 0:SEQ], start=True, stop=True)
                        for g in (1, 2):
                            mm = pe.matmul(score[:, SEQ + P * (g - 1):SEQ + P * g], q[g],
                                           kT[rows_h, c % 2, g, P * a:P * a + P], start=True, stop=True)
                        mm.then_inc(s_pe, 1)
                    u = unit_at(step - 1)
                    if u:
                        pe.wait_ge(s_exp, u[0] + 1)
                        if u[0] >= 1:
                            pe.wait_ge(ptb_ev, u[0])
                        probs_T(u, 0).then_inc(pta_pe, 1)
                else:
                    u = unit_at(step - 1)
                    if u:
                        pe.wait_ge(pta_ev, u[0] + 1)
                        pe.wait_ge(vt_ev, GROUPS * (u[1] + 1))
                        if u[0] >= 1:
                            pe.wait_ge(o_ev, u[0])
                        values_part(u, 0).then_inc(pva_pe, 1)
                        probs_T(u, 1).then_inc(ptb_pe, 1)
                    u = unit_at(step - 2)
                    if u and u[3] == 1:
                        pe.wait_ge(o_ev, u[0] + 1)
                        if MISC[G, 1] > 0:
                            pe.wait_ge(misc_ev, MISC[G, 1])
                        pe.transpose(psum[:, BANK_MISC, 0:P], otok[:, :], ident[:, :]).then_inc(otr_pe, 1)

            for G in range(2 * C0):
                m, t = divmod(G, 2)
                if misc_use(G, 0):
                    keys_values_T(G)
                attend(G)
                if misc_use(G, 2):
                    n = ADA_FIRST + m
                    if MISC[G, 2] > 0:
                        pe.wait_ge(misc_ev, MISC[G, 2])
                    pe.wait_ge(ada_in[n % RING], 16 * (n // RING + 1))
                    modulation(n % RING, psum[:, BANK_MISC, 0:9])
                if t == 0:
                    pe.wait_ge(lo_done, m + 1)
                project(m, m % RING, hHi, hLo, t, free=m if m >= 1 else None)

            pe.wait_ge(cu_done, 2 * KC)
            pe.wait_ge(misc_ev, MISC_ALL)
            for k in range(KC):
                mm = pe.transpose(psum[0:18, 6 + k // 4, P * (k % 4):P * (k % 4) + P], last2[:, k, :], ident[:, :])
            mm.then_inc(lt_pe, 1)

            pe.wait_ge(bank_free[0], C0)
            pe.wait_ge(bank_free[1], C0)
            pe.wait_ge(qb_done, 3 * GROUPS * AC)
            pe.wait_ge(zer_done, 1)
            for half in range(2):
                chunks = [(3 * j + gi, j, g, ch) for j in range(4) for gi, g in enumerate((1, 2, 0)) for ch in range(AC)]

                def keys_T(n):
                    i, j, g, ch = chunks[n]
                    x = half * len(chunks) + n
                    w = 24 * half + i
                    if ch == 0:
                        pe.wait_ge(kv_in[w % RING], 16 * (w // RING + 1))
                    if x >= 2:
                        pe.wait_ge((ktr_act, ktr_dve)[x % 2], x // 2)
                    if half == 1 and n < 2:
                        pe.wait_ge(spt_ev, 3)
                    for r_ in range(kv_tiles(g)):
                        mm = pe.transpose(psum[:, x % 2, P * r_:P * r_ + P],
                                          kvr[:, w % RING, 512 * r_ + P * ch:512 * r_ + P * ch + P], ident[:, :])
                    mm.then_inc(ktr_pe, 1)

                def scores_s(n):
                    i, j, g, ch = chunks[n]
                    x = half * len(chunks) + n
                    pe.wait_ge((ktr_act, ktr_dve)[x % 2], x // 2 + 1)
                    w_ = P * kv_tiles(g)
                    pe.matmul(score_s[32 * j:32 * j + 32, K_COL[g]:K_COL[g] + w_], QB[:, g, ch, 4 * half + j, :],
                              kTs[:, x % RING, 0:w_], start=(ch == 0), stop=(ch == AC - 1)).then_inc(ss_pe, 1)

                if half == 1:
                    pe.wait_ge(ss_mx, 1)
                for n in range(len(chunks) + 1):
                    if n < len(chunks):
                        keys_T(n)
                    if n >= 1:
                        scores_s(n - 1)
                for j in range(4):
                    for g in range(GROUPS):
                        for ch in range(AC):
                            mm = pe.matmul(score_s[32 * j:32 * j + 32, NEW_COL + NS * g:NEW_COL + NS * g + NS],
                                           QB[:, g, ch, 4 * half + j, :], kTn[:, g, ch, :],
                                           start=(ch == 0), stop=(ch == AC - 1))
                mm.then_inc(ssn_pe, 1)
                pe.wait_ge(ss_p, half + 1)
                pe.wait_ge(ktr_act, len(chunks) // 2 * (half + 1))
                pe.wait_ge(ktr_dve, len(chunks) // 2 * (half + 1))
                for part in range(3):
                    if part == 2:
                        pe.wait_ge(spt_ev, 3 * half + 1)
                    for i in range(4):
                        n = 4 * part + i
                        if n < 9:
                            mm = pe.transpose(psum[:, part % 2, P * i:P * i + P], ps_[:, P * n:P * n + P], ident[:, :])
                        else:
                            g = n - 9
                            mm = pe.transpose(psum[0:NS, part % 2, P * i:P * i + P],
                                              ps_[:, NEW_COL + NS * g:NEW_COL + NS * g + NS], ident[:, :])
                    mm.then_inc(spt_pe, 1)
                pe.wait_ge(spt_ev, 3 * half + 3)
                if half == 1:
                    pe.wait_ge(so_ev, 2)
                pe.matmul(psum[:, 5, 0:P], zer[:, :], zer[:, :], start=True, stop=False, skip_group_check=True)
                for i in range(12):
                    j, g = i // 3, (1, 2, 0)[i % 3]
                    w = 24 * half + 12 + i
                    pe.wait_ge(kv_in[w % RING], 16 * (w // RING + 1))
                    for r_ in range(kv_tiles(g)):
                        for ch in range(AC):
                            mm = pe.matmul(psum[:, 5, NS * ch + 8 * j:NS * ch + 8 * j + 8],
                                           kvr[:, w % RING, 512 * r_ + P * ch:512 * r_ + P * ch + P],
                                           pTs[:, K_TILE[g] + r_, NS * j + 8 * ch:NS * j + 8 * ch + 8],
                                           start=False, stop=False, skip_group_check=True)
                    mm.then_inc(spv_pe, 1)
                for j in range(4):
                    for g in range(GROUPS):
                        for ch in range(AC):
                            last = (j, g, ch) == (3, GROUPS - 1, AC - 1)
                            mm = pe.matmul(psum[:, 5, NS * ch + 8 * j:NS * ch + 8 * j + 8],
                                           Vn[:, g, ch, :], pTn[:, g, NS * j + 8 * ch:NS * j + 8 * ch + 8],
                                           start=False, stop=last, skip_group_check=True)
                mm.then_inc(so_pe, 1)

            pe.wait_ge(yo_lo, 2)
            with pe.Fori(0, KC) as f:
                for j in range(RING):
                    pe.wait_ge(lo_done, 4 * f + (C0 + j + 1))
                    xhi, xlo = ((ybHi, ybLo), (hHi, hLo), (oHi, oLo), (hHi, hLo))[j]
                    for t in range(2):
                        project(None, j, xhi, xlo, t, k_n=AC if j == 2 else KC, free=4 * f + (C0 + j))
            for m in range(D0, N_P):
                pe.wait_ge(lo_done, m + 1)
                if m == D0:
                    pe.wait_ge(g_lo, 2 * KC)
                for t in range(2):
                    project(m, m % RING, mixHi, mixLo, t, free=m)

            for n in range(3):
                pe.wait_ge(bc_done, 2 * n + 2)
                if n >= 1:
                    pe.wait_ge(bcT_ev, 2 * n)
                for k in range(KC):
                    mm = pe.transpose(psum[:, 2 + k // 4, P * (k % 4):P * (k % 4) + P], bcp[:, k, :], ident[:, :])
                mm.then_inc(bcT_pe, 1)
                for k in range(KC):
                    mm = pe.transpose(psum[0:NS, 4 + k // 4, P * (k % 4):P * (k % 4) + P], bcs[:, k, :], ident[:, :])
                mm.then_inc(bcT_pe, 1)
            pe.wait_ge(bank_free[0], N_P)
            pe.wait_ge(bank_free[1], N_P)
            pe.wait_ge(bcT_ev, 6)
            for tt in range(TILES + 1):
                n = P if tt < TILES else NS
                if tt >= 2:
                    pe.wait_ge(x2_done, tt - 1)
                for k in range(KC):
                    mm = pe.transpose(psum[0:n, 2 * (tt % 2) + k // 4, P * (k % 4):P * (k % 4) + P],
                                      op[:, k, P * tt:P * tt + n], ident[:, :])
                mm.then_inc(opT_pe, 1)
            pe.wait_ge(x2_done, TILES + 1)
            pe.wait_ge(late_in, 96)
            for tt in range(TILES + 1):
                n = P if tt < TILES else NS
                pe.wait_ge(h2_done, tt + 1)
                if tt >= 2:
                    pe.wait_ge(h2T_ev, tt - 1)
                for k in range(KC):
                    mm = pe.transpose(psum[:, 2 * (tt % 2) + k // 4, P * (k % 4):P * (k % 4) + n],
                                      h2[0:n, tt, P * k:P * k + P], ident[0:n, 0:n])
                mm.then_inc(h2T_pe, 1)
                pe.wait_ge(h2T_ev, tt + 1)
                for k in range(KC):
                    mm = pe.matmul(psum[0:n, 4, 32 * tt:32 * tt + 20], h2T[:, tt % 2, k, 0:n], wr[:, k, :],
                                   start=(k == 0), stop=(k == KC - 1))
                mm.then_inc(lg_pe, 1)
            pe.wait_ge(oh_done, 1)
            for tt in range(TILES + 1):
                n = P if tt < TILES else NS
                for s in range(tt + 1):
                    kk = P if s < TILES else NS
                    pe.matmul(psum[0:n, 5, 16 * tt:16 * tt + 16], (ones if s < tt else tri)[0:kk, 0:n],
                              onehot[0:kk, 2, s, :], start=(s == 0), stop=(s == tt))
            for s in range(TILES + 1):
                kk = P if s < TILES else NS
                mm = pe.matmul(psum[:, 6, 0:16], ones[0:kk, :], onehot[0:kk, 2, s, :],
                               start=(s == 0), stop=(s == TILES))
            mm.then_inc(pos_pe, 1)

            pe.wait_ge(tab_done, 1)
            pairs = pe.value_load(tab[0:1, TABLE:TABLE + 1], min_val=1, max_val=MAX_PAIRS)
            pe.sem_inc(ab_pe, 2)
            pe.sem_inc(ye_pe, 4)
            pe.sem_inc(xgT_pe, 1)

            def rows_T(slot):
                for k in range(KC):
                    mm = pe.transpose(psum[:, k // 4, TS * (k % 4):TS * (k % 4) + TS],
                                      xg[:, slot, P * k:P * k + P], ident[0:TS, 0:TS])
                mm.then_inc(xgT_pe, 1)

            pe.wait_ge(xg_in[0], 16)
            rows_T(0)
            with pe.Fori(0, pairs) as jp:
                for q in range(2):
                    pe.wait_ge(e13_in[q], 32 * jp + 32)
                    pe.wait_ge(xgT_ev, 4 * jp + (2 * q + 2))
                    pe.wait_ge(hid_done, 2 * jp + (q + 1))
                    for w, bank in ((e1, 2 + q), (e3, 4 + q)):
                        for fc in range(FC):
                            for k in range(KC):
                                mm = pe.matmul(psum[:, bank, TS * fc:TS * fc + TS], w[:, q, k, P * fc:P * fc + P],
                                               xgT[:, q, k, :], start=(k == 0), stop=(k == KC - 1))
                    mm.then_inc(ab_pe, 1)
                    pe.wait_ge(xg_in[1 - q], 16 * jp + 16 + 16 * q)
                    rows_T(1 - q)
                    pe.wait_ge(e2_in[q], 16 * jp + 16)
                    pe.wait_ge(hid_done, 2 * jp + (q + 3))
                    pe.wait_ge(ye_ev0, 2 * jp + (q + 1))
                    pe.wait_ge(ye_ev1, 2 * jp + (q + 1))
                    for n in range(2):
                        for fc in range(FC):
                            mm = pe.matmul(psum[0:TS, 6 + n, :], hid[:, q, fc, :], e2[:, q, fc, 512 * n:512 * n + 512],
                                           start=(fc == 0), stop=(fc == FC - 1))
                        mm.then_inc(ye_pe, 1)

        @block.scalar
        def _(act):
            act.wait_ge(cst_in, 128)
            act.activation(ctok[:, :], ctok[:, :], ACT.Silu).then_inc(silu_done, 1)
            act.wait_ge(stat_init, 1)
            act.wait_ge(x_in, 16 * (4 * TILES + 1))
            for tt in range(TILES + 1):
                n = P if tt < TILES else NS
                if tt:
                    act.wait_ge(sq_done, tt)
                act.activation(junk[0:n, :], xt[0:n, tt, :], ACT.Square,
                               accum_out=stat[0:n, tt:tt + 1]).then_inc(sq_done, 1)
            act.wait_ge(ms_done, 1)
            act.activation(rstd[:, :], stat[:, :], ACT.Sqrt).then_inc(sqrt_done, 1)
            for tt in range(TILES + 1):
                n = P if tt < TILES else NS
                act.wait_ge(hraw_done, 2 * tt + 2)
                act.activation(hHi[:, :, P * tt:P * tt + n], hraw[:, tt % 2, :, 0:n], ACT.Copy).then_inc(hhi_done, 1)

            def split_hi(m, slot, count, pe_groups):
                act.wait_ge(raw_in[slot], count)
                if pe_groups is not None:
                    act.wait_ge(grp, pe_groups)
                act.activation(whi[:, slot], wraw[:, slot], ACT.Copy).then_inc(hi_done, 1)

            def split_hi_at(m):
                split_hi(m, m % RING, 16 * (m // RING + 1), 2 * (m - RING + 1) if m >= RING else None)

            for m in range(LEAD):
                split_hi_at(m)
            for G in range(2 * C0):
                m, t = divmod(G, 2)
                if t == 0:
                    if m + LEAD < C0:
                        split_hi_at(m + LEAD)
                    if 2 <= m < B_P + 2 and kind(m - 2) == "v":
                        c, g = divmod((m - 2) // 3, GROUPS)
                        n = GROUPS * c + g
                        act.wait_ge(vt_pe, n + 1)
                        if c >= 2:
                            act.wait_ge(pvb_pe, UNITS * (c - 1))
                            act.wait_ge(v_out[c % 2], 64 * GROUPS * (c // 2))
                        act.activation(Vt[:, c % 2, :, g, :], psum[:, BANK_KV, :].rearrange("p (a n) -> p a n", n=P),
                                       ACT.Copy).then_inc(vt_ev, 1)
                    step = step_of(G)
                    u = unit_at(step - 1)
                    if u:
                        act.wait_ge(pta_pe, u[0] + 1)
                        if u[0] >= 1:
                            act.wait_ge(pva_pe, u[0])
                        act.activation(pTa[:, :], psum[:, BANK_PT, 0:3 * P], ACT.Copy).then_inc(pta_ev, 1)
                    u = unit_at(step)
                    if u:
                        s = u[0] % 2
                        act.wait_ge(s_nb, u[0] + 1)
                        act.activation(pr[:, s], pr[:, s], ACT.Exp, bias=nb[:, s:s + 1], scale=SCALE,
                                       accum_out=rs[:, s:s + 1]).then_inc(s_exp, 1)
                if kind(m) in "qkvu":
                    act.wait_ge(grp, G + 1)
                    if kind(m) in "qk":
                        R = 4 * (m // 3) + 2 * (m % 3) + t
                        if R >= 2:
                            act.wait_ge(rot_done, 2 * (R - 1))
                        dst = rb[:, t, :]
                    elif kind(m) == "v":
                        if m >= 3:
                            act.wait_ge(kn_pe, 2 * (m // 3))
                        dst = vf[:, HALF * t:HALF * t + HALF]
                    else:
                        if m == A0:
                            act.wait_ge(rope_done, 4 * GROUPS * AC)
                        act.wait_ge(bank_free[t], m)
                        dst = u_sb[:, t, :]
                    act.activation(dst, psum[:, t, 0:HALF], ACT.Copy).then_inc(bank_free[t], 1)

            act.wait_ge(lt_pe, 1)
            act.wait_ge(o_ev, UNITS * AC)
            for n in range(2):
                act.activation(ltok[:, 512 * n:512 * n + 512], psum[0:18, 6 + n, :], ACT.Copy).then_inc(lt_ev, 1)
            for half in range(2):
                for n in range(0, 12 * AC, 2):
                    x = half * 12 * AC + n
                    g = (1, 2, 0)[n // AC % 3]
                    act.wait_ge(ktr_pe, x + 1)
                    if x >= RING:
                        act.wait_ge(ss_pe, x - RING + 1)
                    act.activation(kTs[:, x % RING, 0:P * kv_tiles(g)], psum[:, 0, 0:P * kv_tiles(g)],
                                   ACT.Copy).then_inc(ktr_act, 1)
                act.wait_ge(ss_nb, half + 1)
                act.activation(ps_[:, :], ps_[:, :], ACT.Exp, bias=sst[:, 1:2], scale=SCALE,
                               accum_out=sst[:, 2:3]).then_inc(ss_exp, 1)

            act.wait_ge(so_ev, 4)
            act.wait_ge(vn_out, 16 * GROUPS)
            act.wait_ge(conv_out, 32)
            act.activation(ybHi[:, :, :], yb[:, :, :], ACT.Copy).then_inc(yo_hi, 1)
            act.activation(oHi[:, :, :], oT[:, :, :], ACT.Copy).then_inc(yo_hi, 1)
            for m in range(C0, C0 + LEAD):
                split_hi_at(m)
            with act.Fori(0, KC) as f:
                for j in range(RING):
                    split_hi(None, (j + LEAD) % RING, 16 * f + 16 * ((C0 + j + LEAD) // RING + 1), 8 * f + 2 * (C0 + j))
                    for t in range(2):
                        act.wait_ge(grp, 8 * f + (2 * (C0 + j) + t + 1))
                        if j < 2:
                            act.wait_ge(g_m2, 2 * f + (t + 1))
                        else:
                            act.wait_ge(g_m1, 2 * f + (t + 3))
                        act.activation((gsg if j % 2 else gyc)[:, t, :], psum[:, t, 0:HALF],
                                       ACT.Sigmoid if j % 2 else ACT.Copy).then_inc(bank_free[t], 1)
            for m in range(D0 + LEAD, N_P):
                split_hi_at(m)

            for tt in range(TILES + 1):
                n = P if tt < TILES else NS
                act.wait_ge(x2_done, tt + 1)
                if tt:
                    act.wait_ge(ss2_done, tt)
                act.activation(junk2[0:n, :], x2[0:n, tt, :], ACT.Square,
                               accum_out=stat[0:n, tt:tt + 1]).then_inc(ss2_done, 1)
            act.wait_ge(ms2_done, 1)
            act.activation(rstd[:, :], stat[:, :], ACT.Sqrt).then_inc(sqrt2_done, 1)
            for tt in range(TILES + 1):
                n = P if tt < TILES else NS
                act.wait_ge(h2T_pe, tt + 1)
                if tt >= 2:
                    act.wait_ge(lg_pe, tt - 1)
                src = psum[:, 2 * (tt % 2):2 * (tt % 2) + 2, :].rearrange("p b (k n) -> p (b k) n", n=P)
                act.activation(h2T[:, tt % 2, :, 0:n], src[:, :, 0:n], ACT.Copy).then_inc(h2T_ev, 1)
            act.wait_ge(rt_dve, 1)
            act.activation(rt[:, 1], rt[:, 0], ACT.Exp).then_inc(rt_act, 1)
            act.wait_ge(rt_dve, 2)
            act.activation(rs1[:, 0], rs1[:, 11], ACT.Exp).then_inc(rt_act, 1)

            act.wait_ge(tab_done, 1)
            pairs = act.value_load(tab[0:1, TABLE:TABLE + 1], min_val=1, max_val=MAX_PAIRS)
            act.sem_inc(ye_ev0, 1)
            act.sem_inc(ye_out[0], 16)
            act.sem_inc(ye_out[1], 16)
            with act.Fori(0, pairs) as jp:
                for q in range(2):
                    act.wait_ge(ab_pe, 2 * jp + (q + 3))
                    act.wait_ge(hid_done, 2 * jp + (q + 1))
                    act.activation(sil[:, q].rearrange("p f n -> p (f n)"), psum[:, 2 + q, 0:FC * TS],
                                   ACT.Silu).then_inc(sil_done, 1)
                    act.wait_ge(ye_pe, 4 * jp + (2 * q + 5))
                    act.wait_ge(ye_out[q], 16 * jp + 16)
                    act.activation(yev[:, q, 0:512], psum[0:TS, 6, :], ACT.Copy).then_inc(ye_ev0, 1)
                    act.wait_ge(ye_ev0, 2 * jp + (q + 2))
                    act.wait_ge(ye_ev1, 2 * jp + (q + 2))
                    act.dma_start(y_rows[bass.ds((2 * jp + q) * TS, TS), :], yev[:, q, :]).then_inc(ye_out[q], 16)
            for tt in range(TILES + 1):
                n = P if tt < TILES else NS
                act.wait_ge(f_mix, tt + 1)
                if tt:
                    act.wait_ge(f_sq, tt)
                act.activation(junk3[0:n, :], x2[0:n, tt, :], ACT.Square,
                               accum_out=stat[0:n, tt:tt + 1]).then_inc(f_sq, 1)
                act.wait_ge(f_ms, tt + 1)
                act.activation(rstd[0:n, tt:tt + 1], stat[0:n, tt:tt + 1], ACT.Sqrt).then_inc(f_sqrt, 1)

        @block.vector
        def _(dve):
            local = [0]

            def own(ins):
                local[0] += 1
                ins.then_inc(dve_local, 1)
                dve.wait_ge(dve_local, local[0])

            own(dve.memset(stat[:, :], 1.0))
            dve.sem_inc(stat_init, 1)
            dve.sem_inc(ada_ev, 2)
            dve.wait_ge(first_T, 1)
            dve.tensor_copy(small[:, 0:88], psum[:, 0, 0:88]).then_inc(first_ev, 1)
            dve.wait_ge(first_T, 2)
            dve.tensor_copy(cT[:, :, :], psum[:, 1, 0:128].rearrange("p (k n) -> p k n", n=16)[:, :, 0:9])\
               .then_inc(first_ev, 1)
            dve.wait_ge(first_T, 3)
            dve.tensor_copy(stT[:, :, :], psum[:, 2, 0:128].rearrange("p (k n) -> p k n", n=16)).then_inc(first_ev, 1)
            dve.wait_ge(first_ev, 3)
            dve.wait_ge(sq_done, TILES + 1)
            dve.tensor_scalar(stat[:, :], stat[:, :], 1.0 / D, EPS, ALU.mult, ALU.add).then_inc(ms_done, 1)
            dve.wait_ge(sqrt_done, 1)
            own(dve.reciprocal(rstd[:, :], rstd[:, :]))
            for tt in range(TILES + 1):
                n = P if tt < TILES else NS
                dve.tensor_scalar(xt[0:n, tt, :], xt[0:n, tt, :], rstd[0:n, tt:tt + 1], None, ALU.mult)\
                   .then_inc(xn_done, 1)
            with dve.Fori(0, ADA_FIRST // RING) as i:
                for h in range(2):
                    dve.wait_ge(ada_pe, 4 * i + (2 * h + 2))
                    dve.tensor_tensor(modT[:, bass.ds(4 * i + 2 * h, 2), :],
                                      psum[:, 3 + h, 0:32].rearrange("p (k n) -> p k n", n=16)[:, :, 0:9],
                                      small[:, bass.ds(4 * i + 2 * h, 2)].unsqueeze(2).to_broadcast([P, 2, 9]),
                                      ALU.add).then_inc(ada_ev, 1)
            dve.wait_ge(ada_ev, 2 + ADA_FIRST // 2)
            own(dve.tensor_scalar(A1[:, :, :], modT[:, KC:2 * KC, :], 1.0, None, ALU.add))
            own(dve.tensor_tensor(A1[:, :, :], A1[:, :, :], small[:, 48:56].unsqueeze(2).to_broadcast([P, KC, 9]),
                                  ALU.mult))
            for tt in range(TILES + 1):
                s = tt % 2
                dve.wait_ge(xT_pe, tt + 1)
                if tt < TILES:
                    for k in range(KC):
                        ins = dve.tensor_scalar(hraw[:, s, k, :], psum[:, 2 * s + k // 4, P * (k % 4):P * (k % 4) + P],
                                                A1[:, k, 0:1], modT[:, k, 0:1], ALU.mult, ALU.add)
                        if k % 4 == 3:
                            ins.then_inc(hraw_done, 1)
                    n = P
                else:
                    n = NS
                    for k in range(0, KC, 4):
                        src = psum[:, 2 * s + k // 4, :].rearrange("p (k n) -> p k n", n=P)[:, :, 0:NS]\
                            .rearrange("p k (b q) -> p k b q", q=DEC_T)
                        dst = hraw[:, s, k:k + 4, 0:NS].rearrange("p k (b q) -> p k b q", q=DEC_T)
                        shape = [P, 4, DEC_B, DEC_T]
                        own(dve.tensor_tensor(dst, src, A1[:, k:k + 4, 1:9].unsqueeze(3).to_broadcast(shape), ALU.mult))
                        dve.tensor_tensor(dst, dst, modT[:, k:k + 4, 1:9].unsqueeze(3).to_broadcast(shape),
                                          ALU.add).then_inc(hraw_done, 1)
                dve.wait_ge(hhi_done, tt + 1)
                dve.tensor_tensor(hLo[:, :, P * tt:P * tt + n], hraw[:, s, :, 0:n],
                                  hHi[:, :, P * tt:P * tt + n].bitcast(F32), ALU.subtract).then_inc(hlo_done, 1)

            def split_lo(slot, count):
                dve.wait_ge(hi_done, count)
                dve.tensor_tensor(wlo[:, slot], wraw[:, slot], whi[:, slot].bitcast(F32), ALU.subtract)\
                   .then_inc(lo_done, 1)

            for m in range(LEAD):
                split_lo(m % RING, m + 1)

            def rope_add(G):
                m, t = divmod(G, 2)
                c, j = divmod(m, 9)
                g, kv = divmod(j, 3)
                R = 4 * (m // 3) + 2 * kv + t
                dve.wait_ge(rot_done, 2 * R + 2)
                if c >= 2:
                    dve.wait_ge(s_pe, UNITS * (c - 1))
                    dve.wait_ge(kn_pe, 2 * GROUPS * (c - 1))
                    dve.wait_ge(qb_done, 3 * GROUPS * (c - 1))
                dve.tensor_tensor((kT if kv else qT)[:, c % 2, g, HALF * t:HALF * t + HALF], t1[:, t, :],
                                  shb[:, t, :], ALU.add).then_inc(rope_done, 1)

            def conv(f):
                w = [small[:, 64 + KC * j + f:65 + KC * j + f] for j in range(3)]
                own(dve.tensor_scalar(yv[:, 0:SEQ], cu[:, 0:SEQ], w[2], None, ALU.mult))

                def tap(dst, src, j):
                    own(dve.scalar_tensor_tensor(dst, src, w[j], dst, ALU.mult, ALU.add))

                tap(yv[:, P:SEQ], cu[:, 0:SEQ - P], 1)
                tap(yv[:, 32:P], cu[:, 3 * P:SEQ - 32], 1)
                tap(yv[:, 1:32], cu[:, SEQ - 32:SEQ - 1], 1)
                tap(yv[:, 2 * P:SEQ], cu[:, 0:2 * P], 0)
                y2 = yv[:, 0:2 * P].rearrange("p (a n) -> p a n", n=P)
                c2 = cu[:, 2 * P:SEQ].rearrange("p (a n) -> p a n", n=P)
                tap(y2[:, :, 32:P], c2[:, :, 0:P - 32], 0)
                tap(y2[:, :, 1:32], c2[:, :, P - 32:P - 1], 0)
                own(dve.tensor_copy(ext[:, :, 0:2], stT[:, f, :].rearrange("p (b r) -> p b r", r=2)))
                own(dve.tensor_copy(ext[:, :, 2:6], cu[:, SEQ:NT].rearrange("p (b q) -> p b q", q=DEC_T)))
                ysv = yv[:, SEQ:NT].rearrange("p (b q) -> p b q", q=DEC_T)
                own(dve.tensor_scalar(ysv, ext[:, :, 2:6], w[2], None, ALU.mult))
                tap(ysv, ext[:, :, 1:5], 1)
                tap(ysv, ext[:, :, 0:4], 0)
                dve.tensor_copy(last2[:, f, 0:2], cu[:, 383:512:128]).then_inc(cu_done, 1)
                dve.tensor_copy(last2[:, f, 2:18].rearrange("p (b r) -> p b r", r=2), ext[:, :, 4:6])\
                   .then_inc(cu_done, 1)

            SWAP = [i + 8 if i < 8 else i - 8 if i < 16 else i for i in range(32)]
            for G in range(2 * C0):
                m, t = divmod(G, 2)
                step = step_of(G)
                if t == 0 and m + LEAD < C0:
                    split_lo((m + LEAD) % RING, m + LEAD + 1)
                if misc_use(G, 0):
                    c, j = divmod(m - 2, 9)
                    g = j // 3
                    n = GROUPS * c + g
                    if kind(m - 2) == "k":
                        dve.wait_ge(kt_pe, n + 1)
                        if n >= 2:
                            dve.wait_ge(k_out[n % 2], 64 * (n // 2))
                        dve.tensor_copy(Kst[:, n % 2].rearrange("p a n -> p (a n)"), psum[:, BANK_KV, :])\
                           .then_inc(kt_ev, 1)
                        dve.wait_ge(kn_pe, 2 * n + 1)
                        if n >= 1:
                            dve.wait_ge(kn_out, 16 * n)
                        dve.tensor_copy(Kns[:, n % 2], psum[0:NS, BANK_MISC, 0:P]).then_inc(misc_ev, 1)
                    else:
                        dve.wait_ge(kn_pe, 2 * n + 2)
                        dve.tensor_copy(Vn[:, g, c, :], psum[0:NS, BANK_MISC, 0:P]).then_inc(misc_ev, 1)
                if t == 0:
                    u = unit_at(step - 2)
                    if u:
                        n, c, a, h = u
                        dve.wait_ge(s_exp, n + 1)
                        own(dve.reciprocal(ri[:, n % 2:n % 2 + 1], rs[:, n % 2:n % 2 + 1]))
                        dve.wait_ge(pvb_pe, n + 1)
                        if h == 0 and n >= 2:
                            dve.wait_ge(otr_pe, n // 2)
                        dve.tensor_scalar(otok[:, HD * h:HD * h + HD], psum[:, BANK_O, 0:HD],
                                          ri[:, n % 2:n % 2 + 1], None, ALU.mult).then_inc(o_ev, 1)
                    u = unit_at(step)
                    if u:
                        n, c, a, h = u
                        s = n % 2
                        if n == 0:
                            dve.wait_ge(rope_in, 48)
                        dve.wait_ge(s_pe, n + 1)
                        if n >= 2:
                            dve.wait_ge(ptb_pe, n - 1)
                            dve.wait_ge(s_exp, n - 1)
                        dve.tensor_tensor_reduce(out=pr[:, s], in0=score[:, 0:KEYS_P], in1=maskp[:, a].bitcast(BF16),
                                                 scale=1.0, scalar=NEG, op0=ALU.add, op1=ALU.max,
                                                 accum_out=nmx[:, s:s + 1]).then_inc(s_mx, 1)
                        dve.wait_ge(s_mx, n + 1)
                        dve.tensor_scalar(nb[:, s:s + 1], nmx[:, s:s + 1], -SCALE, None, ALU.mult).then_inc(s_nb, 1)
                else:
                    u = unit_at(step - 1)
                    if u:
                        dve.wait_ge(ptb_pe, u[0] + 1)
                        if u[0] >= 1:
                            dve.wait_ge(pvb_pe, u[0])
                        dve.tensor_copy(pTb[:, :], psum[:, BANK_PT, 0:3 * P]).then_inc(ptb_ev, 1)
                    if misc_use(G, 1):
                        n, c, a, h = unit_at(step - 2)
                        dve.wait_ge(otr_pe, n // 2 + 1)
                        dve.tensor_copy(oT[:, c, P * a:P * a + P], psum[:, BANK_MISC, 0:P]).then_inc(misc_ev, 1)
                    if misc_use(G, 2):
                        n = ADA_FIRST + m
                        dve.wait_ge(ada_pe, n + 1)
                        dve.tensor_scalar(modT[:, n, :], psum[:, BANK_MISC, 0:9], small[:, n:n + 1], None,
                                          ALU.add).then_inc(misc_ev, 1)
                if G >= 1 and kind((G - 1) // 2) in "qk":
                    rope_add(G - 1)
                if kind(m) in "qk":
                    R = 4 * (m // 3) + 2 * (m % 3) + t
                    dve.wait_ge(bank_free[t], m + 1)
                    dve.stream_shuffle(shb[:, t, :], rb[:, t, :], SWAP).then_inc(shuf_done, 1)
                elif kind(m) == "c":
                    f = (m - A0) // 3
                    cols = slice(HALF * t, HALF * t + HALF)
                    dve.wait_ge(grp, G + 1)
                    if f >= 1:
                        dve.wait_ge(cu_done, 2 * f)
                    dve.tensor_tensor(cu[:, cols], psum[:, t, 0:HALF], u_sb[:, t, :], ALU.mult)\
                       .then_inc(bank_free[t], 1)
                    if t == 1:
                        dve.wait_ge(bank_free[0], m + 1)
                        dve.wait_ge(bank_free[1], m + 1)
                        conv(f)
                elif kind(m) == "b":
                    f = (m - A0) // 3
                    cols = slice(HALF * t, HALF * t + HALF)
                    dve.wait_ge(grp, G + 1)
                    dve.tensor_tensor(yb[:, f, cols], psum[:, t, 0:HALF], yv[:, cols], ALU.mult)\
                       .then_inc(bank_free[t], 1)

            dve.wait_ge(vt_pe, GROUPS * AC)
            dve.memset(zer[:, :], 0.0).then_inc(zer_done, 1)
            for half in range(2):
                for n in range(1, 12 * AC, 2):
                    x = half * 12 * AC + n
                    g = (1, 2, 0)[n // AC % 3]
                    dve.wait_ge(ktr_pe, x + 1)
                    if x >= RING:
                        dve.wait_ge(ss_pe, x - RING + 1)
                    dve.tensor_copy(kTs[:, x % RING, 0:P * kv_tiles(g)], psum[:, 1, 0:P * kv_tiles(g)])\
                       .then_inc(ktr_dve, 1)
                dve.wait_ge(mask_in, 16)
                dve.wait_ge(ssn_pe, half + 1)
                if half == 1:
                    dve.wait_ge(spt_pe, 3)
                dve.tensor_tensor_reduce(out=ps_[:, :], in0=score_s[:, 0:KEYS_S], in1=masks[:, half].bitcast(BF16),
                                         scale=1.0, scalar=NEG, op0=ALU.add, op1=ALU.max,
                                         accum_out=sst[:, 0:1]).then_inc(ss_mx, 1)
                dve.wait_ge(ss_mx, half + 1)
                dve.tensor_scalar(sst[:, 1:2], sst[:, 0:1], -SCALE, None, ALU.mult).then_inc(ss_nb, 1)
                dve.wait_ge(ss_exp, half + 1)
                own(dve.reciprocal(sst[:, 3:4], sst[:, 2:3]))
                dve.tensor_scalar(ps_[:, :], ps_[:, :], sst[:, 3:4], None, ALU.mult).then_inc(ss_p, 1)
                if half == 1:
                    dve.wait_ge(so_pe, 1)
                for part in range(3):
                    dve.wait_ge(spt_pe, 3 * half + part + 1)
                    if part < 2:
                        dve.tensor_copy(pTs[:, 4 * part:4 * part + 4, :].rearrange("p t n -> p (t n)"),
                                        psum[:, part, :]).then_inc(spt_ev, 1)
                    else:
                        dve.tensor_copy(pTs[:, 8, :], psum[:, 0, 0:P])
                        dve.tensor_copy(pTn[:, :, :].rearrange("p g n -> p (g n)"), psum[0:NS, 0, P:4 * P])\
                           .then_inc(spt_ev, 1)
                dve.wait_ge(so_pe, half + 1)
                for hh in range(2):
                    part = slice(HD * hh, HD * hh + HD)
                    src = psum[part, 5, 0:P].rearrange("p (k j n) -> p k j n", k=AC, j=4)[:, :, :, 4 * hh:4 * hh + 4]
                    dst = oT[part, :, SEQ + 16 * half:SEQ + 16 * half + 16].rearrange("p k (j q) -> p k j q", q=DEC_T)
                    dve.tensor_copy(dst, src).then_inc(so_ev, 1)

            for n, (lo, hi, full) in enumerate(((ybLo, ybHi, yb), (oLo, oHi, oT))):
                dve.wait_ge(yo_hi, n + 1)
                dve.tensor_tensor(lo[:, :, :], full[:, :, :], hi[:, :, :].bitcast(F32), ALU.subtract).then_inc(yo_lo, 1)
            for m in range(C0, C0 + LEAD):
                split_lo(m % RING, m + 1)
            dve.sem_inc(g_m1, 2)
            dve.sem_inc(g_m2, 2)
            with dve.Fori(0, KC) as f:
                for j in range(RING):
                    split_lo((j + LEAD) % RING, 4 * f + (C0 + j + LEAD + 1))
                    for t in range(2):
                        if j == 1:
                            dve.wait_ge(bank_free[t], 4 * f + (C0 + 2))
                            dve.tensor_tensor(gm1[:, t, :], gsg[:, t, :], gyc[:, t, :], ALU.mult).then_inc(g_m1, 1)
                        if j == 3:
                            cols = slice(HALF * t, HALF * t + HALF)
                            dve.wait_ge(bank_free[t], 4 * f + (C0 + 4))
                            dve.tensor_tensor(gmx[:, t, :], gsg[:, t, :], gyc[:, t, :], ALU.mult).then_inc(g_m2, 1)
                            dve.wait_ge(g_m2, 2 * f + (t + 3))
                            dve.tensor_tensor(gmx[:, t, :], gmx[:, t, :], gm1[:, t, :], ALU.add).then_inc(g_mx, 1)
                            dve.wait_ge(g_mx, 2 * f + (t + 1))
                            hi = mixHi[:, bass.ds(f, 1), cols].rearrange("p k n -> p (k n)")
                            dve.tensor_scalar(hi, gmx[:, t, :], 1.0, None, ALU.mult).then_inc(g_hi, 1)
                            dve.wait_ge(g_hi, 2 * f + (t + 1))
                            dve.tensor_tensor(mixLo[:, bass.ds(f, 1), cols].rearrange("p k n -> p (k n)"),
                                              gmx[:, t, :], hi.bitcast(F32), ALU.subtract).then_inc(g_lo, 1)
            own(dve.tensor_scalar(A2[:, :, :], modT[:, 4 * KC:5 * KC, :], 1.0, None, ALU.add))
            own(dve.tensor_tensor(A2[:, :, :], A2[:, :, :], small[:, 56:64].unsqueeze(2).to_broadcast([P, KC, 9]),
                                  ALU.mult))
            for m in range(D0, N_P):
                if m + LEAD < N_P:
                    split_lo((m + LEAD) % RING, m + LEAD + 1)
                f = m - D0
                gate = modT[:, 2 * KC + f, :]
                for t in range(2):
                    dve.wait_ge(grp, 2 * m + t + 1)
                    n = HALF if t == 0 else SEQ - HALF
                    ins = dve.tensor_scalar(op[:, f, HALF * t:HALF * t + n], psum[:, t, 0:n], gate[:, 0:1], None,
                                            ALU.mult)
                    if t == 1:
                        ins = dve.tensor_tensor(op[:, f, SEQ:NT].rearrange("p (b q) -> p b q", q=DEC_T),
                                                psum[:, t, n:HALF].rearrange("p (b q) -> p b q", q=DEC_T),
                                                gate[:, 1:9].unsqueeze(2).to_broadcast([P, DEC_B, DEC_T]), ALU.mult)
                    ins.then_inc(bank_free[t], 1)
            for n, prm in enumerate((A2[:, :, :], modT[:, 3 * KC:4 * KC, :], modT[:, 5 * KC:6 * KC, :])):
                if n >= 1:
                    dve.wait_ge(bcT_pe, 2 * n)
                dve.tensor_copy(bcp[:, :, :], prm[:, :, 0:1].to_broadcast([P, KC, P])).then_inc(bc_done, 1)
                dve.tensor_copy(bcs[:, :, :].rearrange("p k (b q) -> p k b q", q=DEC_T),
                                prm[:, :, 1:9].unsqueeze(3).to_broadcast([P, KC, DEC_B, DEC_T])).then_inc(bc_done, 1)
                dve.wait_ge(bcT_pe, 2 * n + 1)
                dve.tensor_copy(tokt[:, n, :], psum[:, 2:4, :].rearrange("p b n -> p (b n)")).then_inc(bcT_ev, 1)
                dve.wait_ge(bcT_pe, 2 * n + 2)
                dve.tensor_copy(toks[:, n, :], psum[0:NS, 4:6, :].rearrange("p b n -> p (b n)")).then_inc(bcT_ev, 1)
            dve.wait_ge(bcT_ev, 6)
            dve.memset(ones[:, :], 1.0)
            own(dve.memset(lg[:, :, :], 0.0))
            dve.wait_ge(xr_in, 16 * (4 * TILES + 1))
            for tt in range(TILES + 1):
                n = P if tt < TILES else NS
                s = 2 * (tt % 2)
                dve.wait_ge(opT_pe, tt + 1)
                dve.tensor_tensor(x2[0:n, tt, :], psum[0:n, s:s + 2, :].rearrange("p b n -> p (b n)"), x2[0:n, tt, :],
                                  ALU.add).then_inc(x2_done, 1)
            dve.wait_ge(ss2_done, TILES + 1)
            dve.tensor_scalar(stat[:, :], stat[:, :], 1.0 / D, EPS, ALU.mult, ALU.add).then_inc(ms2_done, 1)
            dve.wait_ge(sqrt2_done, 1)
            own(dve.reciprocal(rstd[:, :], rstd[:, :]))
            for tt in range(TILES + 1):
                n = P if tt < TILES else NS
                tab_ = tokt if tt < TILES else toks
                own(dve.scalar_tensor_tensor(h2[0:n, tt, :], x2[0:n, tt, :], rstd[0:n, tt:tt + 1], tab_[0:n, 0, :],
                                             ALU.mult, ALU.mult))
                dve.tensor_tensor(h2[0:n, tt, :], h2[0:n, tt, :], tab_[0:n, 1, :], ALU.add).then_inc(h2_done, 1)

            dve.wait_ge(late_in, 96)
            dve.wait_ge(lg_pe, TILES + 1)
            own(dve.tensor_tensor(lg[:, 0:TILES, :],
                                  psum[:, 4, 0:32 * TILES].rearrange("p (t n) -> p t n", n=32)[:, :, 0:20],
                                  br[:, :].unsqueeze(1).to_broadcast([P, TILES, 20]), ALU.add))
            own(dve.tensor_tensor(lg[0:NS, TILES, :], psum[0:NS, 4, 32 * TILES:32 * TILES + 20], br[0:NS, :], ALU.add))
            tok4 = [P, 5, 4]
            rev = cst[:, 0:4].unsqueeze(1).to_broadcast(tok4)

            def first_best(values, diff, best, mark, pick, key):
                own(dve.tensor_reduce(rs1[:, best], values, AX.X, ALU.max))
                own(dve.tensor_tensor(rt[:, diff], values, rs1[:, best].unsqueeze(2).to_broadcast(tok4), ALU.subtract))
                own(dve.tensor_scalar(rt[:, mark], rt[:, diff], 0.0, None, ALU.is_equal))
                own(dve.tensor_tensor(rt[:, mark], rt[:, mark], rev, ALU.mult))
                own(dve.tensor_reduce(rs1[:, key], rt[:, mark], AX.X, ALU.max))
                own(dve.tensor_tensor(rt[:, pick], rt[:, mark], rs1[:, key].unsqueeze(2).to_broadcast(tok4),
                                      ALU.is_equal))

            first_best(lg[:, :, 0:4], 0, 3, 2, 3, 4)
            dve.sem_inc(rt_dve, 1)
            prod = onehot[:, 3].rearrange("p t (g e) -> p t g e", g=4)
            tok16 = [P, 5, 4, 4]
            own(dve.tensor_tensor(prod, lg[:, :, 4:20].rearrange("p t (g e) -> p t g e", g=4),
                                  rt[:, 3].unsqueeze(3).to_broadcast(tok16), ALU.mult))
            own(dve.tensor_reduce(rt[:, 4], prod.rearrange("p t g e -> p t e g"), AX.X, ALU.add))
            first_best(rt[:, 4], 5, 7, 7, 8, 8)
            own(dve.scalar_tensor_tensor(rt[:, 9], rt[:, 8], -1.0e30, rt[:, 4], ALU.mult, ALU.add))
            first_best(rt[:, 9], 10, 9, 12, 13, 10)
            own(dve.tensor_tensor(rs1[:, 11], rs1[:, 9], rs1[:, 7], ALU.subtract))
            dve.sem_inc(rt_dve, 1)
            for r_ in range(2):
                own(dve.tensor_tensor(onehot[:, r_].rearrange("p t (g e) -> p t g e", g=4),
                                      rt[:, 3].unsqueeze(3).to_broadcast(tok16),
                                      rt[:, 8 if r_ == 0 else 13].unsqueeze(2).to_broadcast(tok16), ALU.mult))
            dve.tensor_tensor(onehot[:, 2], onehot[:, 0], onehot[:, 1], ALU.add).then_inc(oh_done, 1)
            dve.wait_ge(rt_act, 1)
            own(dve.tensor_reduce(rs1[:, 5], rt[:, 1], AX.X, ALU.add))
            own(dve.reciprocal(rs1[:, 6], rs1[:, 5]))
            dve.wait_ge(rt_act, 2)
            own(dve.tensor_scalar(rs1[:, 1], rs1[:, 0], 1.0, None, ALU.add))
            own(dve.reciprocal(rs1[:, 2], rs1[:, 1]))
            own(dve.tensor_tensor(cw[:, 0], rs1[:, 6], rs1[:, 2], ALU.mult))
            own(dve.tensor_tensor(cw[:, 1], cw[:, 0], rs1[:, 0], ALU.mult))
            dve.wait_ge(pos_pe, 1)
            own(dve.tensor_tensor(cmp6[:, :, :], psum[:, 6, 0:16].unsqueeze(2).to_broadcast([P, NE, COUNT_STEPS]),
                                  cst[:, 8:8 + COUNT_STEPS].unsqueeze(1).to_broadcast([P, NE, COUNT_STEPS]), ALU.is_gt))
            own(dve.tensor_reduce(ends[:, 0], cmp6[:, :, :], AX.X, ALU.add))
            for n, sh in enumerate((1, 2, 4, 8)):
                own(dve.tensor_copy(ends[:, n + 1, 0:sh], ends[:, n, 0:sh]))
                own(dve.tensor_tensor(ends[:, n + 1, sh:NE], ends[:, n, sh:NE], ends[:, n, 0:NE - sh], ALU.add))
            own(dve.tensor_tensor(ends[:, 5], ends[:, 4], ends[:, 0], ALU.subtract))
            own(dve.scalar_tensor_tensor(onehot[:, 3], ends[:, 5].unsqueeze(1).to_broadcast([P, 5, NE]), float(TS),
                                         psum[:, 5, 0:80].rearrange("p (t n) -> p t n", n=16), ALU.mult, ALU.add))
            for r_ in range(2):
                own(dve.tensor_tensor(onehot[:, 2], onehot[:, r_], onehot[:, 3], ALU.mult))
                own(dve.tensor_reduce(slotf[:, r_], onehot[:, 2], AX.X, ALU.add))
                own(dve.tensor_copy(sloti[:, r_], slotf[:, r_]))
            dve.sem_inc(slot_done, 1)
            shape = [1, TABLE, NE]
            own(dve.tensor_tensor(cmpt[:, :, :], ends[0:1, 4].unsqueeze(1).to_broadcast(shape),
                                  cst[0:1, 32:32 + TABLE].unsqueeze(2).to_broadcast(shape), ALU.is_le))
            own(dve.tensor_reduce(eidf[:, 0:TABLE], cmpt[:, :, :], AX.X, ALU.add))
            own(dve.tensor_scalar(eidf[:, 0:TABLE], eidf[:, 0:TABLE], float(NE - 1), None, ALU.min))
            own(dve.tensor_copy(tab[:, 0:TABLE], eidf[:, 0:TABLE]))
            own(dve.tensor_tensor(eidf[:, 32:32 + MAX_PAIRS], ends[0:1, 4, NE - 1:NE].to_broadcast([1, MAX_PAIRS]),
                                  cst[0:1, 16:16 + MAX_PAIRS], ALU.is_gt))
            own(dve.tensor_reduce(eidf[:, 47:48], eidf[:, 32:32 + MAX_PAIRS], AX.X, ALU.add))
            own(dve.tensor_copy(tab[:, TABLE:TABLE + 1], eidf[:, 47:48]))
            dve.sem_inc(tab_done, 1)

            pairs = dve.value_load(tab[0:1, TABLE:TABLE + 1], min_val=1, max_val=MAX_PAIRS)
            dve.sem_inc(hid_done, 2)
            dve.sem_inc(ye_ev1, 1)

            def rows_T_copy(slot):
                dve.tensor_copy(xgT[:, slot, 0:4, :].rearrange("p k n -> p (k n)"), psum[:, 0, 0:4 * TS])\
                   .then_inc(xgT_ev, 1)
                dve.tensor_copy(xgT[:, slot, 4:8, :].rearrange("p k n -> p (k n)"), psum[:, 1, 0:4 * TS])\
                   .then_inc(xgT_ev, 1)

            dve.wait_ge(xgT_pe, 2)
            rows_T_copy(0)
            with dve.Fori(0, pairs) as jp:
                for q in range(2):
                    dve.wait_ge(sil_done, 2 * jp + (q + 1))
                    dve.wait_ge(ye_pe, 4 * jp + (2 * q + 2))
                    dve.tensor_tensor(hid[:, q].rearrange("p f n -> p (f n)"), sil[:, q].rearrange("p f n -> p (f n)"),
                                      psum[:, 4 + q, 0:FC * TS], ALU.mult).then_inc(hid_done, 1)
                    dve.wait_ge(xgT_pe, 2 * jp + (q + 3))
                    rows_T_copy(1 - q)
                    dve.wait_ge(ye_pe, 4 * jp + (2 * q + 6))
                    dve.wait_ge(ye_out[q], 16 * jp + 16)
                    dve.tensor_copy(yev[:, q, 512:1024], psum[0:TS, 7, :]).then_inc(ye_ev1, 1)

            dve.wait_ge(nf_in, 16)
            for tt in range(TILES + 1):
                n = P if tt < TILES else NS
                s = tt % 2
                tab_ = tokt if tt < TILES else toks
                dve.wait_ge(yg_in[s], 32 * (tt // 2 + 1))
                own(dve.tensor_scalar(ya[0:n, s], ya[0:n, s], cw[0:n, 0, tt:tt + 1], None, ALU.mult))
                own(dve.scalar_tensor_tensor(ya[0:n, s], yb2[0:n, s], cw[0:n, 1, tt:tt + 1], ya[0:n, s],
                                             ALU.mult, ALU.add))
                own(dve.tensor_tensor(ya[0:n, s], ya[0:n, s], tab_[0:n, 2, :], ALU.mult))
                dve.tensor_tensor(x2[0:n, tt, :], x2[0:n, tt, :], ya[0:n, s], ALU.add).then_inc(f_mix, 1)
                dve.wait_ge(f_sq, tt + 1)
                dve.tensor_scalar(stat[0:n, tt:tt + 1], stat[0:n, tt:tt + 1], 1.0 / D, EPS, ALU.mult, ALU.add)\
                   .then_inc(f_ms, 1)
                dve.wait_ge(f_sqrt, tt + 1)
                own(dve.reciprocal(rstd[0:n, tt:tt + 1], rstd[0:n, tt:tt + 1]))
                dve.scalar_tensor_tensor(x2[0:n, tt, :], x2[0:n, tt, :], rstd[0:n, tt:tt + 1], tokt[0:n, 0, :],
                                         ALU.mult, ALU.mult).then_inc(f_y, 1)

        @block.gpsimd
        def _(pool):
            pool.memset(QB[:, :, :, :, :], 0.0).then_inc(qb_zero, 1)
            pool.wait_ge(qb_zero, 1)
            prompt_v = [[prompt_kv[g][kv][0, 0].rearrange("(n b a) h d -> b n a (h d)", b=4, a=TILES)
                         for kv in range(2)] for g in range(GROUPS)]

            def store(g, kv, c, src, done):
                lo = 24 if g == 0 else 0
                for b in range(4):
                    pool.dma_start(prompt_v[g][kv][b][:, :, P * c:P * c + P], src[32 * b + lo:32 * b + 32])\
                        .then_inc(done, 16)

            rotated = 0
            for G in range(2 * B_P + 8):
                m, t = divmod(G, 2)
                if m < B_P and kind(m) in "qk":
                    R = 4 * (m // 3) + 2 * (m % 3) + t
                    cols = slice(HALF * t, HALF * t + HALF)
                    if R == 0:
                        pool.wait_ge(rope_in, 48)
                    pool.wait_ge(bank_free[t], m + 1)
                    if R >= 2:
                        pool.wait_ge(rope_done, R - 1)
                    pool.tensor_tensor(t1[:, t, :], rb[:, t, :], ropec[:, cols], ALU.mult).then_inc(rot_done, 1)
                    pool.wait_ge(shuf_done, R + 1)
                    pool.tensor_tensor(shb[:, t, :], shb[:, t, :], ropes[:, cols], ALU.mult)\
                        .then_inc(rot_done, 1)
                    rotated += 2
                if t == 0 and 1 <= m and m - 1 < B_P and kind(m - 1) in "qk":
                    c, j = divmod(m - 1, 9)
                    g, kv = divmod(j, 3)
                    pool.wait_ge(rope_done, 4 * ((m - 1) // 3) + 2 * kv + 2)
                    if kv == 0:
                        pool.wait_ge(rot_done, rotated)
                        for h in range(2):
                            part = slice(HD * h, HD * h + HD)
                            pool.tensor_copy(QB[part, g, c, :, 8 * c + 4 * h:8 * c + 4 * h + 4],
                                             qT[part, c % 2, g, SEQ:NT].rearrange("p (b q) -> p b q", q=DEC_T))\
                                .then_inc(qb_done, 1)
                            pool.wait_ge(qb_done, 3 * ((m - 1) // 3) + h + 1)
                    else:
                        pool.tensor_copy(kTn[:, g, c, :], kT[:, c % 2, g, SEQ:NT]).then_inc(qb_done, 1)
                if t == 1 and 2 <= m < B_P + 2 and kind(m - 2) in "kv":
                    c, j = divmod(m - 2, 9)
                    g = j // 3
                    n = GROUPS * c + g
                    if kind(m - 2) == "k":
                        pool.wait_ge(kt_ev, n + 1)
                        store(g, 0, c, Kst[:, n % 2], k_out[n % 2])
                        pool.wait_ge(misc_ev, MISC[G - 1, 0] + 1)
                        pool.dma_start(kn_rows[g, :, P * c:P * c + P], Kns[:, n % 2]).then_inc(kn_out, 16)
                    else:
                        pool.wait_ge(vt_ev, n + 1)
                        store(g, 1, c, Vt[:, c % 2, :, g, :], v_out[c % 2])
            pool.wait_ge(misc_ev, MISC_ALL)
            for g in range(GROUPS):
                pool.dma_start(vn_rows[g], Vn[:, g].rearrange("p c n -> p (c n)")).then_inc(vn_out, 16)
            pool.wait_ge(vn_out, 16 * GROUPS)
            pool.wait_ge(kn_out, 16 * GROUPS * AC)
            for g in range(GROUPS):
                for kv, src in enumerate((kn_rows, vn_rows)):
                    dst = sample_kv[g][kv][0, :, WINDOWS[g] - DEC_T:].rearrange("b q h d -> b (q h d)")
                    pool.dma_start(dst, src[g].rearrange("(b q) n -> b (q n)", q=DEC_T)).then_inc(tail_out, 16)
            pool.wait_ge(lt_ev, 2)
            pool.dma_start(conv_p[0, 0], ltok[0:2, :]).then_inc(conv_out, 16)
            pool.dma_start(conv_s[0].rearrange("b r c -> (b r) c"), ltok[2:18, :]).then_inc(conv_out, 16)
            pool.wait_ge(conv_out, 32)
            pool.wait_ge(so_ev, 4)
            pool.memset(zrow[:, :], 0.0).then_inc(zrow_done, 1)
            pool.wait_ge(xz_out, 16)
            pool.wait_ge(slot_done, 1)
            pool.wait_ge(h2_done, TILES + 1)
            for r_ in range(2):
                for tt in range(TILES + 1):
                    n = P if tt < TILES else NS
                    pool.indirect_dma_start(x_rows, bass.IndirectOffsetOnAxis(sloti[0:n, r_, tt:tt + 1], 0),
                                            h2[0:n, tt, :], None).then_inc(disp_out, 16)
            pool.wait_ge(tab_done, 1)
            pairs = pool.value_load(tab[0:1, TABLE:TABLE + 1], min_val=1, max_val=MAX_PAIRS)
            for k in range(2):
                pool.wait_ge(ye_out[k], 16 * pairs + 16)
                pool.sem_inc(all_stored, 1)
            for tt in range(TILES + 1):
                n = P if tt < TILES else NS
                if tt >= 2:
                    pool.wait_ge(f_mix, tt - 1)
                for r_, dst in enumerate((ya, yb2)):
                    pool.indirect_dma_start(dst[0:n, tt % 2], None, y_rows,
                                            bass.IndirectOffsetOnAxis(sloti[0:n, r_, tt:tt + 1], 0))\
                        .then_inc(yg_in[tt % 2], 16)


_INS = ['x_prompt', 'x_sample', 'cache_k1', 'cache_v1', 'cache_k2', 'cache_v2', 'cache_k3', 'cache_v3', 'state_conv',
        'c_prompt', 'c_sample', 'norm1_g', 'norm2_g', 'normf_g', 'w_ada', 'b_ada', 'w_in', 'conv_w', 'w_conv_out',
        'w_attn_out', 'w_o', 'w_rg', 'b_rg', 'w_re', 'b_re', 'w1', 'w3', 'w2']


def _kv(b, rows):
    return (1, b, rows, HEADS, HD)


_OUTS = [(1, SEQ, D), (DEC_B, DEC_T, D)] \
    + [_kv(1, min(w, SEQ)) for w in WINDOWS for _ in range(2)] + [(1, 1, 2, D)] \
    + [_kv(DEC_B, w) for w in WINDOWS for _ in range(2)] + [(1, DEC_B, 2, D)]


def _constants():
    import numpy as np

    col = np.arange(SEQ)
    time = 16 * (col % 32) + 4 * (col // 32 % 4) + col // P
    pos = np.concatenate([time, 2048 + np.arange(NS) % DEC_T]).astype(np.float32)
    freq = np.power(np.float32(500000.0), -np.arange(ROT, dtype=np.float32) / np.float32(ROT)).astype(np.float32)
    ang = (pos[:, None] * freq[None, :]).astype(np.float32).astype(np.float64)
    ropec = np.ones((P, NT), np.float32)
    ropes = np.zeros((P, NT), np.float32)
    for h in range(2):
        for i in range(ROT):
            for s, sign in ((0, -1.0), (ROT, 1.0)):
                ropec[HD * h + s + i] = np.cos(ang[:, i])
                ropes[HD * h + s + i] = sign * np.sin(ang[:, i])
    off = np.float32(-1.0e30)
    maskp = np.full((P, TILES, KEYS_P), off, np.float32)
    for a in range(TILES):
        tq = time[P * a:P * a + P][:, None]
        back = tq - time[None, :]
        maskp[:, a, 0:SEQ][(back >= 0) & (back <= WINDOWS[0])] = 0
        back = tq - time[P * a:P * a + P][None, :]
        for g, dil in ((1, 4), (2, 16)):
            view = maskp[:, a, SEQ + P * (g - 1):SEQ + P * g]
            view[(back >= 0) & (back % dil == 0) & (back <= WINDOWS[g])] = 0
    masks = np.full((P, 2, KEYS_S), off, np.float32)
    part = np.arange(P)
    j, q = part // NS, part % DEC_T
    row = np.arange(P)
    for half in range(2):
        m = masks[:, half]
        for r in range(DEC_T):
            m[q == r, P * r:P * r + P] = 0
            m[q == r, 4 * P + P * r:4 * P + P * r + P] = 0
        m[:, 8 * P:9 * P][row[None, :] >= q[:, None]] = 0
        new = np.arange(NS)
        own = (new // DEC_T)[None, :] == 4 * half + j[:, None]
        for g in range(GROUPS):
            ok = own & ((new % DEC_T)[None, :] <= q[:, None] if g == 0 else (new % DEC_T)[None, :] == q[:, None])
            m[:, 9 * P + NS * g:9 * P + NS * g + NS][ok] = 0
    small = np.zeros((P, 96), np.float32)
    small[:, 0:4] = [4, 3, 2, 1]
    small[:, 8:8 + COUNT_STEPS] = TS * np.arange(COUNT_STEPS)
    small[:, 16:16 + MAX_PAIRS] = 2 * np.arange(MAX_PAIRS)
    small[:, 32:32 + TABLE] = np.arange(TABLE)
    bf = lambda a: (np.ascontiguousarray(a).view(np.uint32) >> 16).astype(np.uint16)
    return {
        "k_ident": np.eye(P, dtype=np.float32), "k_tri": np.triu(np.ones((P, P), np.float32), 1),
        "k_small": small, "k_ropec": ropec, "k_ropes": ropes, "k_maskp": bf(maskp), "k_masks": bf(masks),
    }


def kernel(**inputs):
    import numpy as _np
    import concourse.bacc as _bacc
    from concourse import mybir as _mybir
    from concourse.bass_utils import run_bass_kernel_spmd as _run

    nc = _bacc.Bacc("TRN2", target_bir_lowering=False, num_devices=1)
    arrays, args = {}, []
    given = {name: _np.ascontiguousarray(inputs[name]) for name in _INS}
    for name, a in {**given, **_constants()}.items():
        arrays[f"in_{name}_dram"] = a
        args.append(nc.dram_tensor(f"in_{name}_dram", a.shape, _mybir.dt.from_np(a.dtype), kind="ExternalInput").ap())
    for i, shape in enumerate(_OUTS):
        args.append(nc.dram_tensor(f"out_{i}_dram", shape, _mybir.dt.float32, kind="ExternalOutput").ap())
    _build(nc, *args)
    r = _run(nc, [arrays], core_ids=[0])
    return tuple(r.results[0][f"out_{i}_dram"] for i in range(len(_OUTS)))
```

```python
from contextlib import ExitStack

import concourse.bass as bass
from concourse import mybir

F32 = mybir.dt.float32
F32R = mybir.dt.float32r
BF16 = mybir.dt.bfloat16
U16 = mybir.dt.uint16
I32 = mybir.dt.int32
ALU = mybir.AluOpType
ACT = mybir.ActivationFunctionType
AX = mybir.AxisListType

P = 128
D = 1024
KC = D // P
SEQ = 512
DEC_B, DEC_T = 8, 4
NS = DEC_B * DEC_T
NT = SEQ + NS
HALF = NT // 2
TILES = SEQ // P
HD = 64
HEADS = 8
GROUPS = 3
AC = HEADS * HD // P
WINDOWS = (128, 512, 2048)
SCALE = HD ** -0.5
EPS = 1e-6
NEG = -3.0e38
NE, DE = 16, 512
FC = DE // P
TS = 96
MAX_TILES = NE + (2 * NT) // TS
MAX_PAIRS = (MAX_TILES + 1) // 2
XTILES = 2 * MAX_PAIRS + 1
TABLE = 32
COUNT_STEPS = -(-NT // TS) - 1

COL_Q = 3 * D
COL_GC = COL_Q + 3 * GROUPS * AC * P
COL_GA = COL_GC + D

B_P = 9 * AC
A_P = 3 * KC
C_P = 4 * KC
D_P = KC
A0, C0 = B_P, B_P + A_P
D0 = C0 + C_P
N_P = D0 + D_P
RING = 4
LEAD = 3
ADA_FIRST = 2 * KC
ADA_ALL = 6 * KC
SLOTS_B = 2 * 9
STEPS = 9
UNITS = 2 * TILES
KEYS_P = SEQ + 2 * P
KEYS_S = 2 * SEQ + P + GROUPS * NS
ROT = 8


def _build(nc, x_prompt, x_sample, cache_k1, cache_v1, cache_k2, cache_v2, cache_k3, cache_v3,
           state_conv, c_prompt, c_sample, norm1_g, norm2_g, normf_g, w_ada, b_ada, w_in, conv_w,
           w_conv_out, w_attn_out, w_o, w_rg, b_rg, w_re, b_re, w1, w3, w2,
           k_ident, k_tri, k_small, k_ropec, k_ropes, k_maskp, k_masks,
           y_prompt, y_sample, k1_p, v1_p, k2_p, v2_p, k3_p, v3_p, conv_p,
           k1_s, v1_s, k2_s, v2_s, k3_s, v3_s, conv_s):
    caches = ((cache_k1, cache_v1), (cache_k2, cache_v2), (cache_k3, cache_v3))
    prompt_kv = ((k1_p, v1_p), (k2_p, v2_p), (k3_p, v3_p))
    sample_kv = ((k1_s, v1_s), (k2_s, v2_s), (k3_s, v3_s))

    x_rows = nc.dram_tensor("x_rows", [XTILES * TS, D], F32, kind="Internal").ap()
    y_rows = x_rows

    base = -(-nc.sbuf_base // 64) * 64
    top = nc.sbuf_top

    class Region:
        def __init__(self, at):
            self.at = at

        def __call__(self, name, shape, dt=F32):
            n = 2 if dt in (BF16, U16) else 4
            for s in shape[1:]:
                n *= s
            t = nc.alloc_sbuf_tensor_at(name, shape, dt, offset=self.at)
            self.at += -(-n // 32) * 32
            assert self.at <= top, (name, self.at, top)
            return t

    keep = Region(base)
    ident = keep("ident", [P, P])
    small = keep("small", [P, 96])
    cT = keep("cT", [P, KC, 9])
    stT = keep("stT", [P, KC, 2 * DEC_B])
    modT = keep("modT", [P, ADA_ALL, 9])
    mrow = keep("mrow", [9, 2, 2 * P])
    A1 = keep("A1", [P, KC, 9])
    A2 = keep("A2", [P, KC, 9])
    last2 = keep("last2", [P, KC, 2 + 2 * DEC_B])
    stat = keep("stat", [P, 8])
    rstd = keep("rstd", [P, 8])
    oT_at = keep.at
    oT = keep("oT", [P, AC, NT])
    yb_at = keep.at
    adar = Region(yb_at)("adar", [P, RING, KC, P])
    yb = keep("yb", [P, KC, NT])
    hHi = keep("hHi", [P, KC, NT], F32R)
    hLo = keep("hLo", [P, KC, NT], F32R)
    wraw = keep("wraw", [P, RING, KC, P])
    whi = keep("whi", [P, RING, KC, P], F32R)
    wlo = keep("wlo", [P, RING, KC, P], F32R)
    c_region = keep.at
    QB = keep("QB", [P, GROUPS, AC, DEC_B, NS])
    kTn = keep("kTn", [P, GROUPS, AC, NS])
    Vn = keep("Vn", [GROUPS * NS, AC, P])

    r = Region(keep.at)
    xt = r("xt", [P, TILES + 1, D])
    hraw = r("hraw", [P, 2, KC, P])
    junk = r("junk", [P, D])
    ctok = r("ctok", [9, D])
    sttok = r("sttok", [2 * DEC_B, D])
    rows = r("rows", [88, P])

    r = Region(keep.at)
    ropec = r("ropec", [P, NT])
    ropes = r("ropes", [P, NT])
    maskp = r("maskp", [P, TILES, KEYS_P], U16)
    qT = r("qT", [P, 2, GROUPS, NT])
    kT = r("kT", [P, 2, GROUPS, NT])
    Vt = r("Vt", [P, 2, TILES, GROUPS, P])
    Kst = r("Kst", [P, 2, TILES, P])
    Kns = r("Kns", [NS, 2, P])
    vf = r("vf", [P, NT])
    pr = r("pr", [P, 2, KEYS_P])
    pTa = r("pTa", [P, 3 * P])
    pTb = r("pTb", [P, 3 * P])
    otok = r("otok", [P, P])
    nmx = r("nmx", [P, 2])
    nb = r("nb", [P, 2])
    rs = r("rs", [P, 2])
    ri = r("ri", [P, 2])
    rope_at = r.at
    rb = r("rb", [P, 2, HALF])
    shb = r("shb", [P, 2, HALF])
    t1 = r("t1", [P, 2, HALF])
    r = Region(rope_at)
    u_sb = r("u_sb", [P, 2, HALF])
    cu = r("cu", [P, NT])
    yv = r("yv", [P, NT])
    ext = r("ext", [P, DEC_B, 6])

    r = Region(keep.at)
    kvr = r("kvr", [P, RING, 4 * HEADS * HD])
    kTs_at = r.at
    kTs = r("kTs", [P, RING, 4 * P])
    ps_ = r("ps_", [P, 2, KEYS_S])
    osm = [ps_[:, n, 0:4 * P] for n in range(2)]
    pTs_at = r.at
    pTs0 = r("pTs0", [P, 9, P])
    pTn0 = r("pTn0", [GROUPS * NS, P])
    masks = r("masks", [P, 2, KEYS_S], U16)
    sst = r("sst", [P, 2, 4])
    sample_end = r.at
    ltok = Region(pTs_at)("ltok", [2 + 2 * DEC_B, D])
    r = Region(kTs_at)
    pTs1 = r("pTs1", [P, 9, P])
    pTn1 = r("pTn1", [GROUPS * NS, P])
    pTs, pTn = (pTs0, pTs1), (pTn0, pTn1)

    toks_at = top - KC * NT * 4
    toks_at -= toks_at % 32
    assert sample_end <= toks_at
    zrow = Region(top - 2048 - 64)("zrow", [P, 512])
    ybHi = Region(toks_at)("ybHi", [P, KC, NT], F32R)
    ybLo = Region(yb_at)("ybLo", [P, KC, NT], F32R)
    r = Region(c_region)
    mixLo = r("mixLo", [P, KC, NT], F32R)
    x2_at = r.at
    gyc = r("gyc", [P, 2, HALF])
    gsg = r("gsg", [P, 2, HALF])
    gm1 = r("gm1", [P, 2, HALF])
    gmx = r("gmx", [P, 2, HALF])
    oHi = r("oHi", [P, AC, NT], F32R)
    oLo = r("oLo", [P, AC, NT], F32R)

    r = Region(x2_at)
    x2 = r("x2", [P, TILES + 1, D])
    tokt = r("tokt", [P, 3, D])
    h2_at = r.at
    mixHi = r("mixHi", [P, KC, NT], F32R)
    bcp = r("bcp", [P, KC, P])
    bcs = r("bcs", [P, KC, NS])
    op = r("op", [P, 2, NT])
    assert r.at <= toks_at
    r = Region(toks_at)
    toks = r("toks", [NS, 3, D])
    wr = r("wr", [P, KC, 20])
    tri = r("tri", [P, P])
    ones = r("ones", [P, P])
    br = r("br", [P, 20])
    cst = r("cst", [P, 96])
    r = Region(h2_at)
    h2 = r("h2", [P, TILES + 1, D])
    lg = r("lg", [P, 5, 20])
    rt = r("rt", [P, 24, 5, 4])
    rs1 = r("rs1", [P, 12, 5])
    onehot = r("onehot", [P, 4, 5, NE])
    cmp6 = r("cmp6", [P, NE, COUNT_STEPS])
    ends = r("ends", [P, 7, NE])
    cmpt = r("cmpt", [1, TABLE, NE])
    eidf = r("eidf", [1, TABLE + 16])
    tab = r("tab", [1, TABLE + 4], I32)
    slotf = r("slotf", [P, 2, 5])
    sloti = r("sloti", [P, 2, 5], I32)
    cw = r("cw", [P, 2, 5])
    assert r.at <= toks_at

    r = Region(oT_at)
    e1 = r("e1", [P, 2, KC, DE])
    e3 = r("e3", [P, 2, KC, DE])
    e2 = r("e2", [P, 2, FC, D])
    h2T_at = r.at
    xg = r("xg", [TS, 2, D])
    xgT = r("xgT", [P, 2, KC, TS])
    sil = r("sil", [P, 2, FC, TS])
    hid = r("hid", [P, 2, FC, TS])
    yev = r("yev", [TS, 2, D])
    assert r.at <= x2_at
    r = Region(h2T_at)
    h2T = r("h2T", [P, 2, KC, P])
    junk2 = r("junk2", [P, D])
    r = Region(oT_at)
    ya = r("ya", [P, 2, D])
    yb2 = r("yb2", [P, 2, D])
    junk3 = r("junk3", [P, D])

    psum = nc.alloc_psum_tensor("psum", [P, 8, 512], F32)
    BANK_S, BANK_PT, BANK_O, BANK_KV, BANK_MISC = 2, 4, 5, 6, 7
    score = psum[:, BANK_S:BANK_S + 2, :].rearrange("p b n -> p (b n)")
    score_s = [psum[:, 2 + 3 * n:5 + 3 * n, :].rearrange("p b n -> p (b n)") for n in range(2)]

    win = w_in[0].rearrange("(k p) n -> p k n", p=P)
    wada = w_ada[0].rearrange("(k p) n -> p k n", p=P)
    wco = w_conv_out[0].rearrange("(k p) n -> p k n", p=P)
    wao = w_attn_out[0].rearrange("(k p) n -> p k n", p=P)
    wgc = win[:, :, COL_GC:COL_GC + D]
    wga = win[:, :, COL_GA:COL_GA + D]
    wo = w_o[0].rearrange("(k p) n -> p k n", p=P)
    w1_v = w1[0].rearrange("g e (k p) f -> (g e) p k f", p=P)
    w3_v = w3[0].rearrange("g e (k p) f -> (g e) p k f", p=P)
    w2_v = w2[0].rearrange("g e (k p) f -> (g e) p k f", p=P)
    xp_v = x_prompt[0].rearrange("(n b a) d -> a b n d", b=4, a=TILES)
    yp_v = y_prompt[0].rearrange("(n b a) d -> a b n d", b=4, a=TILES)
    xs_v = x_sample.rearrange("b q d -> (b q) d")
    ys_v = y_sample.rearrange("b q d -> (b q) d")

    def piece_source(m):
        if m < A0:
            c, j = divmod(m, 9)
            g, kv = divmod(j, 3)
            col = COL_Q + GROUPS * AC * P * kv + AC * P * g + P * c
            return win[:, :, col:col + P]
        if m < C0:
            f, j = divmod(m - A0, 3)
            return win[:, :, D * j + P * f:D * j + P * f + P]
        assert m >= D0
        return wo[:, :, P * (m - D0):P * (m - D0) + P]

    def branch_source(j, cols):
        if j == 0:
            return wco[:, :, cols], wraw[:, 0]
        if j == 2:
            return wao[:, :, cols], wraw[:, 2, 0:AC]
        return (wgc if j == 1 else wga)[:, :, cols], wraw[:, j]

    kn_rows = nc.dram_tensor("kn_rows", [GROUPS, NS, AC * P], F32, kind="Internal").ap()
    vn_rows = nc.dram_tensor("vn_rows", [GROUPS, NS, AC * P], F32, kind="Internal").ap()

    SHIFTS = []
    for g in (2, 1):
        rows_g = WINDOWS[g] - DEC_T
        parts = 4 if g == 2 else 1
        n = rows_g // parts
        for b in range(DEC_B):
            for kv in range(1 if g == 2 else 2):
                for i in range(parts):
                    src = caches[g][kv][0, b, DEC_T + i * n:DEC_T + (i + 1) * n].rearrange("r h d -> (r h d)")
                    dst = sample_kv[g][kv][0, b, i * n:(i + 1) * n].rearrange("r h d -> (r h d)")
                    SHIFTS.append((dst.rearrange("(x y) -> x y", x=64), src.rearrange("(x y) -> x y", x=64)))
    for kv in range(2):
        src = caches[0][kv][0, :, DEC_T:].rearrange("b r h d -> b (r h d)")
        dst = sample_kv[0][kv][0, :, 0:WINDOWS[0] - DEC_T].rearrange("b r h d -> b (r h d)")
        SHIFTS.append((dst.rearrange("b (x y) -> b x y", x=4), src.rearrange("b (x y) -> b x y", x=4)))

    SHIFTS_AB = len(SHIFTS)
    assert SHIFTS_AB <= C0

    kv_units = [(half, kv, j, g) for kv in range(2) for half in range(2) for j in range(4) for g in (1, 2, 0)]
    K_COL = {1: 0, 2: 4 * P, 0: 8 * P}
    K_TILE = {1: 0, 2: 4, 0: 8}
    NEW_COL = 9 * P

    def cache_source(w):
        half, kv, j, g = kv_units[w]
        v = caches[g][kv][0, 4 * half + j]
        if g == 0:
            return v.rearrange("n h d -> n (h d)")
        if g == 1:
            return v.rearrange("(n r) h d -> n (r h d)", r=4)
        return v.rearrange("(n r) h d -> n r (h d)", r=16)[:, 0:DEC_T, :]

    def kv_tiles(g):
        return 1 if g == 0 else 4

    def kind(m):
        if m < A0:
            return "qkv"[m % 3]
        return ("u", "c", "b")[(m - A0) % 3]

    def unit_at(step):
        if not 0 <= step < STEPS * AC or step % STEPS == STEPS - 1:
            return None
        c, k = divmod(step, STEPS)
        return c * UNITS + k, c, k // 2, k % 2

    def step_of(G):
        return (G - SLOTS_B) // 2 if G >= SLOTS_B else -9

    with ExitStack() as ctx:
        def sem(name):
            return ctx.enter_context(nc.semaphore(name))

        cst_in = sem("cst_in")
        x_in = sem("x_in")
        rope_in = sem("rope_in")
        ada_in = [sem(f"ada_in{k}") for k in range(RING)]
        raw_in = [sem(f"raw_in{k}") for k in range(RING)]
        silu_done = sem("silu_done")
        first_T = sem("first_T")
        first_ev = sem("first_ev")
        ada_pe = sem("ada_pe")
        ada_ev = sem("ada_ev")
        mrow_done = sem("mrow_done")
        mT_pe = sem("mT_pe")
        sq_done = sem("sq_done")
        ms_done = sem("ms_done")
        sqrt_done = sem("sqrt_done")
        xn_done = sem("xn_done")
        xT_pe = sem("xT_pe")
        hraw_done = sem("hraw_done")
        hhi_done = sem("hhi_done")
        hlo_done = sem("hlo_done")
        dve_local = sem("dve_local")
        hi_done = sem("hi_done")
        lo_done = sem("lo_done")
        grp = sem("grp")
        bank_free = [sem("bank_free0"), sem("bank_free1")]
        shuf_done = sem("shuf_done")
        rot_done = sem("rot_done")
        rope_done = sem("rope_done")
        qb_zero = sem("qb_zero")
        qb_done = sem("qb_done")
        kt_pe = sem("kt_pe")
        kt_ev = sem("kt_ev")
        vt_pe = sem("vt_pe")
        vt_ev = sem("vt_ev")
        k_out = [sem("k_out0"), sem("k_out1")]
        v_out = [sem("v_out0"), sem("v_out1")]
        misc_pe = sem("misc_pe")
        misc_ev = sem("misc_ev")
        s_pe = sem("s_pe")
        s_mx = sem("s_mx")
        s_nb = sem("s_nb")
        s_exp = sem("s_exp")
        pta_pe = sem("pta_pe")
        pta_ev = sem("pta_ev")
        pva_pe = sem("pva_pe")
        ptb_pe = sem("ptb_pe")
        ptb_ev = sem("ptb_ev")
        pvb_pe = sem("pvb_pe")
        rec_done = sem("rec_done")
        o_ev = sem("o_ev")
        cu_done = sem("cu_done")
        shift_out = sem("shift_out")
        conv_out = sem("conv_out")
        mask_in = sem("mask_in")
        kv_in = [sem(f"kv_in{k}") for k in range(RING)]
        osm_done = sem("osm_done")
        orow_pe = sem("orow_pe")
        ktr_pe = sem("ktr_pe")
        ktr_act = sem("ktr_act")
        ktr_dve = sem("ktr_dve")
        ss_pe = sem("ss_pe")
        ssn_pe = sem("ssn_pe")
        ss_mx = sem("ss_mx")
        ss_nb = sem("ss_nb")
        ss_exp = sem("ss_exp")
        ss_p = sem("ss_p")
        spt_pe = sem("spt_pe")
        spt_ev = sem("spt_ev")
        spv_pe = sem("spv_pe")
        so_pe = sem("so_pe")
        so_ev = sem("so_ev")
        lt_pe = sem("lt_pe")
        lt_ev = sem("lt_ev")
        yo_hi = sem("yo_hi")
        yo_lo = sem("yo_lo")
        g_m1 = sem("g_m1")
        g_m2 = sem("g_m2")
        g_mx = sem("g_mx")
        g_hi = sem("g_hi")
        g_lo = sem("g_lo")
        xr_in = sem("xr_in")
        late_in = sem("late_in")
        op_done = sem("op_done")
        opT_pe = sem("opT_pe")
        x2_half = sem("x2_half")
        x2_done = sem("x2_done")
        op_half = sem("op_half")
        bc_done = sem("bc_done")
        bcT_pe = sem("bcT_pe")
        bcT_ev = sem("bcT_ev")
        ss2_done = sem("ss2_done")
        ms2_done = sem("ms2_done")
        sqrt2_done = sem("sqrt2_done")
        h2_done = sem("h2_done")
        h2T_pe = sem("h2T_pe")
        h2T_ev = sem("h2T_ev")
        lg_pe = sem("lg_pe")
        rt_dve = sem("rt_dve")
        rt_act = sem("rt_act")
        oh_done = sem("oh_done")
        pos_pe = sem("pos_pe")
        slot_done = sem("slot_done")
        tab_done = sem("tab_done")
        zrow_done = sem("zrow_done")
        xz_out = sem("xz_out")
        disp_out = sem("disp_out")
        xg_in = [sem("xg_in0"), sem("xg_in1")]
        e1_in = [sem("e1_in0"), sem("e1_in1")]
        e3_in = [sem("e3_in0"), sem("e3_in1")]
        e2_in = [sem("e2_in0"), sem("e2_in1")]
        xgT_pe = sem("xgT_pe")
        xgT_ev = sem("xgT_ev")
        a_pe = sem("a_pe")
        ab_pe = sem("ab_pe")
        sil_done = sem("sil_done")
        hid_done = sem("hid_done")
        ye_pe = sem("ye_pe")
        ye_ev0 = sem("ye_ev0")
        ye_ev1 = sem("ye_ev1")
        ye_out = [sem("ye_out0"), sem("ye_out1")]
        yg_in = [sem("yg_in0"), sem("yg_in1")]
        nf_in = sem("nf_in")
        f_mix = sem("f_mix")
        f_sq = sem("f_sq")
        f_ms = sem("f_ms")
        f_sqrt = sem("f_sqrt")
        f_y = sem("f_y")
        y_out = sem("y_out")
        otr_pe = sem("otr_pe")
        kn_pe = sem("kn_pe")
        kn_ev = sem("kn_ev")
        kn_out = sem("kn_out")
        stat_init = sem("stat_init")
        tail_out = sem("tail_out")
        all_stored = sem("all_stored")
        shiftc = sem("shiftc")
        vn_out = sem("vn_out")

        block = ctx.enter_context(nc.Block())

        def misc_before(G, part):
            n = 0
            for g in range(G + 1):
                for q in range(4):
                    if (g, q) >= (G, part):
                        return n
                    n += misc_use(g, q)
            return n

        def misc_use(G, part):
            m = G // 2
            if part == 0:
                return G % 2 == 0 and 2 <= m < B_P + 2 and kind(m - 2) in "kv"
            if part == 1:
                u = unit_at(step_of(G) - 2)
                return G % 2 == 1 and u is not None and u[3] == 1
            if part == 2:
                return G % 2 == 1 and m < ADA_ALL - ADA_FIRST
            return G % 2 == 0 and 1 <= m <= ADA_ALL - ADA_FIRST

        MISC = {(G, q): misc_before(G, q) for G in range(2 * C0) for q in range(4) if misc_use(G, q)}
        MISC_ALL = len(MISC)

        @block.sync
        def _(sp):
            sp.dma_start(ident[:, :], k_ident).then_inc(cst_in, 16)
            sp.dma_start(ctok[0:1, :], c_prompt).then_inc(cst_in, 16)
            sp.dma_start(ctok[1:9, :], c_sample).then_inc(cst_in, 16)
            sp.dma_start(rows[0:48, :], b_ada[0].rearrange("(c p) -> c p", p=P)).then_inc(cst_in, 16)
            sp.dma_start(rows[48:56, :], norm1_g[0].rearrange("(c p) -> c p", p=P)).then_inc(cst_in, 16)
            sp.dma_start(rows[56:64, :], norm2_g[0].rearrange("(c p) -> c p", p=P)).then_inc(cst_in, 16)
            sp.dma_start(rows[64:88, :], conv_w[0].rearrange("j (c p) -> (j c) p", p=P)).then_inc(cst_in, 16)
            sp.dma_start(sttok[:, :], state_conv[0].rearrange("b r d -> (b r) d")).then_inc(cst_in, 16)
            for k in range(RING):
                sp.dma_start(adar[:, k], wada[:, :, P * k:P * k + P]).then_inc(ada_in[k], 16)
            for a in range(TILES):
                for b in range(4):
                    sp.dma_start(xt[32 * b:32 * b + 32, a, :], xp_v[a, b]).then_inc(x_in, 16)
            sp.dma_start(xt[0:NS, TILES, :], xs_v).then_inc(x_in, 16)
            with sp.Fori(1, ADA_FIRST // RING) as i:
                for k in range(RING):
                    sp.wait_ge(ada_pe, 4 * i + (k - 3))
                    sp.dma_start(adar[:, k], wada[:, :, bass.ds((4 * i + k) * P, P)]).then_inc(ada_in[k], 16)
            for m in range(C0):
                if m == RING:
                    sp.wait_ge(hlo_done, TILES + 1)
                    sp.wait_ge(first_ev, 3)
                    sp.dma_start(ropec[:, :], k_ropec).then_inc(rope_in, 16)
                    sp.dma_start(ropes[:, :], k_ropes).then_inc(rope_in, 16)
                    sp.dma_start(maskp[:, :, :], k_maskp).then_inc(rope_in, 16)
                if m >= RING:
                    sp.wait_ge(lo_done, m - RING + 1)
                sp.dma_start(wraw[:, m % RING], piece_source(m)).then_inc(raw_in[m % RING], 16)
                if m < ADA_ALL - ADA_FIRST:
                    n = ADA_FIRST + m
                    sp.wait_ge(ada_pe, n - RING + 1)
                    sp.dma_start(adar[:, n % RING], wada[:, :, P * n:P * n + P]).then_inc(ada_in[n % RING], 16)
                if m < SHIFTS_AB:
                    dst, src = SHIFTS[m]
                    sp.dma_start(dst, src).then_inc(shift_out, 16)
                else:
                    if m == SHIFTS_AB:
                        sp.wait_ge(zrow_done, 1)
                    n0, n1 = (XTILES * (m - SHIFTS_AB + n) // (C0 - SHIFTS_AB) for n in range(2))
                    zdst = x_rows[TS * n0:TS * n1].rearrange("(p r) (o n) -> p (r o) n", p=TS, n=512)
                    zsrc = zrow[0:TS, :].rearrange("p (o n) -> p o n", o=1)
                    sp.dma_start(zdst, zsrc.to_broadcast([TS, 2 * (n1 - n0), 512])).then_inc(xz_out, 16)
            for m in range(C0, C0 + RING):
                sp.wait_ge(lo_done, m - RING + 1)
                src, dst = branch_source(m - C0, slice(0, P))
                sp.dma_start(dst, src).then_inc(raw_in[m % RING], 16)
            sp.wait_ge(o_ev, UNITS * AC)
            sp.wait_ge(otr_pe, TILES * AC)
            for k in range(2):
                sp.wait_ge(k_out[k], 64 * (GROUPS * AC // 2))
                sp.wait_ge(v_out[k], 64 * GROUPS * (AC // 2))
            sp.dma_start(masks[:, :, :], k_masks).then_inc(mask_in, 16)
            for w, (half, kv, j, g) in enumerate(kv_units):
                if w >= RING:
                    h0, kv0, j0, g0 = kv_units[w - RING]
                    done = 12 * h0 + 3 * j0 + (1, 2, 0).index(g0) + 1
                    if kv0 == 0:
                        sp.wait_ge(ktr_pe, AC * done)
                    else:
                        sp.wait_ge(spv_pe, done)
                src = cache_source(w)
                dst = kvr[:, w % RING, 0:kv_tiles(g) * 512]
                if g == 2:
                    dst = dst.rearrange("p (r n) -> p r n", n=512)
                sp.dma_start(dst, src).then_inc(kv_in[w % RING], 16)
            def shift_v3(b, j):
                n = (WINDOWS[2] - DEC_T) // 4
                src = cache_v3[0, b, DEC_T + j * n:DEC_T + (j + 1) * n].rearrange("b r h d -> (b r h d)")
                dst = v3_s[0, b, j * n:(j + 1) * n].rearrange("b r h d -> (b r h d)")
                sp.dma_start(dst.rearrange("(x y) -> x y", x=64), src.rearrange("(x y) -> x y", x=64))\
                    .then_inc(shiftc, 16)

            with sp.Fori(0, KC - 1) as f:
                for j in range(RING):
                    shift_v3(bass.ds(f, 1), j)
                    sp.wait_ge(lo_done, 4 * f + (C0 + j + 1))
                    src, dst = branch_source(j, bass.ds(f * P + P, P))
                    sp.dma_start(dst, src).then_inc(raw_in[j], 16)
            for m in range(D0, N_P):
                sp.wait_ge(lo_done, m - RING + 1)
                sp.dma_start(wraw[:, m % RING], piece_source(m)).then_inc(raw_in[m % RING], 16)
                if m == D0 + RING - 1:
                    sp.wait_ge(grp, 2 * D0)
                    sp.wait_ge(g_lo, 2 * KC)
                    for a in range(TILES):
                        for b in range(4):
                            sp.dma_start(x2[32 * b:32 * b + 32, a, :], xp_v[a, b]).then_inc(xr_in, 16)
                    sp.dma_start(x2[0:NS, TILES, :], xs_v).then_inc(xr_in, 16)
            sp.dma_start(tri[:, :], k_tri).then_inc(late_in, 16)
            sp.dma_start(cst[:, :], k_small).then_inc(late_in, 16)
            sp.dma_start(wr[:, :, 0:4], w_rg[0].rearrange("(k p) n -> p k n", p=P)).then_inc(late_in, 16)
            sp.dma_start(wr[:, :, 4:20], w_re[0].rearrange("(k p) n -> p k n", p=P)).then_inc(late_in, 16)
            sp.dma_start(br[:, 0:4], b_rg.to_broadcast([P, 4])).then_inc(late_in, 16)
            sp.dma_start(br[:, 4:20], b_re.to_broadcast([P, 16])).then_inc(late_in, 16)
            sp.dma_start(e1[:, 0], w1_v[0]).then_inc(e1_in[0], 16)
            sp.dma_start(e3[:, 0], w3_v[0]).then_inc(e3_in[0], 16)
            sp.dma_start(e1[:, 1], w1_v[1]).then_inc(e1_in[1], 16)
            for j in range(RING):
                shift_v3(slice(KC - 1, KC), j)
            sp.wait_ge(grp, 2 * N_P)
            sp.dma_start(e2[:, 0], w2_v[0]).then_inc(e2_in[0], 16)
            sp.dma_start(e3[:, 1], w3_v[1]).then_inc(e3_in[1], 16)
            sp.dma_start(e2[:, 1], w2_v[1]).then_inc(e2_in[1], 16)
            sp.wait_ge(disp_out, 160)
            sp.dma_start(xg[:, 0, :], x_rows[0:TS, :]).then_inc(xg_in[0], 16)
            sp.dma_start(xg[:, 1, :], x_rows[TS:2 * TS, :]).then_inc(xg_in[1], 16)
            sp.wait_ge(h2_done, TILES + 1)
            sp.dma_start(tokt[:, 0, :], normf_g.rearrange("(a n) -> a n", a=1).to_broadcast([P, D])).then_inc(nf_in, 16)
            sp.wait_ge(tab_done, 1)
            pairs = sp.value_load(tab[0:1, TABLE:TABLE + 1], min_val=NE // 2, max_val=MAX_PAIRS)
            sp.wait_ge(xgT_pe, 2)
            sp.dma_start(xg[:, 0, :], x_rows[2 * TS:3 * TS, :]).then_inc(xg_in[0], 16)
            with sp.Fori(1, pairs) as jp:
                for q in range(2):
                    e = sp.value_load(tab[0:1, bass.ds(2 * jp + q, 1)], min_val=0, max_val=NE - 1)
                    sp.wait_ge(a_pe, 2 * jp + (q - 1))
                    sp.dma_start(e1[:, q], w1_v[bass.ds(e, 1)].rearrange("e p k f -> (e p) k f")).then_inc(e1_in[q], 16)
                    sp.wait_ge(ab_pe, 2 * jp + (q + 1))
                    sp.dma_start(e3[:, q], w3_v[bass.ds(e, 1)].rearrange("e p k f -> (e p) k f")).then_inc(e3_in[q], 16)
                    sp.wait_ge(xgT_pe, 2 * jp + (q + 1))
                    sp.dma_start(xg[:, 1 - q, :], x_rows[bass.ds((2 * jp + (q + 1)) * TS, TS), :])\
                        .then_inc(xg_in[1 - q], 16)
                    sp.wait_ge(ye_pe, 4 * jp + (2 * q + 2))
                    sp.dma_start(e2[:, q], w2_v[bass.ds(e, 1)].rearrange("e p k f -> (e p) k f")).then_inc(e2_in[q], 16)
            for tt in range(TILES + 1):
                sp.wait_ge(f_y, tt + 1)
                if tt < TILES:
                    for b in range(4):
                        sp.dma_start(yp_v[tt, b], x2[32 * b:32 * b + 32, tt, :]).then_inc(y_out, 16)
                else:
                    sp.dma_start(ys_v, x2[0:NS, tt, :]).then_inc(y_out, 16)
            sp.wait_ge(y_out, 16 * (4 * TILES + 1))
            sp.wait_ge(shift_out, 16 * SHIFTS_AB)
            sp.wait_ge(shiftc, 16 * 4 * KC)
            sp.wait_ge(conv_out, 32)
            sp.wait_ge(kn_out, 16 * GROUPS * AC)
            sp.wait_ge(vn_out, 16 * GROUPS)
            sp.wait_ge(tail_out, 16 * 2 * GROUPS)

        @block.tensor
        def _(pe):
            pe.wait_ge(cst_in, 128)
            pe.transpose(psum[:, 0, 0:88], rows[:, :], ident[0:88, 0:88]).then_inc(first_T, 1)
            pe.wait_ge(silu_done, 1)
            for k in range(KC):
                mm = pe.transpose(psum[:, 1, 16 * k:16 * k + 9], ctok[:, P * k:P * k + P], ident[0:9, 0:9])
            mm.then_inc(first_T, 1)
            for k in range(KC):
                mm = pe.transpose(psum[:, 2, 16 * k:16 * k + 16], sttok[:, P * k:P * k + P], ident[0:16, 0:16])
            mm.then_inc(first_T, 1)

            def modulation(slot, out):
                for k in range(KC):
                    mm = pe.matmul(out, cT[:, k, :], adar[:, slot, k, :], start=(k == 0), stop=(k == KC - 1))
                mm.then_inc(ada_pe, 1)

            def modulation_T(src, out):
                return pe.transpose(out, src, ident[0:9, 0:9])

            pe.wait_ge(first_ev, 3)
            with pe.Fori(0, ADA_FIRST // RING) as i:
                for k in range(RING):
                    pe.wait_ge(ada_in[k], 16 * i + 16)
                    if k % 2 == 0:
                        pe.wait_ge(mrow_done, 2 * i + (k // 2 + 1))
                    modulation(k, psum[0:9, 3 + k // 2, P * (k % 2):P * (k % 2) + P])
                for h in range(2):
                    pe.wait_ge(mrow_done, 2 * i + (h + 3))
                    pe.wait_ge(ada_ev, 2 * i + (h + 1))
                    for k in range(2):
                        mm = pe.matmul(psum[:, 5 + h, 16 * k:16 * k + 9], mrow[:, h, P * k:P * k + P], ident[0:9, 0:9],
                                       start=True, stop=True)
                    mm.then_inc(mT_pe, 1)

            pe.wait_ge(ada_ev, 2 + ADA_FIRST // 2)
            for tt in range(TILES + 1):
                n = P if tt < TILES else NS
                pe.wait_ge(xn_done, tt + 1)
                if tt >= 2:
                    pe.wait_ge(hraw_done, 2 * tt - 2)
                for k in range(KC):
                    mm = pe.transpose(psum[:, 2 * (tt % 2) + k // 4, P * (k % 4):P * (k % 4) + n],
                                      xt[0:n, tt, P * k:P * k + P], ident[0:n, 0:n])
                mm.then_inc(xT_pe, 1)
            pe.wait_ge(hlo_done, TILES + 1)

            def project(m, slot, xhi, xlo, t, k_n=KC, free=None):
                if free is not None:
                    pe.wait_ge(bank_free[t], free)
                cols = slice(HALF * t, HALF * t + HALF)
                for k in range(k_n):
                    for n, (w, x) in enumerate(((whi, xhi), (wlo, xhi), (whi, xlo))):
                        mm = pe.matmul(psum[:, t, 0:HALF], w[:, slot, k, :], x[:, k, cols],
                                       start=(k == 0 and n == 0), stop=(k == k_n - 1 and n == 2))
                mm.then_inc(grp, 1)

            def keys_values_T(G):
                m = G // 2 - 2
                c, j = divmod(m, 9)
                g, kv = divmod(j, 3)
                n = GROUPS * c + g
                if kind(m) == "k":
                    pe.wait_ge(rope_done, 4 * n + 4)
                    if n >= 1:
                        pe.wait_ge(vt_ev, n)
                    src = kT[:, c % 2, g, :]
                else:
                    pe.wait_ge(bank_free[0], m + 1)
                    pe.wait_ge(bank_free[1], m + 1)
                    pe.wait_ge(kt_ev, n + 1)
                    src = vf[:, :]
                for a in range(TILES):
                    mm = pe.transpose(psum[:, BANK_KV, P * a:P * a + P], src[:, P * a:P * a + P], ident[:, :])
                mm.then_inc(kt_pe if kind(m) == "k" else vt_pe, 1)
                if MISC[G, 0] > 0:
                    pe.wait_ge(misc_ev, MISC[G, 0])
                at = 0 if kind(m) == "k" else NS * g
                pe.matmul(psum[at:at + NS, BANK_MISC, 0:P], src[:, SEQ:NT], ident[:, :], start=True, stop=True)\
                    .then_inc(kn_pe, 1)

            def values_part(u, second):
                _, c, a, h = u
                for i in range(3):
                    n = 3 * second + i
                    g, tile_ = (0, n) if n < TILES else (n - TILES + 1, a)
                    mm = pe.matmul(psum[:, BANK_O, 0:HD], (pTb if second else pTa)[:, P * i:P * i + P],
                                   Vt[:, c % 2, tile_, g, HD * h:HD * h + HD], start=(n == 0), stop=(n == 5))
                return mm

            def probs_T(u, second):
                for i in range(3):
                    n = 3 * second + i
                    mm = pe.transpose(psum[:, BANK_PT, P * i:P * i + P], pr[:, u[0] % 2, P * n:P * n + P],
                                      ident[:, :])
                return mm

            def attend(G):
                step = step_of(G)
                if G % 2 == 0:
                    u = unit_at(step - 2)
                    if u:
                        pe.wait_ge(ptb_ev, u[0] + 1)
                        values_part(u, 1).then_inc(pvb_pe, 1)
                    u = unit_at(step)
                    if u:
                        n, c, a, h = u
                        pe.wait_ge(rope_done, 12 * (c + 1))
                        if n >= 1:
                            pe.wait_ge(s_mx, n)
                        rows_h = slice(HD * h, HD * h + HD)
                        q = [qT[rows_h, c % 2, g, P * a:P * a + P] for g in range(GROUPS)]
                        pe.matmul(score[:, 0:SEQ], q[0], kT[rows_h, c % 2, 0, 0:SEQ], start=True, stop=True)
                        for g in (1, 2):
                            mm = pe.matmul(score[:, SEQ + P * (g - 1):SEQ + P * g], q[g],
                                           kT[rows_h, c % 2, g, P * a:P * a + P], start=True, stop=True)
                        mm.then_inc(s_pe, 1)
                    u = unit_at(step - 1)
                    if u:
                        pe.wait_ge(s_exp, u[0] + 1)
                        if u[0] >= 1:
                            pe.wait_ge(ptb_ev, u[0])
                        probs_T(u, 0).then_inc(pta_pe, 1)
                else:
                    u = unit_at(step - 1)
                    if u:
                        pe.wait_ge(pta_ev, u[0] + 1)
                        pe.wait_ge(vt_ev, GROUPS * (u[1] + 1))
                        if u[0] >= 1:
                            pe.wait_ge(o_ev, u[0])
                        values_part(u, 0).then_inc(pva_pe, 1)
                        probs_T(u, 1).then_inc(ptb_pe, 1)
                    u = unit_at(step - 2)
                    if u and u[3] == 1:
                        pe.wait_ge(o_ev, u[0] + 1)
                        if MISC[G, 1] > 0:
                            pe.wait_ge(misc_ev, MISC[G, 1])
                        pe.transpose(psum[:, BANK_MISC, 0:P], otok[:, :], ident[:, :]).then_inc(otr_pe, 1)

            for G in range(2 * C0):
                m, t = divmod(G, 2)
                if misc_use(G, 0):
                    keys_values_T(G)
                attend(G)
                if misc_use(G, 2):
                    n = ADA_FIRST + m
                    if MISC[G, 2] > 0:
                        pe.wait_ge(misc_ev, MISC[G, 2])
                    pe.wait_ge(ada_in[n % RING], 16 * (n // RING + 1))
                    modulation(n % RING, psum[0:9, BANK_MISC, 0:P])
                if misc_use(G, 3):
                    pe.wait_ge(misc_ev, MISC[G, 3])
                    modulation_T(mrow[:, m % 2, 0:P], psum[:, BANK_MISC, 0:9]).then_inc(mT_pe, 1)
                if t == 0:
                    pe.wait_ge(lo_done, m + 1)
                project(m, m % RING, hHi, hLo, t, free=m if m >= 1 else None)

            pe.wait_ge(cu_done, 2 * KC)
            pe.wait_ge(misc_ev, MISC_ALL)
            for k in range(KC):
                mm = pe.transpose(psum[0:18, 6 + k // 4, P * (k % 4):P * (k % 4) + P], last2[:, k, :], ident[:, :])
            mm.then_inc(lt_pe, 1)

            pe.wait_ge(bank_free[0], C0)
            pe.wait_ge(bank_free[1], C0)
            pe.wait_ge(qb_done, 3 * GROUPS * AC)
            pe.wait_ge(lt_ev, 2)
            for half in range(2):
                chunks = [(3 * j + gi, j, g, ch) for j in range(4) for gi, g in enumerate((1, 2, 0)) for ch in range(AC)]

                def keys_T(n):
                    i, j, g, ch = chunks[n]
                    x = half * len(chunks) + n
                    w = 12 * half + i
                    if ch == 0:
                        pe.wait_ge(kv_in[w % RING], 16 * (w // RING + 1))
                    if x >= 2:
                        pe.wait_ge((ktr_act, ktr_dve)[x % 2], x // 2)
                    for r_ in range(kv_tiles(g)):
                        mm = pe.transpose(psum[:, x % 2, P * r_:P * r_ + P],
                                          kvr[:, w % RING, 512 * r_ + P * ch:512 * r_ + P * ch + P], ident[:, :])
                    mm.then_inc(ktr_pe, 1)

                def scores_s(n):
                    i, j, g, ch = chunks[n]
                    x = half * len(chunks) + n
                    pe.wait_ge((ktr_act, ktr_dve)[x % 2], x // 2 + 1)
                    w_ = P * kv_tiles(g)
                    pe.matmul(score_s[half][32 * j:32 * j + 32, K_COL[g]:K_COL[g] + w_], QB[:, g, ch, 4 * half + j, :],
                              kTs[:, x % RING, 0:w_], start=(ch == 0), stop=(ch == AC - 1)).then_inc(ss_pe, 1)

                for n in range(len(chunks) + 1):
                    if n < len(chunks):
                        keys_T(n)
                    if n >= 1:
                        scores_s(n - 1)
                for j in range(4):
                    for g in range(GROUPS):
                        for ch in range(AC):
                            mm = pe.matmul(score_s[half][32 * j:32 * j + 32, NEW_COL + NS * g:NEW_COL + NS * g + NS],
                                           QB[:, g, ch, 4 * half + j, :], kTn[:, g, ch, :],
                                           start=(ch == 0), stop=(ch == AC - 1))
                mm.then_inc(ssn_pe, 1)
            pe.wait_ge(ktr_act, len(chunks))
            pe.wait_ge(ktr_dve, len(chunks))
            for half in range(2):
                pe.wait_ge(ss_p, half + 1)
                for part in range(3 * half, 3 * half + 3):
                    if part >= 2:
                        pe.wait_ge(spt_ev, part - 1)
                    for i in range(4 if part % 3 < 2 else 2):
                        n = 4 * (part % 3) + i
                        if n < 9:
                            mm = pe.transpose(psum[:, part % 2, P * i:P * i + P], ps_[:, half, P * n:P * n + P], ident[:, :])
                        else:
                            mm = pe.transpose(psum[0:GROUPS * NS, part % 2, P * i:P * i + P],
                                              ps_[:, half, NEW_COL:NEW_COL + GROUPS * NS], ident[:, :])
                    mm.then_inc(spt_pe, 1)
                pe.wait_ge(spt_ev, 3 * half + 3)
                for i in range(12):
                    j, g = i // 3, (1, 2, 0)[i % 3]
                    w = 24 + 12 * half + i
                    out = psum[NS * j:NS * j + NS, 2 + half, :]
                    pe.wait_ge(kv_in[w % RING], 16 * (w // RING + 1))
                    for r_ in range(kv_tiles(g)):
                        mm = pe.matmul(out, pTs[half][:, K_TILE[g] + r_, NS * j:NS * j + NS],
                                       kvr[:, w % RING, 512 * r_:512 * r_ + 512], start=(g == 1 and r_ == 0), stop=False)
                    mm.then_inc(spv_pe, 1)
                    if g == 0:
                        mm = pe.matmul(out, pTn[half][:, NS * j:NS * j + NS], Vn[:, :, :].rearrange("p c n -> p (c n)"),
                                       start=False, stop=True)
                mm.then_inc(orow_pe, 1)
                pe.wait_ge(osm_done, half + 1)
                if half == 1:
                    pe.wait_ge(so_ev, 2)
                for ch in range(AC):
                    pick = ident[:, :].rearrange("p (j n) -> p j n", j=4)[:, :, 8 * ch:8 * ch + 8]
                    mm = pe.matmul(psum[:, 4, NS * ch:NS * ch + NS], osm[half][:, P * ch:P * ch + P], pick, start=True, stop=True)
                mm.then_inc(so_pe, 1)

            pe.wait_ge(yo_lo, KC)
            with pe.Fori(0, KC) as f:
                for j in range(RING):
                    pe.wait_ge(lo_done, 4 * f + (C0 + j + 1))
                    if j == 2:
                        pe.wait_ge(yo_lo, KC + 1)
                    xhi, xlo = ((ybHi, ybLo), (hHi, hLo), (oHi, oLo), (hHi, hLo))[j]
                    for t in range(2):
                        project(None, j, xhi, xlo, t, k_n=AC if j == 2 else KC, free=4 * f + (C0 + j))
            def mixed_T(f):
                pe.wait_ge(op_done, f + 1)
                if f >= 1:
                    pe.wait_ge(x2_half, f)
                    pe.wait_ge(x2_done, f)
                for a in range(TILES):
                    pe.transpose(psum[:, 2 + f % 2, P * a:P * a + P], op[:, f % 2, P * a:P * a + P], ident[:, :])
                pe.transpose(psum[0:NS, 4, 0:P], op[:, f % 2, SEQ:NT], ident[:, :]).then_inc(opT_pe, 1)

            for m in range(D0, N_P):
                pe.wait_ge(lo_done, m + 1)
                if m == D0:
                    pe.wait_ge(g_lo, 2 * KC)
                for t in range(2):
                    project(m, m % RING, mixHi, mixLo, t, free=m)
                f = m - D0
                if 1 <= f < 7:
                    pe.wait_ge(bc_done, f)
                    if f >= 2:
                        pe.wait_ge(bcT_ev, f - 1)
                    src, rows_n = (bcp, P) if f % 2 else (bcs, NS)
                    for k in range(KC):
                        mm = pe.transpose(psum[0:rows_n, 5 + k // 4, P * (k % 4):P * (k % 4) + P], src[:, k, :],
                                          ident[:, :])
                    mm.then_inc(bcT_pe, 1)
                if f >= 1:
                    mixed_T(f - 1)
            mixed_T(KC - 1)
            pe.wait_ge(x2_half, KC)
            pe.wait_ge(x2_done, KC)
            pe.wait_ge(late_in, 96)
            for tt in range(TILES + 1):
                n = P if tt < TILES else NS
                pe.wait_ge(h2_done, tt + 1)
                if tt >= 2:
                    pe.wait_ge(h2T_ev, tt - 1)
                for k in range(KC):
                    mm = pe.transpose(psum[:, 2 * (tt % 2) + k // 4, P * (k % 4):P * (k % 4) + n],
                                      h2[0:n, tt, P * k:P * k + P], ident[0:n, 0:n])
                mm.then_inc(h2T_pe, 1)
                pe.wait_ge(h2T_ev, tt + 1)
                for k in range(KC):
                    mm = pe.matmul(psum[0:n, 4, 32 * tt:32 * tt + 20], h2T[:, tt % 2, k, 0:n], wr[:, k, :],
                                   start=(k == 0), stop=(k == KC - 1))
                mm.then_inc(lg_pe, 1)
            pe.wait_ge(oh_done, 1)
            for tt in range(TILES + 1):
                n = P if tt < TILES else NS
                for s in range(tt + 1):
                    kk = P if s < TILES else NS
                    pe.matmul(psum[0:n, 5, 16 * tt:16 * tt + 16], (ones if s < tt else tri)[0:kk, 0:n],
                              onehot[0:kk, 2, s, :], start=(s == 0), stop=(s == tt))
            for s in range(TILES + 1):
                kk = P if s < TILES else NS
                mm = pe.matmul(psum[:, 6, 0:16], ones[0:kk, :], onehot[0:kk, 2, s, :],
                               start=(s == 0), stop=(s == TILES))
            mm.then_inc(pos_pe, 1)

            pe.wait_ge(tab_done, 1)
            pairs = pe.value_load(tab[0:1, TABLE:TABLE + 1], min_val=NE // 2, max_val=MAX_PAIRS)
            pe.sem_inc(ab_pe, 2)
            pe.sem_inc(ye_pe, 4)
            pe.sem_inc(xgT_pe, 1)

            def rows_T(slot):
                for k in range(KC):
                    mm = pe.transpose(psum[:, k // 4, TS * (k % 4):TS * (k % 4) + TS],
                                      xg[:, slot, P * k:P * k + P], ident[0:TS, 0:TS])
                mm.then_inc(xgT_pe, 1)

            pe.wait_ge(xg_in[0], 16)
            rows_T(0)
            with pe.Fori(0, pairs) as jp:
                for q in range(2):
                    pe.wait_ge(xgT_ev, 4 * jp + (2 * q + 2))
                    pe.wait_ge(hid_done, 2 * jp + (q + 1))
                    for w, bank, landed, done in ((e1, 2 + q, e1_in, a_pe), (e3, 4 + q, e3_in, ab_pe)):
                        pe.wait_ge(landed[q], 16 * jp + 16)
                        for fc in range(FC):
                            for k in range(KC):
                                mm = pe.matmul(psum[:, bank, TS * fc:TS * fc + TS], w[:, q, k, P * fc:P * fc + P],
                                               xgT[:, q, k, :], start=(k == 0), stop=(k == KC - 1))
                        mm.then_inc(done, 1)
                    pe.wait_ge(xg_in[1 - q], 16 * jp + 16 + 16 * q)
                    rows_T(1 - q)
                    pe.wait_ge(e2_in[q], 16 * jp + 16)
                    pe.wait_ge(hid_done, 2 * jp + (q + 3))
                    pe.wait_ge(ye_ev0, 2 * jp + (q + 1))
                    pe.wait_ge(ye_ev1, 2 * jp + (q + 1))
                    for n in range(2):
                        for fc in range(FC):
                            mm = pe.matmul(psum[0:TS, 6 + n, :], hid[:, q, fc, :], e2[:, q, fc, 512 * n:512 * n + 512],
                                           start=(fc == 0), stop=(fc == FC - 1))
                        mm.then_inc(ye_pe, 1)

        @block.scalar
        def _(act):
            act.wait_ge(cst_in, 128)
            act.activation(ctok[:, :], ctok[:, :], ACT.Silu).then_inc(silu_done, 1)
            act.wait_ge(stat_init, 1)
            act.wait_ge(x_in, 16 * (4 * TILES + 1))
            for tt in range(TILES + 1):
                n = P if tt < TILES else NS
                if tt:
                    act.wait_ge(sq_done, tt)
                act.activation(junk[0:n, :], xt[0:n, tt, :], ACT.Square,
                               accum_out=stat[0:n, tt:tt + 1]).then_inc(sq_done, 1)
            act.wait_ge(ms_done, 1)
            act.activation(rstd[:, :], stat[:, :], ACT.Sqrt).then_inc(sqrt_done, 1)
            for tt in range(TILES + 1):
                n = P if tt < TILES else NS
                act.wait_ge(hraw_done, 2 * tt + 2)
                act.activation(hHi[:, :, P * tt:P * tt + n], hraw[:, tt % 2, :, 0:n], ACT.Copy).then_inc(hhi_done, 1)

            def split_hi(m, slot, count, pe_groups):
                act.wait_ge(raw_in[slot], count)
                if pe_groups is not None:
                    act.wait_ge(grp, pe_groups)
                act.activation(whi[:, slot], wraw[:, slot], ACT.Copy).then_inc(hi_done, 1)

            def split_hi_at(m):
                split_hi(m, m % RING, 16 * (m // RING + 1), 2 * (m - RING + 1) if m >= RING else None)

            for m in range(LEAD):
                split_hi_at(m)
            for G in range(2 * C0):
                m, t = divmod(G, 2)
                if t == 0:
                    if m + LEAD < C0:
                        split_hi_at(m + LEAD)
                    if 2 <= m < B_P + 2 and kind(m - 2) == "v":
                        c, g = divmod((m - 2) // 3, GROUPS)
                        n = GROUPS * c + g
                        act.wait_ge(vt_pe, n + 1)
                        if c >= 2:
                            act.wait_ge(pvb_pe, UNITS * (c - 1))
                            act.wait_ge(v_out[c % 2], 64 * GROUPS * (c // 2))
                        act.activation(Vt[:, c % 2, :, g, :], psum[:, BANK_KV, :].rearrange("p (a n) -> p a n", n=P),
                                       ACT.Copy).then_inc(vt_ev, 1)
                    step = step_of(G)
                    u = unit_at(step - 1)
                    if u:
                        act.wait_ge(pta_pe, u[0] + 1)
                        if u[0] >= 1:
                            act.wait_ge(pva_pe, u[0])
                        act.activation(pTa[:, :], psum[:, BANK_PT, 0:3 * P], ACT.Copy).then_inc(pta_ev, 1)
                    u = unit_at(step)
                    if u:
                        s = u[0] % 2
                        act.wait_ge(s_nb, u[0] + 1)
                        act.activation(pr[:, s], pr[:, s], ACT.Exp, bias=nb[:, s:s + 1], scale=SCALE,
                                       accum_out=rs[:, s:s + 1]).then_inc(s_exp, 1)
                if kind(m) in "qkvu":
                    act.wait_ge(grp, G + 1)
                    if kind(m) in "qk":
                        R = 4 * (m // 3) + 2 * (m % 3) + t
                        if R >= 2:
                            act.wait_ge(rot_done, 2 * (R - 1))
                        dst = rb[:, t, :]
                    elif kind(m) == "v":
                        if m >= 3:
                            act.wait_ge(kn_pe, 2 * (m // 3))
                        dst = vf[:, HALF * t:HALF * t + HALF]
                    else:
                        if m == A0:
                            act.wait_ge(rope_done, 4 * GROUPS * AC)
                        act.wait_ge(bank_free[t], m)
                        dst = u_sb[:, t, :]
                    act.activation(dst, psum[:, t, 0:HALF], ACT.Copy).then_inc(bank_free[t], 1)

            act.wait_ge(lt_pe, 1)
            act.wait_ge(mask_in, 16)
            for n in range(2):
                act.activation(ltok[:, 512 * n:512 * n + 512], psum[0:18, 6 + n, :], ACT.Copy).then_inc(lt_ev, 1)
            for m in range(C0, C0 + LEAD):
                split_hi_at(m)
            act.wait_ge(bank_free[0], C0)
            act.wait_ge(bank_free[1], C0)
            for half in range(2):
                for n in range(0, 12 * AC, 2):
                    x = half * 12 * AC + n
                    g = (1, 2, 0)[n // AC % 3]
                    act.wait_ge(ktr_pe, x + 1)
                    if x >= RING:
                        act.wait_ge(ss_pe, x - RING + 1)
                    act.activation(kTs[:, x % RING, 0:P * kv_tiles(g)], psum[:, 0, 0:P * kv_tiles(g)],
                                   ACT.Copy).then_inc(ktr_act, 1)
                    if half == 0 and n % 4 == 0 and n // 4 < KC:
                        act.activation(ybHi[:, n // 4, :], yb[:, n // 4, :], ACT.Copy).then_inc(yo_hi, 1)
                act.wait_ge(ss_nb, half + 1)
                act.activation(ps_[:, half], ps_[:, half], ACT.Exp, bias=sst[:, half, 1:2], scale=SCALE,
                               accum_out=sst[:, half, 2:3]).then_inc(ss_exp, 1)

            act.wait_ge(so_ev, 4)
            act.wait_ge(vn_out, 16 * GROUPS)
            act.activation(oHi[:, :, :], oT[:, :, :], ACT.Copy).then_inc(yo_hi, 1)
            with act.Fori(0, KC) as f:
                for j in range(RING):
                    split_hi(None, (j + LEAD) % RING, 16 * f + 16 * ((C0 + j + LEAD) // RING + 1), 8 * f + 2 * (C0 + j))
                    for t in range(2):
                        act.wait_ge(grp, 8 * f + (2 * (C0 + j) + t + 1))
                        if j < 2:
                            act.wait_ge(g_m2, 2 * f + (t + 1))
                        else:
                            act.wait_ge(g_m1, 2 * f + (t + 3))
                        act.activation((gsg if j % 2 else gyc)[:, t, :], psum[:, t, 0:HALF],
                                       ACT.Sigmoid if j % 2 else ACT.Copy).then_inc(bank_free[t], 1)
            for m in range(D0 + LEAD, N_P):
                split_hi_at(m)

            for tt in range(TILES + 1):
                n = P if tt < TILES else NS
                act.wait_ge(x2_half, KC)
                act.wait_ge(x2_done, KC)
                if tt:
                    act.wait_ge(ss2_done, tt)
                act.activation(junk2[0:n, :], x2[0:n, tt, :], ACT.Square,
                               accum_out=stat[0:n, tt:tt + 1]).then_inc(ss2_done, 1)
            act.wait_ge(ms2_done, 1)
            act.activation(rstd[:, :], stat[:, :], ACT.Sqrt).then_inc(sqrt2_done, 1)
            for tt in range(TILES + 1):
                n = P if tt < TILES else NS
                act.wait_ge(h2T_pe, tt + 1)
                if tt >= 2:
                    act.wait_ge(lg_pe, tt - 1)
                src = psum[:, 2 * (tt % 2):2 * (tt % 2) + 2, :].rearrange("p b (k n) -> p (b k) n", n=P)
                act.activation(h2T[:, tt % 2, :, 0:n], src[:, :, 0:n], ACT.Copy).then_inc(h2T_ev, 1)
            act.wait_ge(rt_dve, 1)
            act.activation(rt[:, 1], rt[:, 0], ACT.Exp).then_inc(rt_act, 1)
            act.wait_ge(rt_dve, 2)
            act.activation(rs1[:, 0], rs1[:, 11], ACT.Exp).then_inc(rt_act, 1)

            act.wait_ge(tab_done, 1)
            pairs = act.value_load(tab[0:1, TABLE:TABLE + 1], min_val=NE // 2, max_val=MAX_PAIRS)
            act.sem_inc(ye_ev0, 1)
            act.sem_inc(ye_out[0], 16)
            act.sem_inc(ye_out[1], 16)
            with act.Fori(0, pairs) as jp:
                for q in range(2):
                    act.wait_ge(ab_pe, 2 * jp + (q + 3))
                    act.wait_ge(hid_done, 2 * jp + (q + 1))
                    act.activation(sil[:, q].rearrange("p f n -> p (f n)"), psum[:, 2 + q, 0:FC * TS],
                                   ACT.Silu).then_inc(sil_done, 1)
                    act.wait_ge(ye_pe, 4 * jp + (2 * q + 5))
                    act.wait_ge(ye_out[q], 16 * jp + 16)
                    act.activation(yev[:, q, 0:512], psum[0:TS, 6, :], ACT.Copy).then_inc(ye_ev0, 1)
                    act.wait_ge(ye_ev0, 2 * jp + (q + 2))
                    act.wait_ge(ye_ev1, 2 * jp + (q + 2))
                    act.dma_start(y_rows[bass.ds((2 * jp + q) * TS, TS), :], yev[:, q, :]).then_inc(ye_out[q], 16)
            for tt in range(TILES + 1):
                n = P if tt < TILES else NS
                act.wait_ge(f_mix, tt + 1)
                if tt:
                    act.wait_ge(f_sq, tt)
                act.activation(junk3[0:n, :], x2[0:n, tt, :], ACT.Square,
                               accum_out=stat[0:n, tt:tt + 1]).then_inc(f_sq, 1)
                act.wait_ge(f_ms, tt + 1)
                act.activation(rstd[0:n, tt:tt + 1], stat[0:n, tt:tt + 1], ACT.Sqrt).then_inc(f_sqrt, 1)

        @block.vector
        def _(dve):
            local = [0]

            def own(ins):
                local[0] += 1
                ins.then_inc(dve_local, 1)
                dve.wait_ge(dve_local, local[0])

            own(dve.memset(stat[:, :], 1.0))
            dve.sem_inc(stat_init, 1)
            dve.sem_inc(ada_ev, 2)
            dve.sem_inc(mrow_done, 2)
            dve.wait_ge(first_T, 1)
            dve.tensor_copy(small[:, 0:88], psum[:, 0, 0:88]).then_inc(first_ev, 1)
            dve.wait_ge(first_T, 2)
            dve.tensor_copy(cT[:, :, :], psum[:, 1, 0:128].rearrange("p (k n) -> p k n", n=16)[:, :, 0:9])\
               .then_inc(first_ev, 1)
            dve.wait_ge(first_T, 3)
            dve.tensor_copy(stT[:, :, :], psum[:, 2, 0:128].rearrange("p (k n) -> p k n", n=16)).then_inc(first_ev, 1)
            dve.wait_ge(first_ev, 3)
            dve.wait_ge(sq_done, TILES + 1)
            dve.tensor_scalar(stat[:, :], stat[:, :], 1.0 / D, EPS, ALU.mult, ALU.add).then_inc(ms_done, 1)
            dve.wait_ge(sqrt_done, 1)
            own(dve.reciprocal(rstd[:, :], rstd[:, :]))
            for tt in range(TILES + 1):
                n = P if tt < TILES else NS
                dve.tensor_scalar(xt[0:n, tt, :], xt[0:n, tt, :], rstd[0:n, tt:tt + 1], None, ALU.mult)\
                   .then_inc(xn_done, 1)
            with dve.Fori(0, ADA_FIRST // RING) as i:
                for h in range(2):
                    dve.wait_ge(ada_pe, 4 * i + (2 * h + 2))
                    dve.tensor_copy(mrow[:, h, :], psum[0:9, 3 + h, 0:2 * P]).then_inc(mrow_done, 1)
                for h in range(2):
                    dve.wait_ge(mT_pe, 2 * i + (h + 1))
                    dve.tensor_tensor(modT[:, bass.ds(4 * i + 2 * h, 2), :],
                                      psum[:, 5 + h, 0:32].rearrange("p (k n) -> p k n", n=16)[:, :, 0:9],
                                      small[:, bass.ds(4 * i + 2 * h, 2)].unsqueeze(2).to_broadcast([P, 2, 9]),
                                      ALU.add).then_inc(ada_ev, 1)
            dve.wait_ge(ada_ev, 2 + ADA_FIRST // 2)
            own(dve.tensor_scalar(A1[:, :, :], modT[:, KC:2 * KC, :], 1.0, None, ALU.add))
            own(dve.tensor_tensor(A1[:, :, :], A1[:, :, :], small[:, 48:56].unsqueeze(2).to_broadcast([P, KC, 9]),
                                  ALU.mult))
            for tt in range(TILES + 1):
                s = tt % 2
                dve.wait_ge(xT_pe, tt + 1)
                if tt < TILES:
                    for k in range(KC):
                        ins = dve.tensor_scalar(hraw[:, s, k, :], psum[:, 2 * s + k // 4, P * (k % 4):P * (k % 4) + P],
                                                A1[:, k, 0:1], modT[:, k, 0:1], ALU.mult, ALU.add)
                        if k % 4 == 3:
                            ins.then_inc(hraw_done, 1)
                    n = P
                else:
                    n = NS
                    for k in range(0, KC, 4):
                        src = psum[:, 2 * s + k // 4, :].rearrange("p (k n) -> p k n", n=P)[:, :, 0:NS]\
                            .rearrange("p k (b q) -> p k b q", q=DEC_T)
                        dst = hraw[:, s, k:k + 4, 0:NS].rearrange("p k (b q) -> p k b q", q=DEC_T)
                        shape = [P, 4, DEC_B, DEC_T]
                        own(dve.tensor_tensor(dst, src, A1[:, k:k + 4, 1:9].unsqueeze(3).to_broadcast(shape), ALU.mult))
                        dve.tensor_tensor(dst, dst, modT[:, k:k + 4, 1:9].unsqueeze(3).to_broadcast(shape),
                                          ALU.add).then_inc(hraw_done, 1)
                dve.wait_ge(hhi_done, tt + 1)
                dve.tensor_tensor(hLo[:, :, P * tt:P * tt + n], hraw[:, s, :, 0:n],
                                  hHi[:, :, P * tt:P * tt + n].bitcast(F32), ALU.subtract).then_inc(hlo_done, 1)

            def split_lo(slot, count):
                dve.wait_ge(hi_done, count)
                dve.tensor_tensor(wlo[:, slot], wraw[:, slot], whi[:, slot].bitcast(F32), ALU.subtract)\
                   .then_inc(lo_done, 1)

            for m in range(LEAD):
                split_lo(m % RING, m + 1)

            def rope_add(G):
                m, t = divmod(G, 2)
                c, j = divmod(m, 9)
                g, kv = divmod(j, 3)
                R = 4 * (m // 3) + 2 * kv + t
                dve.wait_ge(rot_done, 2 * R + 2)
                if c >= 2:
                    dve.wait_ge(s_pe, UNITS * (c - 1))
                    dve.wait_ge(kn_pe, 2 * GROUPS * (c - 1))
                    dve.wait_ge(qb_done, 3 * GROUPS * (c - 1))
                dve.tensor_tensor((kT if kv else qT)[:, c % 2, g, HALF * t:HALF * t + HALF], t1[:, t, :],
                                  shb[:, t, :], ALU.add).then_inc(rope_done, 1)

            def conv(f):
                w = [small[:, 64 + KC * j + f:65 + KC * j + f] for j in range(3)]
                own(dve.tensor_scalar(yv[:, 0:SEQ], cu[:, 0:SEQ], w[2], None, ALU.mult))

                def tap(dst, src, j):
                    own(dve.scalar_tensor_tensor(dst, src, w[j], dst, ALU.mult, ALU.add))

                tap(yv[:, P:SEQ], cu[:, 0:SEQ - P], 1)
                tap(yv[:, 32:P], cu[:, 3 * P:SEQ - 32], 1)
                tap(yv[:, 1:32], cu[:, SEQ - 32:SEQ - 1], 1)
                tap(yv[:, 2 * P:SEQ], cu[:, 0:2 * P], 0)
                y2 = yv[:, 0:2 * P].rearrange("p (a n) -> p a n", n=P)
                c2 = cu[:, 2 * P:SEQ].rearrange("p (a n) -> p a n", n=P)
                tap(y2[:, :, 32:P], c2[:, :, 0:P - 32], 0)
                tap(y2[:, :, 1:32], c2[:, :, P - 32:P - 1], 0)
                own(dve.tensor_copy(ext[:, :, 0:2], stT[:, f, :].rearrange("p (b r) -> p b r", r=2)))
                own(dve.tensor_copy(ext[:, :, 2:6], cu[:, SEQ:NT].rearrange("p (b q) -> p b q", q=DEC_T)))
                ysv = yv[:, SEQ:NT].rearrange("p (b q) -> p b q", q=DEC_T)
                own(dve.tensor_scalar(ysv, ext[:, :, 2:6], w[2], None, ALU.mult))
                tap(ysv, ext[:, :, 1:5], 1)
                tap(ysv, ext[:, :, 0:4], 0)
                dve.tensor_copy(last2[:, f, 0:2], cu[:, 383:512:128]).then_inc(cu_done, 1)
                dve.tensor_copy(last2[:, f, 2:18].rearrange("p (b r) -> p b r", r=2), ext[:, :, 4:6])\
                   .then_inc(cu_done, 1)

            SWAP = [i + 8 if i < 8 else i - 8 if i < 16 else i for i in range(32)]
            for G in range(2 * C0):
                m, t = divmod(G, 2)
                step = step_of(G)
                if t == 0 and m + LEAD < C0:
                    split_lo((m + LEAD) % RING, m + LEAD + 1)
                if misc_use(G, 0):
                    c, j = divmod(m - 2, 9)
                    g = j // 3
                    n = GROUPS * c + g
                    if kind(m - 2) == "k":
                        dve.wait_ge(kt_pe, n + 1)
                        if n >= 2:
                            dve.wait_ge(k_out[n % 2], 64 * (n // 2))
                        dve.tensor_copy(Kst[:, n % 2].rearrange("p a n -> p (a n)"), psum[:, BANK_KV, :])\
                           .then_inc(kt_ev, 1)
                        dve.wait_ge(kn_pe, 2 * n + 1)
                        if n >= 1:
                            dve.wait_ge(kn_out, 16 * n)
                        dve.tensor_copy(Kns[:, n % 2], psum[0:NS, BANK_MISC, 0:P]).then_inc(misc_ev, 1)
                    else:
                        dve.wait_ge(kn_pe, 2 * n + 2)
                        dve.tensor_copy(Vn[NS * g:NS * g + NS, c, :], psum[NS * g:NS * g + NS, BANK_MISC, 0:P])\
                           .then_inc(misc_ev, 1)
                if t == 0:
                    u = unit_at(step - 2)
                    if u:
                        n, c, a, h = u
                        dve.wait_ge(s_exp, n + 1)
                        own(dve.reciprocal(ri[:, n % 2:n % 2 + 1], rs[:, n % 2:n % 2 + 1]))
                        dve.wait_ge(pvb_pe, n + 1)
                        if h == 0 and n >= 2:
                            dve.wait_ge(otr_pe, n // 2)
                        dve.tensor_scalar(otok[:, HD * h:HD * h + HD], psum[:, BANK_O, 0:HD],
                                          ri[:, n % 2:n % 2 + 1], None, ALU.mult).then_inc(o_ev, 1)
                    u = unit_at(step)
                    if u:
                        n, c, a, h = u
                        s = n % 2
                        if n == 0:
                            dve.wait_ge(rope_in, 48)
                        dve.wait_ge(s_pe, n + 1)
                        if n >= 2:
                            dve.wait_ge(ptb_pe, n - 1)
                            dve.wait_ge(s_exp, n - 1)
                        dve.tensor_tensor_reduce(out=pr[:, s], in0=score[:, 0:KEYS_P], in1=maskp[:, a].bitcast(BF16),
                                                 scale=1.0, scalar=NEG, op0=ALU.add, op1=ALU.max,
                                                 accum_out=nmx[:, s:s + 1]).then_inc(s_mx, 1)
                        dve.wait_ge(s_mx, n + 1)
                        dve.tensor_scalar(nb[:, s:s + 1], nmx[:, s:s + 1], -SCALE, None, ALU.mult).then_inc(s_nb, 1)
                else:
                    u = unit_at(step - 1)
                    if u:
                        dve.wait_ge(ptb_pe, u[0] + 1)
                        if u[0] >= 1:
                            dve.wait_ge(pvb_pe, u[0])
                        dve.tensor_copy(pTb[:, :], psum[:, BANK_PT, 0:3 * P]).then_inc(ptb_ev, 1)
                    if misc_use(G, 1):
                        n, c, a, h = unit_at(step - 2)
                        dve.wait_ge(otr_pe, n // 2 + 1)
                        dve.tensor_copy(oT[:, c, P * a:P * a + P], psum[:, BANK_MISC, 0:P]).then_inc(misc_ev, 1)
                    if misc_use(G, 2):
                        n = ADA_FIRST + m
                        dve.wait_ge(ada_pe, n + 1)
                        if m >= 2:
                            dve.wait_ge(mT_pe, ADA_FIRST // 2 + m - 1)
                        dve.tensor_copy(mrow[:, (m + 1) % 2, 0:P], psum[0:9, BANK_MISC, 0:P]).then_inc(misc_ev, 1)
                if misc_use(G, 3):
                    n = ADA_FIRST + m - 1
                    dve.wait_ge(mT_pe, ADA_FIRST // 2 + m)
                    dve.tensor_scalar(modT[:, n, :], psum[:, BANK_MISC, 0:9], small[:, n:n + 1], None,
                                      ALU.add).then_inc(misc_ev, 1)
                if G >= 1 and kind((G - 1) // 2) in "qk":
                    rope_add(G - 1)
                if kind(m) in "qk":
                    R = 4 * (m // 3) + 2 * (m % 3) + t
                    dve.wait_ge(bank_free[t], m + 1)
                    dve.stream_shuffle(shb[:, t, :], rb[:, t, :], SWAP).then_inc(shuf_done, 1)
                elif kind(m) == "c":
                    f = (m - A0) // 3
                    cols = slice(HALF * t, HALF * t + HALF)
                    dve.wait_ge(grp, G + 1)
                    if f >= 1:
                        dve.wait_ge(cu_done, 2 * f)
                    dve.tensor_tensor(cu[:, cols], psum[:, t, 0:HALF], u_sb[:, t, :], ALU.mult)\
                       .then_inc(bank_free[t], 1)
                    if t == 1:
                        dve.wait_ge(bank_free[0], m + 1)
                        dve.wait_ge(bank_free[1], m + 1)
                        conv(f)
                elif kind(m) == "b":
                    f = (m - A0) // 3
                    cols = slice(HALF * t, HALF * t + HALF)
                    dve.wait_ge(grp, G + 1)
                    dve.tensor_tensor(yb[:, f, cols], psum[:, t, 0:HALF], yv[:, cols], ALU.mult)\
                       .then_inc(bank_free[t], 1)

            for m in range(C0, C0 + LEAD):
                split_lo(m % RING, m + 1)

            def normalise(half):
                dve.wait_ge(ss_exp, half + 1)
                own(dve.reciprocal(sst[:, half, 3:4], sst[:, half, 2:3]))
                dve.tensor_scalar(ps_[:, half], ps_[:, half], sst[:, half, 3:4], None, ALU.mult).then_inc(ss_p, 1)

            for half in range(2):
                for n in range(1, 12 * AC, 2):
                    x = half * 12 * AC + n
                    g = (1, 2, 0)[n // AC % 3]
                    dve.wait_ge(ktr_pe, x + 1)
                    if x >= RING:
                        dve.wait_ge(ss_pe, x - RING + 1)
                    dve.tensor_copy(kTs[:, x % RING, 0:P * kv_tiles(g)], psum[:, 1, 0:P * kv_tiles(g)])\
                       .then_inc(ktr_dve, 1)
                    if half == 0 and n % 4 == 3 and n // 4 < KC:
                        dve.wait_ge(yo_hi, n // 4 + 1)
                        dve.tensor_tensor(ybLo[:, n // 4, :], yb[:, n // 4, :], ybHi[:, n // 4, :].bitcast(F32),
                                          ALU.subtract).then_inc(yo_lo, 1)
                    if half == 1 and n == 9:
                        normalise(0)
                dve.wait_ge(mask_in, 16)
                dve.wait_ge(ssn_pe, half + 1)
                dve.tensor_tensor_reduce(out=ps_[:, half], in0=score_s[half][:, 0:KEYS_S],
                                         in1=masks[:, half].bitcast(BF16), scale=1.0, scalar=NEG, op0=ALU.add,
                                         op1=ALU.max, accum_out=sst[:, half, 0:1]).then_inc(ss_mx, 1)
                dve.wait_ge(ss_mx, half + 1)
                dve.tensor_scalar(sst[:, half, 1:2], sst[:, half, 0:1], -SCALE, None, ALU.mult).then_inc(ss_nb, 1)
            dve.wait_ge(conv_out, 32)
            for half in range(2):
                for part in range(3 * half, 3 * half + 3):
                    dve.wait_ge(spt_pe, part + 1)
                    if part % 3 < 2:
                        n = 4 * (part % 3)
                        dve.tensor_copy(pTs[half][:, n:n + 4, :].rearrange("p t n -> p (t n)"),
                                        psum[:, part % 2, :]).then_inc(spt_ev, 1)
                    else:
                        dve.tensor_copy(pTs[half][:, 8, :], psum[:, part % 2, 0:P])
                        dve.tensor_copy(pTn[half][:, :], psum[0:GROUPS * NS, part % 2, P:2 * P]).then_inc(spt_ev, 1)
                if half == 0:
                    normalise(1)
                dve.wait_ge(orow_pe, half + 1)
                dve.tensor_copy(osm[half], psum[:, 2 + half, :]).then_inc(osm_done, 1)
                dve.wait_ge(so_pe, half + 1)
                for hh in range(2):
                    part = slice(HD * hh, HD * hh + HD)
                    src = psum[part, 4, 0:P].rearrange("p (k j n) -> p k j n", k=AC, j=4)[:, :, :, 4 * hh:4 * hh + 4]
                    dst = oT[part, :, SEQ + 16 * half:SEQ + 16 * half + 16].rearrange("p k (j q) -> p k j q", q=DEC_T)
                    dve.tensor_copy(dst, src).then_inc(so_ev, 1)

            dve.wait_ge(yo_hi, KC + 1)
            dve.tensor_tensor(oLo[:, :, :], oT[:, :, :], oHi[:, :, :].bitcast(F32), ALU.subtract).then_inc(yo_lo, 1)
            dve.sem_inc(g_m1, 2)
            dve.sem_inc(g_m2, 2)
            with dve.Fori(0, KC) as f:
                for j in range(RING):
                    split_lo((j + LEAD) % RING, 4 * f + (C0 + j + LEAD + 1))
                    for t in range(2):
                        if j == 1:
                            dve.wait_ge(bank_free[t], 4 * f + (C0 + 2))
                            dve.tensor_tensor(gm1[:, t, :], gsg[:, t, :], gyc[:, t, :], ALU.mult).then_inc(g_m1, 1)
                        if j == 3:
                            cols = slice(HALF * t, HALF * t + HALF)
                            dve.wait_ge(bank_free[t], 4 * f + (C0 + 4))
                            dve.tensor_tensor(gmx[:, t, :], gsg[:, t, :], gyc[:, t, :], ALU.mult).then_inc(g_m2, 1)
                            dve.wait_ge(g_m2, 2 * f + (t + 3))
                            dve.tensor_tensor(gmx[:, t, :], gmx[:, t, :], gm1[:, t, :], ALU.add).then_inc(g_mx, 1)
                            dve.wait_ge(g_mx, 2 * f + (t + 1))
                            hi = mixHi[:, bass.ds(f, 1), cols].rearrange("p k n -> p (k n)")
                            dve.tensor_scalar(hi, gmx[:, t, :], 1.0, None, ALU.mult).then_inc(g_hi, 1)
                            dve.wait_ge(g_hi, 2 * f + (t + 1))
                            dve.tensor_tensor(mixLo[:, bass.ds(f, 1), cols].rearrange("p k n -> p (k n)"),
                                              gmx[:, t, :], hi.bitcast(F32), ALU.subtract).then_inc(g_lo, 1)
            own(dve.tensor_scalar(A2[:, :, :], modT[:, 4 * KC:5 * KC, :], 1.0, None, ALU.add))
            own(dve.tensor_tensor(A2[:, :, :], A2[:, :, :], small[:, 56:64].unsqueeze(2).to_broadcast([P, KC, 9]),
                                  ALU.mult))
            def residual(f):
                if f == 0:
                    dve.wait_ge(xr_in, 16 * (4 * TILES + 1))
                dve.wait_ge(opT_pe, f + 1)
                cols = slice(P * f, P * f + P)
                dve.tensor_tensor(x2[:, 0:TILES, cols], psum[:, 2 + f % 2, :].rearrange("p (a n) -> p a n", n=P),
                                  x2[:, 0:TILES, cols], ALU.add).then_inc(x2_half, 1)
                dve.tensor_tensor(x2[0:NS, TILES, cols], psum[0:NS, 4, 0:P], x2[0:NS, TILES, cols], ALU.add)\
                   .then_inc(x2_done, 1)

            for m in range(D0, N_P):
                if m + LEAD < N_P:
                    split_lo((m + LEAD) % RING, m + LEAD + 1)
                f = m - D0
                gate = modT[:, 2 * KC + f, :]
                if f >= 2:
                    dve.wait_ge(opT_pe, f - 1)
                for t in range(2):
                    dve.wait_ge(grp, 2 * m + t + 1)
                    n = HALF if t == 0 else SEQ - HALF
                    ins = dve.tensor_scalar(op[:, f % 2, HALF * t:HALF * t + n], psum[:, t, 0:n], gate[:, 0:1], None,
                                            ALU.mult)
                    if t == 1:
                        ins.then_inc(op_half, 1)
                        ins = dve.tensor_tensor(op[:, f % 2, SEQ:NT].rearrange("p (b q) -> p b q", q=DEC_T),
                                                psum[:, t, n:HALF].rearrange("p (b q) -> p b q", q=DEC_T),
                                                gate[:, 1:9].unsqueeze(2).to_broadcast([P, DEC_B, DEC_T]), ALU.mult)
                    ins.then_inc(bank_free[t], 1)
                dve.wait_ge(bank_free[0], m + 1)
                dve.wait_ge(bank_free[1], m + 1)
                dve.wait_ge(op_half, f + 1)
                dve.sem_inc(op_done, 1)
                if f < 6:
                    prm = (A2[:, :, :], modT[:, 3 * KC:4 * KC, :], modT[:, 5 * KC:6 * KC, :])[f // 2]
                    if f >= 2:
                        dve.wait_ge(bcT_pe, f - 1)
                    if f % 2 == 0:
                        dve.tensor_copy(bcp[:, :, :], prm[:, :, 0:1].to_broadcast([P, KC, P])).then_inc(bc_done, 1)
                    else:
                        dve.tensor_copy(bcs[:, :, :].rearrange("p k (b q) -> p k b q", q=DEC_T),
                                        prm[:, :, 1:9].unsqueeze(3).to_broadcast([P, KC, DEC_B, DEC_T]))\
                           .then_inc(bc_done, 1)
                if 1 <= f < 7:
                    dve.wait_ge(bcT_pe, f)
                    rows_n = P if f % 2 else NS
                    dve.tensor_copy((tokt if f % 2 else toks)[:, (f - 1) // 2, :],
                                    psum[0:rows_n, 5:7, :].rearrange("p b n -> p (b n)")).then_inc(bcT_ev, 1)
                if f >= 1:
                    residual(f - 1)
            residual(KC - 1)
            dve.memset(ones[:, :], 1.0)
            own(dve.memset(lg[:, :, :], 0.0))
            dve.wait_ge(ss2_done, TILES + 1)
            dve.tensor_scalar(stat[:, :], stat[:, :], 1.0 / D, EPS, ALU.mult, ALU.add).then_inc(ms2_done, 1)
            dve.wait_ge(sqrt2_done, 1)
            own(dve.reciprocal(rstd[:, :], rstd[:, :]))
            for tt in range(TILES + 1):
                n = P if tt < TILES else NS
                tab_ = tokt if tt < TILES else toks
                own(dve.scalar_tensor_tensor(h2[0:n, tt, :], x2[0:n, tt, :], rstd[0:n, tt:tt + 1], tab_[0:n, 0, :],
                                             ALU.mult, ALU.mult))
                dve.tensor_tensor(h2[0:n, tt, :], h2[0:n, tt, :], tab_[0:n, 1, :], ALU.add).then_inc(h2_done, 1)

            dve.wait_ge(late_in, 96)
            dve.wait_ge(lg_pe, TILES + 1)
            own(dve.tensor_tensor(lg[:, 0:TILES, :],
                                  psum[:, 4, 0:32 * TILES].rearrange("p (t n) -> p t n", n=32)[:, :, 0:20],
                                  br[:, :].unsqueeze(1).to_broadcast([P, TILES, 20]), ALU.add))
            own(dve.tensor_tensor(lg[0:NS, TILES, :], psum[0:NS, 4, 32 * TILES:32 * TILES + 20], br[0:NS, :], ALU.add))
            tok4 = [P, 5, 4]
            rev = cst[:, 0:4].unsqueeze(1).to_broadcast(tok4)

            def first_best(values, diff, best, mark, pick, key):
                own(dve.tensor_reduce(rs1[:, best], values, AX.X, ALU.max))
                own(dve.tensor_tensor(rt[:, diff], values, rs1[:, best].unsqueeze(2).to_broadcast(tok4), ALU.subtract))
                own(dve.tensor_scalar(rt[:, mark], rt[:, diff], 0.0, None, ALU.is_equal))
                own(dve.tensor_tensor(rt[:, mark], rt[:, mark], rev, ALU.mult))
                own(dve.tensor_reduce(rs1[:, key], rt[:, mark], AX.X, ALU.max))
                own(dve.tensor_tensor(rt[:, pick], rt[:, mark], rs1[:, key].unsqueeze(2).to_broadcast(tok4),
                                      ALU.is_equal))

            first_best(lg[:, :, 0:4], 0, 3, 2, 3, 4)
            dve.sem_inc(rt_dve, 1)
            prod = onehot[:, 3].rearrange("p t (g e) -> p t g e", g=4)
            tok16 = [P, 5, 4, 4]
            own(dve.tensor_tensor(prod, lg[:, :, 4:20].rearrange("p t (g e) -> p t g e", g=4),
                                  rt[:, 3].unsqueeze(3).to_broadcast(tok16), ALU.mult))
            own(dve.tensor_reduce(rt[:, 4], prod.rearrange("p t g e -> p t e g"), AX.X, ALU.add))
            first_best(rt[:, 4], 5, 7, 7, 8, 8)
            own(dve.scalar_tensor_tensor(rt[:, 9], rt[:, 8], -1.0e30, rt[:, 4], ALU.mult, ALU.add))
            first_best(rt[:, 9], 10, 9, 12, 13, 10)
            own(dve.tensor_tensor(rs1[:, 11], rs1[:, 9], rs1[:, 7], ALU.subtract))
            dve.sem_inc(rt_dve, 1)
            for r_ in range(2):
                own(dve.tensor_tensor(onehot[:, r_].rearrange("p t (g e) -> p t g e", g=4),
                                      rt[:, 3].unsqueeze(3).to_broadcast(tok16),
                                      rt[:, 8 if r_ == 0 else 13].unsqueeze(2).to_broadcast(tok16), ALU.mult))
            dve.tensor_tensor(onehot[:, 2], onehot[:, 0], onehot[:, 1], ALU.add).then_inc(oh_done, 1)
            dve.wait_ge(rt_act, 1)
            own(dve.tensor_reduce(rs1[:, 5], rt[:, 1], AX.X, ALU.add))
            own(dve.reciprocal(rs1[:, 6], rs1[:, 5]))
            dve.wait_ge(rt_act, 2)
            own(dve.tensor_scalar(rs1[:, 1], rs1[:, 0], 1.0, None, ALU.add))
            own(dve.reciprocal(rs1[:, 2], rs1[:, 1]))
            own(dve.tensor_tensor(cw[:, 0], rs1[:, 6], rs1[:, 2], ALU.mult))
            own(dve.tensor_tensor(cw[:, 1], cw[:, 0], rs1[:, 0], ALU.mult))
            dve.wait_ge(pos_pe, 1)
            own(dve.tensor_tensor(cmp6[:, :, :], psum[:, 6, 0:16].unsqueeze(2).to_broadcast([P, NE, COUNT_STEPS]),
                                  cst[:, 8:8 + COUNT_STEPS].unsqueeze(1).to_broadcast([P, NE, COUNT_STEPS]), ALU.is_gt))
            own(dve.tensor_reduce(ends[:, 0], cmp6[:, :, :], AX.X, ALU.add))
            for n, sh in enumerate((1, 2, 4, 8)):
                own(dve.tensor_copy(ends[:, n + 1, 0:sh], ends[:, n, 0:sh]))
                own(dve.tensor_tensor(ends[:, n + 1, sh:NE], ends[:, n, sh:NE], ends[:, n, 0:NE - sh], ALU.add))
            own(dve.tensor_tensor(ends[:, 5], ends[:, 4], ends[:, 0], ALU.subtract))
            own(dve.tensor_tensor(ends[:, 5], ends[:, 5], cst[:, 64:64 + NE], ALU.add))
            before = psum[:, 5, 0:80].rearrange("p (t n) -> p t n", n=16)
            own(dve.scalar_tensor_tensor(onehot[:, 3], before, float(TS), ends[:, 5].unsqueeze(1).to_broadcast([P, 5, NE]),
                                         ALU.is_ge, ALU.mult))
            own(dve.tensor_tensor(onehot[:, 3], onehot[:, 3], cst[:, 80:80 + NE].unsqueeze(1).to_broadcast([P, 5, NE]),
                                  ALU.add))
            own(dve.scalar_tensor_tensor(onehot[:, 3], onehot[:, 3], float(TS), before, ALU.mult, ALU.add))
            for r_ in range(2):
                own(dve.tensor_tensor(onehot[:, 2], onehot[:, r_], onehot[:, 3], ALU.mult))
                own(dve.tensor_reduce(slotf[:, r_], onehot[:, 2], AX.X, ALU.add))
                own(dve.tensor_copy(sloti[:, r_], slotf[:, r_]))
            dve.sem_inc(slot_done, 1)
            shape = [1, TABLE, NE]
            own(dve.tensor_tensor(cmpt[:, :, :], ends[0:1, 4].unsqueeze(1).to_broadcast(shape),
                                  cst[0:1, 32:32 + TABLE].unsqueeze(2).to_broadcast(shape), ALU.is_le))
            own(dve.tensor_reduce(eidf[:, 0:TABLE], cmpt[:, :, :], AX.X, ALU.add))
            own(dve.tensor_scalar(eidf[:, 0:TABLE], eidf[:, 0:TABLE], float(NE - 1), None, ALU.min))
            own(dve.tensor_tensor(eidf[:, 0:NE], eidf[:, 0:NE], cst[0:1, 80:80 + NE], ALU.add))
            own(dve.tensor_copy(tab[:, 0:TABLE], eidf[:, 0:TABLE]))
            more = MAX_PAIRS - NE // 2
            own(dve.tensor_tensor(eidf[:, 32:32 + more], ends[0:1, 4, NE - 1:NE].to_broadcast([1, more]),
                                  cst[0:1, 16:16 + more], ALU.is_gt))
            own(dve.tensor_reduce(eidf[:, 47:48], eidf[:, 32:32 + more], AX.X, ALU.add))
            own(dve.tensor_scalar(eidf[:, 47:48], eidf[:, 47:48], float(NE // 2), None, ALU.add))
            own(dve.tensor_copy(tab[:, TABLE:TABLE + 1], eidf[:, 47:48]))
            dve.sem_inc(tab_done, 1)

            pairs = dve.value_load(tab[0:1, TABLE:TABLE + 1], min_val=NE // 2, max_val=MAX_PAIRS)
            dve.sem_inc(hid_done, 2)
            dve.sem_inc(ye_ev1, 1)

            def rows_T_copy(slot):
                dve.tensor_copy(xgT[:, slot, 0:4, :].rearrange("p k n -> p (k n)"), psum[:, 0, 0:4 * TS])\
                   .then_inc(xgT_ev, 1)
                dve.tensor_copy(xgT[:, slot, 4:8, :].rearrange("p k n -> p (k n)"), psum[:, 1, 0:4 * TS])\
                   .then_inc(xgT_ev, 1)

            dve.wait_ge(xgT_pe, 2)
            rows_T_copy(0)
            with dve.Fori(0, pairs) as jp:
                for q in range(2):
                    dve.wait_ge(sil_done, 2 * jp + (q + 1))
                    dve.wait_ge(ye_pe, 4 * jp + (2 * q + 2))
                    dve.tensor_tensor(hid[:, q].rearrange("p f n -> p (f n)"), sil[:, q].rearrange("p f n -> p (f n)"),
                                      psum[:, 4 + q, 0:FC * TS], ALU.mult).then_inc(hid_done, 1)
                    dve.wait_ge(xgT_pe, 2 * jp + (q + 3))
                    rows_T_copy(1 - q)
                    dve.wait_ge(ye_pe, 4 * jp + (2 * q + 6))
                    dve.wait_ge(ye_out[q], 16 * jp + 16)
                    dve.tensor_copy(yev[:, q, 512:1024], psum[0:TS, 7, :]).then_inc(ye_ev1, 1)

            dve.wait_ge(nf_in, 16)
            for tt in range(TILES + 1):
                n = P if tt < TILES else NS
                s = tt % 2
                tab_ = tokt if tt < TILES else toks
                dve.wait_ge(yg_in[s], 32 * (tt // 2 + 1))
                own(dve.tensor_scalar(ya[0:n, s], ya[0:n, s], cw[0:n, 0, tt:tt + 1], None, ALU.mult))
                own(dve.scalar_tensor_tensor(ya[0:n, s], yb2[0:n, s], cw[0:n, 1, tt:tt + 1], ya[0:n, s],
                                             ALU.mult, ALU.add))
                own(dve.tensor_tensor(ya[0:n, s], ya[0:n, s], tab_[0:n, 2, :], ALU.mult))
                dve.tensor_tensor(x2[0:n, tt, :], x2[0:n, tt, :], ya[0:n, s], ALU.add).then_inc(f_mix, 1)
                dve.wait_ge(f_sq, tt + 1)
                dve.tensor_scalar(stat[0:n, tt:tt + 1], stat[0:n, tt:tt + 1], 1.0 / D, EPS, ALU.mult, ALU.add)\
                   .then_inc(f_ms, 1)
                dve.wait_ge(f_sqrt, tt + 1)
                own(dve.reciprocal(rstd[0:n, tt:tt + 1], rstd[0:n, tt:tt + 1]))
                dve.scalar_tensor_tensor(x2[0:n, tt, :], x2[0:n, tt, :], rstd[0:n, tt:tt + 1], tokt[0:n, 0, :],
                                         ALU.mult, ALU.mult).then_inc(f_y, 1)

        @block.gpsimd
        def _(pool):
            pool.memset(zrow[:, :], 0.0).then_inc(zrow_done, 1)
            pool.memset(QB[:, :, :, :, :], 0.0).then_inc(qb_zero, 1)
            pool.wait_ge(qb_zero, 1)
            prompt_v = [[prompt_kv[g][kv][0, 0].rearrange("(n b a) h d -> b n a (h d)", b=4, a=TILES)
                         for kv in range(2)] for g in range(GROUPS)]

            def store(g, kv, c, src, done):
                lo = 24 if g == 0 else 0
                for b in range(4):
                    pool.dma_start(prompt_v[g][kv][b][:, :, P * c:P * c + P], src[32 * b + lo:32 * b + 32])\
                        .then_inc(done, 16)

            rotated = 0
            for G in range(2 * B_P + 8):
                m, t = divmod(G, 2)
                if m < B_P and kind(m) in "qk":
                    R = 4 * (m // 3) + 2 * (m % 3) + t
                    cols = slice(HALF * t, HALF * t + HALF)
                    if R == 0:
                        pool.wait_ge(rope_in, 48)
                    pool.wait_ge(bank_free[t], m + 1)
                    if R >= 2:
                        pool.wait_ge(rope_done, R - 1)
                    pool.tensor_tensor(t1[:, t, :], rb[:, t, :], ropec[:, cols], ALU.mult).then_inc(rot_done, 1)
                    pool.wait_ge(shuf_done, R + 1)
                    pool.tensor_tensor(shb[:, t, :], shb[:, t, :], ropes[:, cols], ALU.mult)\
                        .then_inc(rot_done, 1)
                    rotated += 2
                if t == 0 and 1 <= m and m - 1 < B_P and kind(m - 1) in "qk":
                    c, j = divmod(m - 1, 9)
                    g, kv = divmod(j, 3)
                    pool.wait_ge(rope_done, 4 * ((m - 1) // 3) + 2 * kv + 2)
                    if kv == 0:
                        pool.wait_ge(rot_done, rotated)
                        for h in range(2):
                            part = slice(HD * h, HD * h + HD)
                            pool.tensor_copy(QB[part, g, c, :, 8 * c + 4 * h:8 * c + 4 * h + 4],
                                             qT[part, c % 2, g, SEQ:NT].rearrange("p (b q) -> p b q", q=DEC_T))\
                                .then_inc(qb_done, 1)
                            pool.wait_ge(qb_done, 3 * ((m - 1) // 3) + h + 1)
                    else:
                        pool.tensor_copy(kTn[:, g, c, :], kT[:, c % 2, g, SEQ:NT]).then_inc(qb_done, 1)
                if t == 1 and 2 <= m < B_P + 2 and kind(m - 2) in "kv":
                    c, j = divmod(m - 2, 9)
                    g = j // 3
                    n = GROUPS * c + g
                    if kind(m - 2) == "k":
                        pool.wait_ge(kt_ev, n + 1)
                        store(g, 0, c, Kst[:, n % 2], k_out[n % 2])
                        pool.wait_ge(misc_ev, MISC[G - 1, 0] + 1)
                        pool.dma_start(kn_rows[g, :, P * c:P * c + P], Kns[:, n % 2]).then_inc(kn_out, 16)
                    else:
                        pool.wait_ge(vt_ev, n + 1)
                        store(g, 1, c, Vt[:, c % 2, :, g, :], v_out[c % 2])
            pool.wait_ge(misc_ev, MISC_ALL)
            for g in range(GROUPS):
                pool.dma_start(vn_rows[g], Vn[NS * g:NS * g + NS].rearrange("p c n -> p (c n)")).then_inc(vn_out, 16)
            pool.wait_ge(vn_out, 16 * GROUPS)
            pool.wait_ge(kn_out, 16 * GROUPS * AC)
            for g in range(GROUPS):
                for kv, src in enumerate((kn_rows, vn_rows)):
                    dst = sample_kv[g][kv][0, :, WINDOWS[g] - DEC_T:].rearrange("b q h d -> b (q h d)")
                    pool.dma_start(dst, src[g].rearrange("(b q) n -> b (q n)", q=DEC_T)).then_inc(tail_out, 16)
            pool.wait_ge(lt_ev, 2)
            pool.dma_start(conv_p[0, 0], ltok[0:2, :]).then_inc(conv_out, 16)
            pool.dma_start(conv_s[0].rearrange("b r c -> (b r) c"), ltok[2:18, :]).then_inc(conv_out, 16)
            pool.wait_ge(conv_out, 32)
            pool.wait_ge(xz_out, 16 * (C0 - SHIFTS_AB))
            pool.wait_ge(slot_done, 1)
            pool.wait_ge(h2_done, TILES + 1)
            for r_ in range(2):
                for tt in range(TILES + 1):
                    n = P if tt < TILES else NS
                    pool.indirect_dma_start(x_rows, bass.IndirectOffsetOnAxis(sloti[0:n, r_, tt:tt + 1], 0),
                                            h2[0:n, tt, :], None).then_inc(disp_out, 16)
            pool.wait_ge(tab_done, 1)
            pairs = pool.value_load(tab[0:1, TABLE:TABLE + 1], min_val=NE // 2, max_val=MAX_PAIRS)
            for k in range(2):
                pool.wait_ge(ye_out[k], 16 * pairs + 16)
                pool.sem_inc(all_stored, 1)
            for tt in range(TILES + 1):
                n = P if tt < TILES else NS
                if tt >= 2:
                    pool.wait_ge(f_mix, tt - 1)
                for r_, dst in enumerate((ya, yb2)):
                    pool.indirect_dma_start(dst[0:n, tt % 2], None, y_rows,
                                            bass.IndirectOffsetOnAxis(sloti[0:n, r_, tt:tt + 1], 0))\
                        .then_inc(yg_in[tt % 2], 16)


_INS = ['x_prompt', 'x_sample', 'cache_k1', 'cache_v1', 'cache_k2', 'cache_v2', 'cache_k3', 'cache_v3', 'state_conv',
        'c_prompt', 'c_sample', 'norm1_g', 'norm2_g', 'normf_g', 'w_ada', 'b_ada', 'w_in', 'conv_w', 'w_conv_out',
        'w_attn_out', 'w_o', 'w_rg', 'b_rg', 'w_re', 'b_re', 'w1', 'w3', 'w2']


def _kv(b, rows):
    return (1, b, rows, HEADS, HD)


_OUTS = [(1, SEQ, D), (DEC_B, DEC_T, D)] \
    + [_kv(1, min(w, SEQ)) for w in WINDOWS for _ in range(2)] + [(1, 1, 2, D)] \
    + [_kv(DEC_B, w) for w in WINDOWS for _ in range(2)] + [(1, DEC_B, 2, D)]


def _constants():
    import numpy as np

    col = np.arange(SEQ)
    time = 16 * (col % 32) + 4 * (col // 32 % 4) + col // P
    pos = np.concatenate([time, 2048 + np.arange(NS) % DEC_T]).astype(np.float32)
    freq = np.power(np.float32(500000.0), -np.arange(ROT, dtype=np.float32) / np.float32(ROT)).astype(np.float32)
    ang = (pos[:, None] * freq[None, :]).astype(np.float32).astype(np.float64)
    ropec = np.ones((P, NT), np.float32)
    ropes = np.zeros((P, NT), np.float32)
    for h in range(2):
        for i in range(ROT):
            for s, sign in ((0, -1.0), (ROT, 1.0)):
                ropec[HD * h + s + i] = np.cos(ang[:, i])
                ropes[HD * h + s + i] = sign * np.sin(ang[:, i])
    off = np.float32(-1.0e30)
    maskp = np.full((P, TILES, KEYS_P), off, np.float32)
    for a in range(TILES):
        tq = time[P * a:P * a + P][:, None]
        back = tq - time[None, :]
        maskp[:, a, 0:SEQ][(back >= 0) & (back <= WINDOWS[0])] = 0
        back = tq - time[P * a:P * a + P][None, :]
        for g, dil in ((1, 4), (2, 16)):
            view = maskp[:, a, SEQ + P * (g - 1):SEQ + P * g]
            view[(back >= 0) & (back % dil == 0) & (back <= WINDOWS[g])] = 0
    masks = np.full((P, 2, KEYS_S), off, np.float32)
    part = np.arange(P)
    j, q = part // NS, part % DEC_T
    row = np.arange(P)
    for half in range(2):
        m = masks[:, half]
        for r in range(DEC_T):
            m[q == r, P * r:P * r + P] = 0
            m[q == r, 4 * P + P * r:4 * P + P * r + P] = 0
        m[:, 8 * P:9 * P][row[None, :] >= q[:, None]] = 0
        new = np.arange(NS)
        own = (new // DEC_T)[None, :] == 4 * half + j[:, None]
        for g in range(GROUPS):
            ok = own & ((new % DEC_T)[None, :] <= q[:, None] if g == 0 else (new % DEC_T)[None, :] == q[:, None])
            m[:, 9 * P + NS * g:9 * P + NS * g + NS][ok] = 0
    small = np.zeros((P, 96), np.float32)
    small[:, 0:4] = [4, 3, 2, 1]
    small[:, 8:8 + COUNT_STEPS] = TS * np.arange(1, COUNT_STEPS + 1)
    small[:, 16:32] = 2 * np.arange(16)
    small[:, 32:32 + TABLE] = np.arange(TABLE) - NE
    small[:, 64:64 + NE] = NE - 1 - np.arange(NE)
    small[:, 80:80 + NE] = np.arange(NE)
    bf = lambda a: (np.ascontiguousarray(a).view(np.uint32) >> 16).astype(np.uint16)
    return {
        "k_ident": np.eye(P, dtype=np.float32), "k_tri": np.triu(np.ones((P, P), np.float32), 1),
        "k_small": small, "k_ropec": ropec, "k_ropes": ropes, "k_maskp": bf(maskp), "k_masks": bf(masks),
    }


def kernel(**inputs):
    import numpy as _np
    import concourse.bacc as _bacc
    from concourse import mybir as _mybir
    from concourse.bass_utils import run_bass_kernel_spmd as _run

    nc = _bacc.Bacc("TRN2", target_bir_lowering=False, num_devices=1)
    arrays, args = {}, []
    given = {name: _np.ascontiguousarray(inputs[name]) for name in _INS}
    for name, a in {**given, **_constants()}.items():
        arrays[f"in_{name}_dram"] = a
        args.append(nc.dram_tensor(f"in_{name}_dram", a.shape, _mybir.dt.from_np(a.dtype), kind="ExternalInput").ap())
    for i, shape in enumerate(_OUTS):
        args.append(nc.dram_tensor(f"out_{i}_dram", shape, _mybir.dt.float32, kind="ExternalOutput").ap())
    _build(nc, *args)
    r = _run(nc, [arrays], core_ids=[0])
    return tuple(r.results[0][f"out_{i}_dram"] for i in range(len(_OUTS)))
```

```python
from contextlib import ExitStack

import concourse.bass as bass
from concourse import mybir

F32 = mybir.dt.float32
F32R = mybir.dt.float32r
BF16 = mybir.dt.bfloat16
U16 = mybir.dt.uint16
I32 = mybir.dt.int32
ALU = mybir.AluOpType
ACT = mybir.ActivationFunctionType
AX = mybir.AxisListType

P = 128
D = 1024
KC = D // P
SEQ = 512
DEC_B, DEC_T = 8, 4
NS = DEC_B * DEC_T
NT = SEQ + NS
HALF = NT // 2
TILES = SEQ // P
HD = 64
HEADS = 8
GROUPS = 3
AC = HEADS * HD // P
WINDOWS = (128, 512, 2048)
SCALE = HD ** -0.5
EPS = 1e-6
NEG = -3.0e38
NE, DE = 16, 512
FC = DE // P
TS = 96
MAX_TILES = NE + (2 * NT) // TS
MAX_PAIRS = (MAX_TILES + 1) // 2
XTILES = 2 * MAX_PAIRS + 1
TABLE = 32
COUNT_STEPS = -(-NT // TS) - 1

COL_Q = 3 * D
COL_GC = COL_Q + 3 * GROUPS * AC * P
COL_GA = COL_GC + D

B_P = 9 * AC
A_P = 3 * KC
C_P = 4 * KC
D_P = KC
A0, C0 = B_P, B_P + A_P
D0 = C0 + C_P
N_P = D0 + D_P
RING = 4
LEAD = 3
ADA_FIRST = 2 * KC
ADA_MID = 5 * KC
ADA_ALL = 6 * KC
SLOTS_B = 2 * 9
STEPS = 9
UNITS = 2 * TILES
KEYS_P = SEQ + 2 * P
KEYS_S = 2 * SEQ + P + GROUPS * NS
ROT = 8


def _build(nc, x_prompt, x_sample, cache_k1, cache_v1, cache_k2, cache_v2, cache_k3, cache_v3,
           state_conv, c_prompt, c_sample, norm1_g, norm2_g, normf_g, w_ada, b_ada, w_in, conv_w,
           w_conv_out, w_attn_out, w_o, w_rg, b_rg, w_re, b_re, w1, w3, w2,
           k_ident, k_tri, k_sel, k_small, k_ropec, k_ropes, k_maskp, k_masks,
           y_prompt, y_sample, k1_p, v1_p, k2_p, v2_p, k3_p, v3_p, conv_p,
           k1_s, v1_s, k2_s, v2_s, k3_s, v3_s, conv_s):
    caches = ((cache_k1, cache_v1), (cache_k2, cache_v2), (cache_k3, cache_v3))
    prompt_kv = ((k1_p, v1_p), (k2_p, v2_p), (k3_p, v3_p))
    sample_kv = ((k1_s, v1_s), (k2_s, v2_s), (k3_s, v3_s))

    x_rows = nc.dram_tensor("x_rows", [XTILES * TS, D], F32, kind="Internal").ap()
    y_rows = x_rows

    base = -(-nc.sbuf_base // 64) * 64
    top = nc.sbuf_top

    class Region:
        def __init__(self, at):
            self.at = at

        def __call__(self, name, shape, dt=F32):
            n = 2 if dt in (BF16, U16) else 4
            for s in shape[1:]:
                n *= s
            t = nc.alloc_sbuf_tensor_at(name, shape, dt, offset=self.at)
            self.at += -(-n // 32) * 32
            assert self.at <= top, (name, self.at, top)
            return t

    keep = Region(base)
    ident = keep("ident", [P, P])
    small = keep("small", [P, 96])
    cT = keep("cT", [P, KC, 9])
    stT = keep("stT", [P, KC, 2 * DEC_B])
    modT = keep("modT", [P, ADA_MID, 9])
    mrow = keep("mrow", [9, 2, 2 * P])
    A1 = keep("A1", [P, KC, 9])
    A2 = keep("A2", [P, KC, 9])
    last2 = keep("last2", [P, KC, 2 + 2 * DEC_B])
    stat = keep("stat", [P, 8])
    rstd = keep("rstd", [P, 8])
    oT_at = keep.at
    oT = keep("oT", [P, AC, NT])
    yb_at = keep.at
    adar = Region(yb_at)("adar", [P, RING, KC, P])
    yb = keep("yb", [P, KC, NT])
    hHi = keep("hHi", [P, KC, NT], F32R)
    hLo = keep("hLo", [P, KC, NT], F32R)
    wraw = keep("wraw", [P, RING, KC, P])
    whi = keep("whi", [P, RING, KC, P], F32R)
    wlo = keep("wlo", [P, RING, KC, P], F32R)
    c_region = keep.at
    QB = keep("QB", [P, GROUPS, AC, DEC_B, NS])
    kTn = keep("kTn", [P, GROUPS, AC, NS])
    Vn = keep("Vn", [GROUPS * NS, AC, P])

    r = Region(keep.at)
    xt = r("xt", [P, TILES + 1, D])
    hraw = r("hraw", [P, 2, KC, P])
    junk = r("junk", [P, D])
    ctok = r("ctok", [9, D])
    sttok = r("sttok", [2 * DEC_B, D])
    rows = r("rows", [88, P])

    r = Region(keep.at)
    ropec = r("ropec", [P, NT])
    ropes = r("ropes", [P, NT])
    maskp = r("maskp", [P, TILES, KEYS_P], U16)
    qT = r("qT", [P, 2, GROUPS, NT])
    kT = r("kT", [P, 2, GROUPS, NT])
    Vt = r("Vt", [P, 2, TILES, GROUPS, P])
    Kst = r("Kst", [P, 2, TILES, P])
    Kns = r("Kns", [NS, 2, P])
    vf = r("vf", [P, NT])
    pr = r("pr", [P, 2, KEYS_P])
    pTa = r("pTa", [P, 3 * P])
    pTb = r("pTb", [P, 3 * P])

    nmx = r("nmx", [P, 2])
    nb = r("nb", [P, 2])
    rs = r("rs", [P, 2])
    ri = r("ri", [P, 2])
    rope_at = r.at
    rb = r("rb", [P, 2, HALF])
    shb = r("shb", [P, 2, HALF])
    t1 = r("t1", [P, 2, HALF])
    r = Region(rope_at)
    u_sb = r("u_sb", [P, 2, HALF])
    cu = r("cu", [P, NT])
    yv = r("yv", [P, NT])
    ext = r("ext", [P, DEC_B, 6])
    gb = r("gb", [P, 2, HALF])

    r = Region(keep.at)
    kvr = r("kvr", [P, RING, 4 * HEADS * HD])
    kTs_at = r.at
    kTs = r("kTs", [P, RING, 4 * P])
    ps_ = r("ps_", [P, 2, KEYS_S])
    osm = [ps_[:, n, 0:4 * P] for n in range(2)]
    pTs_at = r.at
    pTs0 = r("pTs0", [P, 9, P])
    pTn0 = r("pTn0", [GROUPS * NS, P])
    masks = r("masks", [P, 2, KEYS_S], U16)
    sst = r("sst", [P, 2, 4])
    sample_end = r.at
    ltok = Region(pTs_at)("ltok", [2 + 2 * DEC_B, D])
    r = Region(kTs_at)
    pTs1 = r("pTs1", [P, 9, P])
    pTn1 = r("pTn1", [GROUPS * NS, P])
    pTs, pTn = (pTs0, pTs1), (pTn0, pTn1)

    toks_at = top - KC * NT * 4
    toks_at -= toks_at % 32
    assert sample_end <= toks_at
    zrow = Region(top - 2048 - 64)("zrow", [P, 512])
    ybHi = Region(toks_at)("ybHi", [P, KC, NT], F32R)
    ybLo = Region(yb_at)("ybLo", [P, KC, NT], F32R)
    r = Region(c_region)
    mixLo = r("mixLo", [P, KC, NT], F32R)
    x2_at = r.at
    gyc = r("gyc", [P, 2, HALF])
    gsg = r("gsg", [P, 2, HALF])
    gm1 = r("gm1", [P, 2, HALF])
    gmx = r("gmx", [P, 2, HALF])
    oHi = r("oHi", [P, AC, NT], F32R)
    oLo = r("oLo", [P, AC, NT], F32R)

    r = Region(x2_at)
    x2 = r("x2", [P, TILES + 1, D])
    tokt = r("tokt", [P, 3, D])
    h2_at = r.at
    mixHi = r("mixHi", [P, KC, NT], F32R)
    bcp = r("bcp", [P, KC, P])
    bcs = r("bcs", [P, KC, NS])
    op = r("op", [P, 2, NT])

    assert r.at <= toks_at
    r = Region(toks_at)
    toks = r("toks", [NS, 3, D])
    wr = r("wr", [P, KC, 20])
    tri = r("tri", [P, P])
    tri_b = r("tri_b", [P, P], BF16)
    ones_b = r("ones_b", [P, P], BF16)
    br = r("br", [P, 20])
    cst = r("cst", [P, 96])
    sel = r("sel", [9, P + NS])
    sqp = r("sqp", [P, TILES + 1, KC])
    sqj_at = r.at
    sqj = r("sqj", [P, TILES + 1, P], BF16)
    lgT = Region(sqj_at)("lgT", [20, 2, P])
    r = Region(h2_at)
    h2 = r("h2", [P, TILES + 1, D])
    lg_at = r.at
    lg = r("lg", [P, 5, 20])
    rt = r("rt", [P, 24, 5, 4])
    rs1 = r("rs1", [P, 12, 5])
    onehot = r("onehot", [P, 4, 5, NE])
    chosen = r("chosen", [P, 5, NE], BF16)
    cmp6 = r("cmp6", [P, NE, COUNT_STEPS])
    ends = r("ends", [P, 7, NE])
    cmpt = r("cmpt", [1, TABLE, NE])
    eidf = r("eidf", [1, TABLE + 16])
    tab = r("tab", [1, TABLE + 4], I32)
    slotf = r("slotf", [P, 2, 5])
    sloti = r("sloti", [P, 2, 5], I32)
    cw = r("cw", [P, 2, 5])
    assert r.at <= toks_at

    r = Region(oT_at)
    e1 = r("e1", [P, 2, KC, DE])
    e3 = r("e3", [P, 2, KC, DE])
    e2_at = r.at
    e2 = r("e2", [P, 2, FC, D])
    h2T_at = r.at
    xg = r("xg", [TS, 2, D])
    xgT = r("xgT", [P, 2, KC, TS])
    sil = r("sil", [P, 2, FC, TS])
    hid_at = r.at
    hid = r("hid", [P, 2, FC, TS])
    hidLo = Region(hid_at)("hidLo", [P, 2, FC, TS], F32R)
    yev = r("yev", [TS, 2, D])
    assert r.at <= x2_at
    e2Lo = Region(e2_at)("e2Lo", [P, 2, FC, D], F32R)
    r = Region(h2_at)
    e2Hi = r("e2Hi", [P, FC, D], F32R)
    hidHi = r("hidHi", [P, FC, TS], F32R)
    assert r.at <= lg_at
    r = Region(h2T_at)
    h2T = r("h2T", [P, 2, KC, P])
    gate2 = r("gate2", [9, D])
    adar2 = r("adar2", [P, RING, KC, P])
    assert r.at <= x2_at
    r = Region(oT_at)
    ya = r("ya", [P, TILES + 1, D])
    yb2 = r("yb2", [P, TILES + 1, D])
    junk3 = r("junk3", [P, D])

    psum = nc.alloc_psum_tensor("psum", [P, 8, 512], F32)
    BANK_S, BANK_PT, BANK_O, BANK_KV, BANK_MISC = 2, 4, 5, 6, 7
    score = psum[:, BANK_S:BANK_S + 2, :].rearrange("p b n -> p (b n)")
    score_s = [psum[:, 2 + 3 * n:5 + 3 * n, :].rearrange("p b n -> p (b n)") for n in range(2)]

    win = w_in[0].rearrange("(k p) n -> p k n", p=P)
    wada = w_ada[0].rearrange("(k p) n -> p k n", p=P)
    wco = w_conv_out[0].rearrange("(k p) n -> p k n", p=P)
    wao = w_attn_out[0].rearrange("(k p) n -> p k n", p=P)
    wgc = win[:, :, COL_GC:COL_GC + D]
    wga = win[:, :, COL_GA:COL_GA + D]
    wo = w_o[0].rearrange("(k p) n -> p k n", p=P)
    w1_v = w1[0].rearrange("g e (k p) f -> (g e) p k f", p=P)
    w3_v = w3[0].rearrange("g e (k p) f -> (g e) p k f", p=P)
    w2_v = w2[0].rearrange("g e (k p) f -> (g e) p k f", p=P)
    xp_v = x_prompt[0].rearrange("(n b a) d -> a b n d", b=4, a=TILES)
    yp_v = y_prompt[0].rearrange("(n b a) d -> a b n d", b=4, a=TILES)
    xs_v = x_sample.rearrange("b q d -> (b q) d")
    ys_v = y_sample.rearrange("b q d -> (b q) d")

    def piece_source(m):
        if m < A0:
            c, j = divmod(m, 9)
            g, kv = divmod(j, 3)
            col = COL_Q + GROUPS * AC * P * kv + AC * P * g + P * c
            return win[:, :, col:col + P]
        if m < C0:
            f, j = divmod(m - A0, 3)
            return win[:, :, D * j + P * f:D * j + P * f + P]
        assert m >= D0
        return wo[:, :, P * (m - D0):P * (m - D0) + P]

    def branch_source(j, cols):
        if j == 0:
            return wco[:, :, cols], wraw[:, 0]
        if j == 2:
            return wao[:, :, cols], wraw[:, 2, 0:AC]
        return (wgc if j == 1 else wga)[:, :, cols], wraw[:, j]

    kn_rows = nc.dram_tensor("kn_rows", [GROUPS, NS, AC * P], F32, kind="Internal").ap()
    vn_rows = nc.dram_tensor("vn_rows", [GROUPS, NS, AC * P], F32, kind="Internal").ap()

    SHIFTS = []
    for g in (2, 1):
        rows_g = WINDOWS[g] - DEC_T
        parts = 4 if g == 2 else 1
        n = rows_g // parts
        for b in range(DEC_B):
            for kv in range(1 if g == 2 else 2):
                for i in range(parts):
                    src = caches[g][kv][0, b, DEC_T + i * n:DEC_T + (i + 1) * n].rearrange("r h d -> (r h d)")
                    dst = sample_kv[g][kv][0, b, i * n:(i + 1) * n].rearrange("r h d -> (r h d)")
                    SHIFTS.append((dst.rearrange("(x y) -> x y", x=64), src.rearrange("(x y) -> x y", x=64)))
    for kv in range(2):
        src = caches[0][kv][0, :, DEC_T:].rearrange("b r h d -> b (r h d)")
        dst = sample_kv[0][kv][0, :, 0:WINDOWS[0] - DEC_T].rearrange("b r h d -> b (r h d)")
        SHIFTS.append((dst.rearrange("b (x y) -> b x y", x=4), src.rearrange("b (x y) -> b x y", x=4)))

    SHIFTS_AB = len(SHIFTS)
    assert SHIFTS_AB <= C0

    kv_units = [(half, kv, j, g) for kv in range(2) for half in range(2) for j in range(4) for g in (1, 2, 0)]
    K_COL = {1: 0, 2: 4 * P, 0: 8 * P}
    K_TILE = {1: 0, 2: 4, 0: 8}
    NEW_COL = 9 * P

    def cache_source(w):
        half, kv, j, g = kv_units[w]
        v = caches[g][kv][0, 4 * half + j]
        if g == 0:
            return v.rearrange("n h d -> n (h d)")
        if g == 1:
            return v.rearrange("(n r) h d -> n (r h d)", r=4)
        return v.rearrange("(n r) h d -> n r (h d)", r=16)[:, 0:DEC_T, :]

    def kv_tiles(g):
        return 1 if g == 0 else 4

    def kind(m):
        if m < A0:
            return "qkv"[m % 3]
        return ("u", "c", "b")[(m - A0) % 3]

    def unit_at(step):
        if not 0 <= step < STEPS * AC or step % STEPS == STEPS - 1:
            return None
        c, k = divmod(step, STEPS)
        return c * UNITS + k, c, k // 2, k % 2

    def step_of(G):
        return (G - SLOTS_B) // 2 if G >= SLOTS_B else -9

    with ExitStack() as ctx:
        def sem(name):
            return ctx.enter_context(nc.semaphore(name))

        cst_in = sem("cst_in")
        x_in = sem("x_in")
        rope_in = sem("rope_in")
        ada_in = [sem(f"ada_in{k}") for k in range(RING)]
        raw_in = [sem(f"raw_in{k}") for k in range(RING)]
        silu_done = sem("silu_done")
        first_T = sem("first_T")
        first_ev = sem("first_ev")
        ada_pe = sem("ada_pe")
        ada_ev = sem("ada_ev")
        mrow_done = sem("mrow_done")
        mT_pe = sem("mT_pe")
        sq_done = sem("sq_done")
        ms_done = sem("ms_done")
        sqrt_done = sem("sqrt_done")
        xn_done = sem("xn_done")
        xT_pe = sem("xT_pe")
        rec_done = sem("rec_done")
        hraw_act = sem("hraw_act")
        hraw_done = sem("hraw_done")
        hhi_done = sem("hhi_done")
        hlo_done = sem("hlo_done")
        dve_local = sem("dve_local")
        hi_done = sem("hi_done")
        lo_done = sem("lo_done")
        grp = sem("grp")
        bank_free = [sem("bank_free0"), sem("bank_free1")]
        shuf_done = sem("shuf_done")
        rot_done = sem("rot_done")
        rope_done = sem("rope_done")
        qb_zero = sem("qb_zero")
        qb_done = sem("qb_done")
        kt_pe = sem("kt_pe")
        kt_ev = sem("kt_ev")
        vt_pe = sem("vt_pe")
        vt_ev = sem("vt_ev")
        k_out = [sem("k_out0"), sem("k_out1")]
        v_out = [sem("v_out0"), sem("v_out1")]
        misc_ev = sem("misc_ev")
        s_pe = sem("s_pe")
        s_mx = sem("s_mx")
        s_nb = sem("s_nb")
        s_exp = sem("s_exp")
        p_done = sem("p_done")
        pta_pe = sem("pta_pe")
        pta_ev = sem("pta_ev")
        pva_pe = sem("pva_pe")
        ptb_pe = sem("ptb_pe")
        ptb_ev = sem("ptb_ev")
        pvb_pe = sem("pvb_pe")

        o_ev = sem("o_ev")
        cu_done = sem("cu_done")
        yb_done = sem("yb_done")
        shift_out = sem("shift_out")
        conv_out = sem("conv_out")
        mask_in = sem("mask_in")
        kv_in = [sem(f"kv_in{k}") for k in range(RING)]
        osm_done = sem("osm_done")
        orow_pe = sem("orow_pe")
        ktr_pe = sem("ktr_pe")
        ktr_act = sem("ktr_act")
        ktr_dve = sem("ktr_dve")
        ss_pe = sem("ss_pe")
        ssn_pe = sem("ssn_pe")
        ss_mx = sem("ss_mx")
        ss_nb = sem("ss_nb")
        ss_exp = sem("ss_exp")
        ss_p = sem("ss_p")
        spt_pe = sem("spt_pe")
        spt_ev = sem("spt_ev")
        spv_pe = sem("spv_pe")
        so_pe = sem("so_pe")
        so_ev = sem("so_ev")
        lt_pe = sem("lt_pe")
        lt_ev = sem("lt_ev")
        yo_hi = sem("yo_hi")
        yo_lo = sem("yo_lo")
        g_m1 = sem("g_m1")
        g_m2 = sem("g_m2")
        g_mx = sem("g_mx")
        g_hi = sem("g_hi")
        g_lo = sem("g_lo")
        xr_in = sem("xr_in")
        late_in = sem("late_in")
        op_done = sem("op_done")
        opT_pe = sem("opT_pe")
        x2_half = sem("x2_half")
        x2_done = sem("x2_done")
        op_half = sem("op_half")
        bc_done = sem("bc_done")
        bcT_pe = sem("bcT_pe")
        bcT_ev = sem("bcT_ev")
        ss2_done = sem("ss2_done")
        h2_done = sem("h2_done")
        h2T_pe = sem("h2T_pe")
        h2T_ev = sem("h2T_ev")
        lg_pe = sem("lg_pe")
        lgT_ev = sem("lgT_ev")
        lgT_pe = sem("lgT_pe")
        rt_dve = sem("rt_dve")
        rt_act = sem("rt_act")
        oh_done = sem("oh_done")
        pos_pe = sem("pos_pe")
        slot_done = sem("slot_done")
        tab_done = sem("tab_done")
        zrow_done = sem("zrow_done")
        xz_out = sem("xz_out")
        disp_out = sem("disp_out")
        xg_in = [sem("xg_in0"), sem("xg_in1")]
        e1_in = [sem("e1_in0"), sem("e1_in1")]
        e3_in = [sem("e3_in0"), sem("e3_in1")]
        e2_in = [sem("e2_in0"), sem("e2_in1")]
        xgT_pe = sem("xgT_pe")
        xgT_ev = sem("xgT_ev")
        a_pe = sem("a_pe")
        ab_pe = sem("ab_pe")
        sil_done = sem("sil_done")
        hid_done = sem("hid_done")
        ye_pe = sem("ye_pe")
        ye_ev0 = sem("ye_ev0")
        ye_ev1 = sem("ye_ev1")
        ye_out = [sem("ye_out0"), sem("ye_out1")]
        ya_done = sem("ya_done")
        yg_in = [sem(f"yg_in{k}") for k in range(TILES + 1)]
        nf_in = sem("nf_in")
        f_mix = sem("f_mix")
        f_sq = sem("f_sq")
        f_y = sem("f_y")
        y_out = sem("y_out")

        kn_pe = sem("kn_pe")
        kn_out = sem("kn_out")
        tail_out = sem("tail_out")
        all_stored = sem("all_stored")
        vn_out = sem("vn_out")

        block = ctx.enter_context(nc.Block())

        def misc_before(G, part):
            n = 0
            for g in range(G + 1):
                for q in range(3):
                    if (g, q) >= (G, part):
                        return n
                    n += misc_use(g, q)
            return n

        def misc_use(G, part):
            m = G // 2
            if part == 0:
                return G % 2 == 0 and 2 <= m < B_P + 2 and kind(m - 2) in "kv"
            if part == 1:
                return G % 2 == 1 and m < ADA_MID - ADA_FIRST
            return G % 2 == 0 and 1 <= m <= ADA_MID - ADA_FIRST

        MISC = {(G, q): misc_before(G, q) for G in range(2 * C0) for q in range(3) if misc_use(G, q)}
        MISC_ALL = len(MISC)

        @block.sync
        def _(sp):
            sp.dma_start(ident[:, :], k_ident).then_inc(cst_in, 16)
            sp.dma_start(ctok[0:1, :], c_prompt).then_inc(cst_in, 16)
            sp.dma_start(ctok[1:9, :], c_sample).then_inc(cst_in, 16)
            sp.dma_start(rows[0:48, :], b_ada[0].rearrange("(c p) -> c p", p=P)).then_inc(cst_in, 16)
            sp.dma_start(rows[48:56, :], norm1_g[0].rearrange("(c p) -> c p", p=P)).then_inc(cst_in, 16)
            sp.dma_start(rows[56:64, :], norm2_g[0].rearrange("(c p) -> c p", p=P)).then_inc(cst_in, 16)
            sp.dma_start(rows[64:88, :], conv_w[0].rearrange("j (c p) -> (j c) p", p=P)).then_inc(cst_in, 16)
            sp.dma_start(sttok[:, :], state_conv[0].rearrange("b r d -> (b r) d")).then_inc(cst_in, 16)
            for k in range(RING):
                sp.dma_start(adar[:, k], wada[:, :, P * k:P * k + P]).then_inc(ada_in[k], 16)
            for a in range(TILES):
                for b in range(4):
                    sp.dma_start(xt[32 * b:32 * b + 32, a, :], xp_v[a, b]).then_inc(x_in, 16)
            sp.dma_start(xt[0:NS, TILES, :], xs_v).then_inc(x_in, 16)
            with sp.Fori(1, ADA_FIRST // RING) as i:
                for k in range(RING):
                    sp.wait_ge(ada_pe, 4 * i + (k - 3))
                    sp.dma_start(adar[:, k], wada[:, :, bass.ds((4 * i + k) * P, P)]).then_inc(ada_in[k], 16)
            for m in range(C0):
                if m == RING:
                    sp.wait_ge(hlo_done, TILES + 1)
                    sp.wait_ge(first_ev, 3)
                    sp.dma_start(ropec[:, :], k_ropec).then_inc(rope_in, 16)
                    sp.dma_start(ropes[:, :], k_ropes).then_inc(rope_in, 16)
                    sp.dma_start(maskp[:, :, :], k_maskp).then_inc(rope_in, 16)
                if m >= RING:
                    sp.wait_ge(lo_done, m - RING + 1)
                sp.dma_start(wraw[:, m % RING], piece_source(m)).then_inc(raw_in[m % RING], 16)
                if m < ADA_MID - ADA_FIRST:
                    n = ADA_FIRST + m
                    sp.wait_ge(ada_pe, n - RING + 1)
                    sp.dma_start(adar[:, n % RING], wada[:, :, P * n:P * n + P]).then_inc(ada_in[n % RING], 16)
                if m < SHIFTS_AB:
                    dst, src = SHIFTS[m]
                    sp.dma_start(dst, src).then_inc(shift_out, 16)
                else:
                    if m == SHIFTS_AB:
                        sp.wait_ge(zrow_done, 1)
                    n0, n1 = (XTILES * (m - SHIFTS_AB + n) // (C0 - SHIFTS_AB) for n in range(2))
                    zdst = x_rows[TS * n0:TS * n1].rearrange("(p r) (o n) -> p (r o) n", p=TS, n=512)
                    zsrc = zrow[0:TS, :].rearrange("p (o n) -> p o n", o=1)
                    sp.dma_start(zdst, zsrc.to_broadcast([TS, 2 * (n1 - n0), 512])).then_inc(xz_out, 16)
            for m in range(C0, C0 + RING):
                sp.wait_ge(lo_done, m - RING + 1)
                src, dst = branch_source(m - C0, slice(0, P))
                sp.dma_start(dst, src).then_inc(raw_in[m % RING], 16)
            sp.wait_ge(o_ev, UNITS * AC)

            for k in range(2):
                sp.wait_ge(k_out[k], 64 * (GROUPS * AC // 2))
                sp.wait_ge(v_out[k], 64 * GROUPS * (AC // 2))
            sp.dma_start(masks[:, :, :], k_masks).then_inc(mask_in, 16)
            for w, (half, kv, j, g) in enumerate(kv_units):
                if w >= RING:
                    h0, kv0, j0, g0 = kv_units[w - RING]
                    done = 12 * h0 + 3 * j0 + (1, 2, 0).index(g0) + 1
                    if kv0 == 0:
                        sp.wait_ge(ktr_pe, AC * done)
                    else:
                        sp.wait_ge(spv_pe, done)
                src = cache_source(w)
                dst = kvr[:, w % RING, 0:kv_tiles(g) * 512]
                if g == 2:
                    dst = dst.rearrange("p (r n) -> p r n", n=512)
                sp.dma_start(dst, src).then_inc(kv_in[w % RING], 16)
            def shift_v3(b, j):
                n = (WINDOWS[2] - DEC_T) // 4
                src = cache_v3[0, b, DEC_T + j * n:DEC_T + (j + 1) * n].rearrange("b r h d -> (b r h d)")
                dst = v3_s[0, b, j * n:(j + 1) * n].rearrange("b r h d -> (b r h d)")
                sp.dma_start(dst.rearrange("(x y) -> x y", x=64), src.rearrange("(x y) -> x y", x=64))\
                    .then_inc(shift_out, 16)

            with sp.Fori(0, KC - 1) as f:
                for j in range(RING):
                    shift_v3(bass.ds(f, 1), j)
                    sp.wait_ge(lo_done, 4 * f + (C0 + j + 1))
                    src, dst = branch_source(j, bass.ds(f * P + P, P))
                    sp.dma_start(dst, src).then_inc(raw_in[j], 16)
            for m in range(D0, N_P):
                sp.wait_ge(lo_done, m - RING + 1)
                sp.dma_start(wraw[:, m % RING], piece_source(m)).then_inc(raw_in[m % RING], 16)
                if m == D0 + RING - 1:
                    sp.wait_ge(grp, 2 * D0)
                    sp.wait_ge(g_lo, 2 * KC)
                    for a in range(TILES):
                        for b in range(4):
                            sp.dma_start(x2[32 * b:32 * b + 32, a, :], xp_v[a, b]).then_inc(xr_in, 16)
                    sp.dma_start(x2[0:NS, TILES, :], xs_v).then_inc(xr_in, 16)
            sp.dma_start(tri[:, :], k_tri).then_inc(late_in, 16)
            sp.dma_start(cst[:, :], k_small).then_inc(late_in, 16)
            sp.dma_start(sel[:, :], k_sel).then_inc(late_in, 16)
            sp.dma_start(wr[:, :, 0:4], w_rg[0].rearrange("(k p) n -> p k n", p=P)).then_inc(late_in, 16)
            sp.dma_start(wr[:, :, 4:20], w_re[0].rearrange("(k p) n -> p k n", p=P)).then_inc(late_in, 16)
            sp.dma_start(br[:, 0:4], b_rg.to_broadcast([P, 4])).then_inc(late_in, 16)
            sp.dma_start(br[:, 4:20], b_re.to_broadcast([P, 16])).then_inc(late_in, 16)
            sp.dma_start(e1[:, 0], w1_v[0]).then_inc(e1_in[0], 16)
            sp.dma_start(e3[:, 0], w3_v[0]).then_inc(e3_in[0], 16)
            sp.dma_start(e1[:, 1], w1_v[1]).then_inc(e1_in[1], 16)
            for j in range(RING):
                shift_v3(slice(KC - 1, KC), j)
            sp.wait_ge(grp, 2 * N_P)
            sp.dma_start(gate2[:, :], b_ada[0:1, 5 * D:6 * D].to_broadcast([9, D])).then_inc(late_in, 16)
            for n in range(ADA_MID, ADA_MID + RING):
                sp.dma_start(adar2[:, n % RING], wada[:, :, P * n:P * n + P]).then_inc(ada_in[n % RING], 16)
            sp.dma_start(e2[:, 0], w2_v[0]).then_inc(e2_in[0], 16)
            sp.dma_start(e3[:, 1], w3_v[1]).then_inc(e3_in[1], 16)
            sp.dma_start(e2[:, 1], w2_v[1]).then_inc(e2_in[1], 16)
            for n in range(ADA_MID + RING, ADA_ALL):
                sp.wait_ge(ada_pe, n - RING + 1)
                sp.dma_start(adar2[:, n % RING], wada[:, :, P * n:P * n + P]).then_inc(ada_in[n % RING], 16)
            sp.wait_ge(disp_out, 160)
            sp.dma_start(xg[:, 0, :], x_rows[0:TS, :]).then_inc(xg_in[0], 16)
            sp.dma_start(xg[:, 1, :], x_rows[TS:2 * TS, :]).then_inc(xg_in[1], 16)
            sp.wait_ge(h2_done, TILES + 1)
            sp.dma_start(tokt[:, 0, :], normf_g.rearrange("(a n) -> a n", a=1).to_broadcast([P, D])).then_inc(nf_in, 16)
            sp.wait_ge(tab_done, 1)
            pairs = sp.value_load(tab[0:1, TABLE:TABLE + 1], min_val=NE // 2, max_val=MAX_PAIRS)
            sp.wait_ge(xgT_pe, 2)
            sp.dma_start(xg[:, 0, :], x_rows[2 * TS:3 * TS, :]).then_inc(xg_in[0], 16)
            with sp.Fori(1, pairs) as jp:
                for q in range(2):
                    e = sp.value_load(tab[0:1, bass.ds(2 * jp + q, 1)], min_val=0, max_val=NE - 1)
                    sp.wait_ge(a_pe, 2 * jp + (q - 1))
                    sp.dma_start(e1[:, q], w1_v[bass.ds(e, 1)].rearrange("e p k f -> (e p) k f")).then_inc(e1_in[q], 16)
                    sp.wait_ge(ab_pe, 2 * jp + (q + 1))
                    sp.dma_start(e3[:, q], w3_v[bass.ds(e, 1)].rearrange("e p k f -> (e p) k f")).then_inc(e3_in[q], 16)
                    sp.wait_ge(xgT_pe, 2 * jp + (q + 1))
                    sp.dma_start(xg[:, 1 - q, :], x_rows[bass.ds((2 * jp + (q + 1)) * TS, TS), :])\
                        .then_inc(xg_in[1 - q], 16)
                    sp.wait_ge(ye_pe, 4 * jp + (2 * q + 2))
                    sp.dma_start(e2[:, q], w2_v[bass.ds(e, 1)].rearrange("e p k f -> (e p) k f")).then_inc(e2_in[q], 16)
            for tt in range(TILES + 1):
                sp.wait_ge(f_y, tt + 1)
                if tt < TILES:
                    for b in range(4):
                        sp.dma_start(yp_v[tt, b], x2[32 * b:32 * b + 32, tt, :]).then_inc(y_out, 16)
                else:
                    sp.dma_start(ys_v, x2[0:NS, tt, :]).then_inc(y_out, 16)
            sp.wait_ge(y_out, 16 * (4 * TILES + 1))
            sp.wait_ge(shift_out, 16 * (SHIFTS_AB + 4 * KC))
            sp.wait_ge(conv_out, 32)
            sp.wait_ge(kn_out, 16 * GROUPS * AC)
            sp.wait_ge(vn_out, 16 * GROUPS)
            sp.wait_ge(tail_out, 16 * 2 * GROUPS)

        @block.tensor
        def _(pe):
            pe.wait_ge(cst_in, 128)
            pe.transpose(psum[:, 0, 0:88], rows[:, :], ident[0:88, 0:88]).then_inc(first_T, 1)
            pe.wait_ge(silu_done, 1)
            for k in range(KC):
                mm = pe.transpose(psum[:, 1, 16 * k:16 * k + 9], ctok[:, P * k:P * k + P], ident[0:9, 0:9])
            mm.then_inc(first_T, 1)
            for k in range(KC):
                mm = pe.transpose(psum[:, 2, 16 * k:16 * k + 16], sttok[:, P * k:P * k + P], ident[0:16, 0:16])
            mm.then_inc(first_T, 1)

            def modulation(slot, out, ring=adar):
                for k in range(KC):
                    mm = pe.matmul(out, cT[:, k, :], ring[:, slot, k, :], start=(k == 0), stop=(k == KC - 1))
                mm.then_inc(ada_pe, 1)

            def modulation_T(src, out):
                return pe.transpose(out, src, ident[0:9, 0:9])

            pe.wait_ge(first_ev, 3)
            with pe.Fori(0, ADA_FIRST // RING) as i:
                for k in range(RING):
                    pe.wait_ge(ada_in[k], 16 * i + 16)
                    if k % 2 == 0:
                        pe.wait_ge(mrow_done, 2 * i + (k // 2 + 1))
                    modulation(k, psum[0:9, 4 + k // 2, P * (k % 2):P * (k % 2) + P])
                for h in range(2):
                    pe.wait_ge(mrow_done, 2 * i + (h + 3))
                    pe.wait_ge(ada_ev, 2 * i + (h + 1))
                    for k in range(2):
                        mm = pe.matmul(psum[:, 6 + h, 16 * k:16 * k + 9], mrow[:, h, P * k:P * k + P], ident[0:9, 0:9],
                                       start=True, stop=True)
                    mm.then_inc(mT_pe, 1)

            for tt in range(TILES + 1):
                n = P if tt < TILES else NS
                pe.wait_ge(xn_done, tt + 1)
                if tt >= 2:
                    pe.wait_ge(hraw_done, tt - 1)
                    pe.wait_ge(hraw_act, min(tt - 1, TILES))
                for k in range(KC):
                    mm = pe.transpose(psum[:, 2 * (tt % 2) + k // 4, P * (k % 4):P * (k % 4) + n],
                                      xt[0:n, tt, P * k:P * k + P], ident[0:n, 0:n])
                mm.then_inc(xT_pe, 1)
            def project(m, slot, xhi, xlo, t, k_n=KC, free=None):
                if free is not None:
                    pe.wait_ge(bank_free[t], free)
                cols = slice(HALF * t, HALF * t + HALF)
                for k in range(k_n):
                    for n, (w, x) in enumerate(((whi, xhi), (wlo, xhi), (whi, xlo))):
                        mm = pe.matmul(psum[:, t, 0:HALF], w[:, slot, k, :], x[:, k, cols],
                                       start=(k == 0 and n == 0), stop=(k == k_n - 1 and n == 2))
                mm.then_inc(grp, 1)

            def keys_values_T(G):
                m = G // 2 - 2
                c, j = divmod(m, 9)
                g, kv = divmod(j, 3)
                n = GROUPS * c + g
                if kind(m) == "k":
                    pe.wait_ge(rope_done, 4 * n + 4)
                    if n >= 1:
                        pe.wait_ge(vt_ev, n)
                    src = kT[:, c % 2, g, :]
                else:
                    pe.wait_ge(bank_free[0], m + 1)
                    pe.wait_ge(bank_free[1], m + 1)
                    pe.wait_ge(kt_ev, n + 1)
                    src = vf[:, :]
                for a in range(TILES):
                    mm = pe.transpose(psum[:, BANK_KV, P * a:P * a + P], src[:, P * a:P * a + P], ident[:, :])
                mm.then_inc(kt_pe if kind(m) == "k" else vt_pe, 1)
                if MISC[G, 0] > 0:
                    pe.wait_ge(misc_ev, MISC[G, 0])
                at = 0 if kind(m) == "k" else NS * g
                pe.matmul(psum[at:at + NS, BANK_MISC, 0:P], src[:, SEQ:NT], ident[:, :], start=True, stop=True)\
                    .then_inc(kn_pe, 1)

            def values_part(u, second):
                _, c, a, h = u
                for i in range(3):
                    n = 3 * second + i
                    g, tile_ = (0, n) if n < TILES else (n - TILES + 1, a)
                    mm = pe.matmul(psum[HD * h:HD * h + HD, BANK_O, 0:P], Vt[:, c % 2, tile_, g, HD * h:HD * h + HD],
                                   (pTb if second else pTa)[:, P * i:P * i + P], start=(n == 0), stop=(n == 5))
                return mm

            def probs_T(u, second):
                for i in range(3):
                    n = 3 * second + i
                    mm = pe.transpose(psum[:, BANK_PT, P * i:P * i + P], pr[:, u[0] % 2, P * n:P * n + P],
                                      ident[:, :])
                return mm

            def attend(G):
                step = step_of(G)
                if G % 2 == 0:
                    u = unit_at(step - 2)
                    if u:
                        pe.wait_ge(ptb_ev, u[0] + 1)
                        values_part(u, 1).then_inc(pvb_pe, 1)
                    u = unit_at(step)
                    if u:
                        n, c, a, h = u
                        pe.wait_ge(rope_done, 12 * (c + 1))
                        if n >= 1:
                            pe.wait_ge(s_mx, n)
                        rows_h = slice(HD * h, HD * h + HD)
                        q = [qT[rows_h, c % 2, g, P * a:P * a + P] for g in range(GROUPS)]
                        pe.matmul(score[:, 0:SEQ], q[0], kT[rows_h, c % 2, 0, 0:SEQ], start=True, stop=True)
                        for g in (1, 2):
                            mm = pe.matmul(score[:, SEQ + P * (g - 1):SEQ + P * g], q[g],
                                           kT[rows_h, c % 2, g, P * a:P * a + P], start=True, stop=True)
                        mm.then_inc(s_pe, 1)
                    u = unit_at(step - 1)
                    if u:
                        pe.wait_ge(p_done, u[0] + 1)
                        if u[0] >= 1:
                            pe.wait_ge(ptb_ev, u[0])
                        probs_T(u, 0).then_inc(pta_pe, 1)
                else:
                    u = unit_at(step - 1)
                    if u:
                        pe.wait_ge(pta_ev, u[0] + 1)
                        pe.wait_ge(vt_ev, GROUPS * (u[1] + 1))
                        if u[0] >= 1:
                            pe.wait_ge(o_ev, u[0])
                        values_part(u, 0).then_inc(pva_pe, 1)
                        probs_T(u, 1).then_inc(ptb_pe, 1)

            for G in range(2 * C0):
                m, t = divmod(G, 2)
                if misc_use(G, 0):
                    keys_values_T(G)
                attend(G)
                if misc_use(G, 1):
                    n = ADA_FIRST + m
                    if MISC[G, 1] > 0:
                        pe.wait_ge(misc_ev, MISC[G, 1])
                    pe.wait_ge(ada_in[n % RING], 16 * (n // RING + 1))
                    modulation(n % RING, psum[0:9, BANK_MISC, 0:P])
                if misc_use(G, 2):
                    pe.wait_ge(misc_ev, MISC[G, 2])
                    modulation_T(mrow[:, m % 2, 0:P], psum[:, BANK_MISC, 0:9]).then_inc(mT_pe, 1)
                if t == 0:
                    pe.wait_ge(lo_done, m + 1)
                if G == 0:
                    pe.wait_ge(hlo_done, TILES + 1)
                project(m, m % RING, hHi, hLo, t, free=m if m >= 1 else None)

            pe.wait_ge(cu_done, 2 * KC)
            pe.wait_ge(misc_ev, MISC_ALL)
            for k in range(KC):
                mm = pe.transpose(psum[0:18, 6 + k // 4, P * (k % 4):P * (k % 4) + P], last2[:, k, :], ident[:, :])
            mm.then_inc(lt_pe, 1)

            pe.wait_ge(bank_free[0], C0)
            pe.wait_ge(bank_free[1], C0)
            pe.wait_ge(qb_done, 3 * GROUPS * AC)
            pe.wait_ge(lt_ev, 2)
            for half in range(2):
                chunks = [(3 * j + gi, j, g, ch) for j in range(4) for gi, g in enumerate((1, 2, 0)) for ch in range(AC)]

                def keys_T(n):
                    i, j, g, ch = chunks[n]
                    x = half * len(chunks) + n
                    w = 12 * half + i
                    if ch == 0:
                        pe.wait_ge(kv_in[w % RING], 16 * (w // RING + 1))
                    if x >= 2:
                        pe.wait_ge((ktr_act, ktr_dve)[x % 2], x // 2)
                    for r_ in range(kv_tiles(g)):
                        mm = pe.transpose(psum[:, x % 2, P * r_:P * r_ + P],
                                          kvr[:, w % RING, 512 * r_ + P * ch:512 * r_ + P * ch + P], ident[:, :])
                    mm.then_inc(ktr_pe, 1)

                def scores_s(n):
                    i, j, g, ch = chunks[n]
                    x = half * len(chunks) + n
                    pe.wait_ge((ktr_act, ktr_dve)[x % 2], x // 2 + 1)
                    w_ = P * kv_tiles(g)
                    pe.matmul(score_s[half][32 * j:32 * j + 32, K_COL[g]:K_COL[g] + w_], QB[:, g, ch, 4 * half + j, :],
                              kTs[:, x % RING, 0:w_], start=(ch == 0), stop=(ch == AC - 1)).then_inc(ss_pe, 1)

                for n in range(len(chunks) + 1):
                    if n < len(chunks):
                        keys_T(n)
                    if n >= 1:
                        scores_s(n - 1)
                for j in range(4):
                    for g in range(GROUPS):
                        for ch in range(AC):
                            mm = pe.matmul(score_s[half][32 * j:32 * j + 32, NEW_COL + NS * g:NEW_COL + NS * g + NS],
                                           QB[:, g, ch, 4 * half + j, :], kTn[:, g, ch, :],
                                           start=(ch == 0), stop=(ch == AC - 1))
                mm.then_inc(ssn_pe, 1)
            pe.wait_ge(ktr_act, len(chunks))
            pe.wait_ge(ktr_dve, len(chunks))
            for half in range(2):
                pe.wait_ge(ss_p, half + 1)
                for part in range(3 * half, 3 * half + 3):
                    if part >= 2:
                        pe.wait_ge(spt_ev, part - 1)
                    for i in range(4 if part % 3 < 2 else 2):
                        n = 4 * (part % 3) + i
                        if n < 9:
                            mm = pe.transpose(psum[:, part % 2, P * i:P * i + P], ps_[:, half, P * n:P * n + P], ident[:, :])
                        else:
                            mm = pe.transpose(psum[0:GROUPS * NS, part % 2, P * i:P * i + P],
                                              ps_[:, half, NEW_COL:NEW_COL + GROUPS * NS], ident[:, :])
                    mm.then_inc(spt_pe, 1)
                pe.wait_ge(spt_ev, 3 * half + 3)
                for i in range(12):
                    j, g = i // 3, (1, 2, 0)[i % 3]
                    w = 24 + 12 * half + i
                    out = psum[NS * j:NS * j + NS, 2 + half, :]
                    pe.wait_ge(kv_in[w % RING], 16 * (w // RING + 1))
                    for r_ in range(kv_tiles(g)):
                        mm = pe.matmul(out, pTs[half][:, K_TILE[g] + r_, NS * j:NS * j + NS],
                                       kvr[:, w % RING, 512 * r_:512 * r_ + 512], start=(g == 1 and r_ == 0), stop=False)
                    mm.then_inc(spv_pe, 1)
                    if g == 0:
                        mm = pe.matmul(out, pTn[half][:, NS * j:NS * j + NS], Vn[:, :, :].rearrange("p c n -> p (c n)"),
                                       start=False, stop=True)
                mm.then_inc(orow_pe, 1)
                pe.wait_ge(osm_done, half + 1)
                if half == 1:
                    pe.wait_ge(so_ev, 2)
                for ch in range(AC):
                    pick = ident[:, :].rearrange("p (j n) -> p j n", j=4)[:, :, 8 * ch:8 * ch + 8]
                    mm = pe.matmul(psum[:, 4, NS * ch:NS * ch + NS], osm[half][:, P * ch:P * ch + P], pick,
                                   start=True, stop=True)
                mm.then_inc(so_pe, 1)

            pe.wait_ge(yo_lo, KC)
            with pe.Fori(0, KC) as f:
                for j in range(RING):
                    pe.wait_ge(lo_done, 4 * f + (C0 + j + 1))
                    if j == 2:
                        pe.wait_ge(yo_lo, KC + 1)
                    xhi, xlo = ((ybHi, ybLo), (hHi, hLo), (oHi, oLo), (hHi, hLo))[j]
                    for t in range(2):
                        project(None, j, xhi, xlo, t, k_n=AC if j == 2 else KC, free=4 * f + (C0 + j))
            def mixed_T(f):
                pe.wait_ge(op_done, f + 1)
                if f >= 1:
                    pe.wait_ge(x2_half, f)
                    pe.wait_ge(x2_done, f)
                for a in range(TILES):
                    pe.transpose(psum[:, 2 + f % 2, P * a:P * a + P], op[:, f % 2, P * a:P * a + P], ident[:, :])
                pe.transpose(psum[0:NS, 4, 0:P], op[:, f % 2, SEQ:NT], ident[:, :]).then_inc(opT_pe, 1)

            for m in range(D0, N_P):
                pe.wait_ge(lo_done, m + 1)
                if m == D0:
                    pe.wait_ge(g_lo, 2 * KC)
                for t in range(2):
                    project(m, m % RING, mixHi, mixLo, t, free=m)
                f = m - D0
                if 1 <= f < 5:
                    pe.wait_ge(bc_done, f)
                    if f >= 2:
                        pe.wait_ge(bcT_ev, f - 1)
                    src, rows_n = (bcp, P) if f % 2 else (bcs, NS)
                    for k in range(KC):
                        mm = pe.transpose(psum[0:rows_n, 5 + k // 4, P * (k % 4):P * (k % 4) + P], src[:, k, :],
                                          ident[:, :])
                    mm.then_inc(bcT_pe, 1)
                if f >= 1:
                    mixed_T(f - 1)
            mixed_T(KC - 1)
            def router(tt):
                n = P if tt < TILES else NS
                pe.wait_ge(h2T_ev, tt + 1)
                if tt >= 2:
                    pe.wait_ge(lgT_ev, tt - 1)
                for k in range(KC):
                    mm = pe.matmul(psum[0:20, 5 + tt % 2, 0:n], wr[:, k, :], h2T[:, tt % 2, k, 0:n],
                                   start=(k == 0), stop=(k == KC - 1))
                mm.then_inc(lg_pe, 1)

            def router_T(tt):
                n = P if tt < TILES else NS
                pe.wait_ge(lgT_ev, tt + 1)
                pe.transpose(psum[0:n, 4, 32 * tt:32 * tt + 20], lgT[:, tt % 2, 0:n], ident[0:20, 0:20])\
                    .then_inc(lgT_pe, 1)

            pe.wait_ge(x2_half, KC)
            pe.wait_ge(x2_done, KC)
            pe.wait_ge(late_in, 128)
            for tt in range(TILES + 1):
                n = P if tt < TILES else NS
                pe.wait_ge(h2_done, tt + 1)
                if tt >= 2:
                    pe.wait_ge(h2T_ev, tt - 1)
                for k in range(KC):
                    mm = pe.transpose(psum[:, 2 * (tt % 2) + k // 4, P * (k % 4):P * (k % 4) + n],
                                      h2[0:n, tt, P * k:P * k + P], ident[0:n, 0:n])
                mm.then_inc(h2T_pe, 1)
                if tt >= 1:
                    router(tt - 1)
                if tt >= 2:
                    router_T(tt - 2)
            router(TILES)
            router_T(TILES - 1)
            router_T(TILES)
            def last_gate_rows(n):
                pe.wait_ge(ada_in[n % RING], 16 * (n // RING + 1))
                at = n - ADA_MID
                modulation(n % RING, psum[0:9, 2 + at // 4, P * (at % 4):P * (at % 4) + P], adar2)

            for n in range(ADA_MID, ADA_MID + 3):
                last_gate_rows(n)
            pe.wait_ge(oh_done, 1)
            for tt in range(TILES + 1):
                n = P if tt < TILES else NS
                for s in range(tt + 1):
                    kk = P if s < TILES else NS
                    pe.matmul(psum[0:n, 5, 16 * tt:16 * tt + 16], (ones_b if s < tt else tri_b)[0:kk, 0:n],
                              chosen[0:kk, s, :], start=(s == 0), stop=(s == tt))
            for s in range(TILES + 1):
                kk = P if s < TILES else NS
                mm = pe.matmul(psum[:, 6, 0:16], ones_b[0:kk, :], chosen[0:kk, s, :],
                               start=(s == 0), stop=(s == TILES))
            mm.then_inc(pos_pe, 1)

            for n in range(ADA_MID + 3, ADA_ALL):
                last_gate_rows(n)
            pe.wait_ge(mrow_done, 3 + ADA_FIRST // 2)
            def last_gate():
                for banks, cols, rows_n in (((6, 7), slice(0, P), P), ((3, 5), slice(P, P + NS), NS)):
                    for n in range(2):
                        mm = pe.matmul(psum[0:rows_n, banks[n], :], sel[:, cols], gate2[:, 512 * n:512 * n + 512],
                                       start=True, stop=True)
                    mm.then_inc(bcT_pe, 1)

            pe.wait_ge(tab_done, 1)
            pairs = pe.value_load(tab[0:1, TABLE:TABLE + 1], min_val=NE // 2, max_val=MAX_PAIRS)
            pe.sem_inc(ab_pe, 2)
            pe.sem_inc(ye_pe, 4)
            pe.sem_inc(xgT_pe, 1)

            def rows_T(slot):
                for k in range(KC):
                    mm = pe.transpose(psum[:, k // 4, TS * (k % 4):TS * (k % 4) + TS],
                                      xg[:, slot, P * k:P * k + P], ident[0:TS, 0:TS])
                mm.then_inc(xgT_pe, 1)

            last_gate()
            pe.wait_ge(xg_in[0], 16)
            rows_T(0)
            with pe.Fori(0, pairs) as jp:
                for q in range(2):
                    pe.wait_ge(xgT_ev, 4 * jp + (2 * q + 2))
                    pe.wait_ge(hid_done, 2 * jp + (q + 1))
                    for w, bank, landed, done in ((e1, 2 + q, e1_in, a_pe), (e3, 4 + q, e3_in, ab_pe)):
                        pe.wait_ge(landed[q], 16 * jp + 16)
                        for fc in range(FC):
                            for k in range(KC):
                                mm = pe.matmul(psum[:, bank, TS * fc:TS * fc + TS], w[:, q, k, P * fc:P * fc + P],
                                               xgT[:, q, k, :], start=(k == 0), stop=(k == KC - 1))
                        mm.then_inc(done, 1)
                    pe.wait_ge(xg_in[1 - q], 16 * jp + 16 + 16 * q)
                    rows_T(1 - q)
                    pe.wait_ge(hid_done, 2 * jp + (q + 3))
                    pe.wait_ge(ye_ev0, 2 * jp + (q + 1))
                    pe.wait_ge(ye_ev1, 2 * jp + (q + 1))
                    for n in range(2):
                        cols = slice(512 * n, 512 * n + 512)
                        pe.wait_ge(hi_done, 4 * jp + (N_P + 2 * q + n + 1))
                        pe.wait_ge(lo_done, 4 * jp + (N_P + 2 * q + n + 1))
                        for part, (x, w) in enumerate(((hidHi, e2Hi[:, :, cols]), (hidHi, e2Lo[:, q, :, cols]),
                                                       (hidLo[:, q], e2Hi[:, :, cols]))):
                            if part == 2 and n == 0:
                                pe.wait_ge(g_lo, 2 * jp + (2 * KC + q + 1))
                            for fc in range(FC):
                                mm = pe.matmul(psum[0:TS, 6 + n, :], x[:, fc, :], w[:, fc, :],
                                               start=(part == 0 and fc == 0), stop=(part == 2 and fc == FC - 1))
                        mm.then_inc(ye_pe, 1)

        @block.scalar
        def _(act):
            act.wait_ge(cst_in, 128)
            act.activation(ctok[:, :], ctok[:, :], ACT.Silu).then_inc(silu_done, 1)
            act.wait_ge(first_ev, 1)
            act.wait_ge(x_in, 16 * (4 * TILES + 1))
            for tt in range(TILES + 1):
                n = P if tt < TILES else NS
                if tt:
                    act.wait_ge(sq_done, tt)
                act.activation(junk[0:n, :], xt[0:n, tt, :], ACT.Square,
                               accum_out=stat[0:n, tt:tt + 1]).then_inc(sq_done, 1)
            act.wait_ge(ms_done, 1)
            act.activation(rstd[:, :], stat[:, :], ACT.Sqrt).then_inc(sqrt_done, 1)
            act.wait_ge(rec_done, 1)
            for tt in range(TILES + 1):
                n = P if tt < TILES else NS
                act.activation(xt[0:n, tt, :], xt[0:n, tt, :], ACT.Copy, scale=rstd[0:n, tt:tt + 1]).then_inc(xn_done, 1)
            act.wait_ge(rec_done, 2)

            def split_hi(m, slot, count, pe_groups):
                act.wait_ge(raw_in[slot], count)
                if pe_groups is not None:
                    act.wait_ge(grp, pe_groups)
                act.activation(whi[:, slot], wraw[:, slot], ACT.Copy).then_inc(hi_done, 1)

            def split_hi_at(m):
                split_hi(m, m % RING, 16 * (m // RING + 1), 2 * (m - RING + 1) if m >= RING else None)

            def modulate(tt):
                if tt < TILES:
                    act.wait_ge(xT_pe, tt + 1)
                    if tt >= 2:
                        act.wait_ge(hlo_done, tt - 1)
                    for k in range(KC // 2, KC):
                        ins = act.activation(hraw[:, tt % 2, k, :],
                                             psum[:, 2 * (tt % 2) + 1, P * (k % 4):P * (k % 4) + P], ACT.Identity,
                                             bias=modT[:, k, 0:1], scale=A1[:, k, 0:1])
                    ins.then_inc(hraw_act, 1)

            modulate(0)
            for tt in range(TILES + 1):
                n = P if tt < TILES else NS
                modulate(tt + 1)
                act.wait_ge(hraw_act, min(tt + 1, TILES))
                act.wait_ge(hraw_done, tt + 1)
                act.activation(hHi[:, :, P * tt:P * tt + n], hraw[:, tt % 2, :, 0:n], ACT.Copy).then_inc(hhi_done, 1)
                if 1 <= tt <= LEAD:
                    split_hi_at(tt - 1)
            for G in range(2 * C0):
                m, t = divmod(G, 2)
                if t == 0:
                    if m + LEAD < C0:
                        split_hi_at(m + LEAD)
                    if 2 <= m < B_P + 2 and kind(m - 2) == "v":
                        c, g = divmod((m - 2) // 3, GROUPS)
                        n = GROUPS * c + g
                        act.wait_ge(vt_pe, n + 1)
                        if c >= 2:
                            act.wait_ge(pvb_pe, UNITS * (c - 1))
                            act.wait_ge(v_out[c % 2], 64 * GROUPS * (c // 2))
                        act.activation(Vt[:, c % 2, :, g, :], psum[:, BANK_KV, :].rearrange("p (a n) -> p a n", n=P),
                                       ACT.Copy).then_inc(vt_ev, 1)
                    step = step_of(G)
                    u = unit_at(step - 1)
                    if u:
                        act.wait_ge(pta_pe, u[0] + 1)
                        if u[0] >= 1:
                            act.wait_ge(pva_pe, u[0])
                        act.activation(pTa[:, :], psum[:, BANK_PT, 0:3 * P], ACT.Copy).then_inc(pta_ev, 1)
                    u = unit_at(step)
                    if u:
                        s = u[0] % 2
                        act.wait_ge(s_nb, u[0] + 1)
                        act.activation(pr[:, s], pr[:, s], ACT.Exp, bias=nb[:, s:s + 1], scale=SCALE,
                                       accum_out=rs[:, s:s + 1]).then_inc(s_exp, 1)
                if kind(m) == "b":
                    act.wait_ge(grp, G + 1)
                    f = (m - A0) // 3
                    if f >= 1:
                        act.wait_ge(yb_done, 2 * f - 1 + t)
                    act.activation(gb[:, t, :], psum[:, t, 0:HALF], ACT.Copy).then_inc(bank_free[t], 1)
                if kind(m) in "qkvu":
                    act.wait_ge(grp, G + 1)
                    if kind(m) in "qk":
                        R = 4 * (m // 3) + 2 * (m % 3) + t
                        if R >= 2:
                            act.wait_ge(rot_done, 2 * (R - 1))
                        dst = rb[:, t, :]
                    elif kind(m) == "v":
                        if m >= 3:
                            act.wait_ge(kn_pe, 2 * (m // 3))
                        dst = vf[:, HALF * t:HALF * t + HALF]
                    else:
                        if m == A0:
                            act.wait_ge(rope_done, 4 * GROUPS * AC)
                        act.wait_ge(bank_free[t], m)
                        dst = u_sb[:, t, :]
                    act.activation(dst, psum[:, t, 0:HALF], ACT.Copy).then_inc(bank_free[t], 1)

            act.wait_ge(lt_pe, 1)
            act.wait_ge(mask_in, 16)
            for n in range(2):
                act.activation(ltok[:, 512 * n:512 * n + 512], psum[0:18, 6 + n, :], ACT.Copy).then_inc(lt_ev, 1)
            for m in range(C0, C0 + LEAD):
                split_hi_at(m)
            act.wait_ge(yb_done, 2 * KC)
            for half in range(2):
                for n in range(0, 12 * AC, 2):
                    x = half * 12 * AC + n
                    g = (1, 2, 0)[n // AC % 3]
                    act.wait_ge(ktr_pe, x + 1)
                    if x >= RING:
                        act.wait_ge(ss_pe, x - RING + 1)
                    act.activation(kTs[:, x % RING, 0:P * kv_tiles(g)], psum[:, 0, 0:P * kv_tiles(g)],
                                   ACT.Copy).then_inc(ktr_act, 1)
                    if half == 0 and n % 4 == 0 and n // 4 < KC:
                        act.activation(ybHi[:, n // 4, :], yb[:, n // 4, :], ACT.Copy).then_inc(yo_hi, 1)
                act.wait_ge(ss_nb, half + 1)
                act.activation(ps_[:, half], ps_[:, half], ACT.Exp, bias=sst[:, half, 1:2], scale=SCALE,
                               accum_out=sst[:, half, 2:3]).then_inc(ss_exp, 1)

            act.wait_ge(so_ev, 4)
            act.wait_ge(vn_out, 16 * GROUPS)
            act.activation(oHi[:, :, :], oT[:, :, :], ACT.Copy).then_inc(yo_hi, 1)
            with act.Fori(0, KC) as f:
                for j in range(RING):
                    split_hi(None, (j + LEAD) % RING, 16 * f + 16 * ((C0 + j + LEAD) // RING + 1), 8 * f + 2 * (C0 + j))
                    for t in range(2):
                        act.wait_ge(grp, 8 * f + (2 * (C0 + j) + t + 1))
                        if j < 2:
                            act.wait_ge(g_m2, 2 * f + (t + 1))
                        else:
                            act.wait_ge(g_m1, 2 * f + (t + 3))
                        act.activation((gsg if j % 2 else gyc)[:, t, :], psum[:, t, 0:HALF],
                                       ACT.Sigmoid if j % 2 else ACT.Copy).then_inc(bank_free[t], 1)
            split_hi_at(D0 + LEAD)
            for f in range(KC):
                if D0 + LEAD + 1 + f < N_P:
                    split_hi_at(D0 + LEAD + 1 + f)
                act.wait_ge(x2_half, f + 1)
                act.wait_ge(x2_done, f + 1)
                if f:
                    act.wait_ge(ss2_done, (TILES + 1) * f)
                for tt in range(TILES + 1):
                    n = P if tt < TILES else NS
                    act.activation(sqj[0:n, tt, :], x2[0:n, tt, P * f:P * f + P], ACT.Square,
                                   accum_out=sqp[0:n, tt, f:f + 1]).then_inc(ss2_done, 1)
            act.wait_ge(ms_done, 2)
            act.activation(rstd[:, :], stat[:, :], ACT.Sqrt).then_inc(sqrt_done, 1)
            for tt in range(TILES + 1):
                n = P if tt < TILES else NS
                act.wait_ge(h2T_pe, tt + 1)
                if tt >= 2:
                    act.wait_ge(lg_pe, tt - 1)
                src = psum[:, 2 * (tt % 2):2 * (tt % 2) + 2, :].rearrange("p b (k n) -> p (b k) n", n=P)
                act.activation(h2T[:, tt % 2, :, 0:n], src[:, :, 0:n], ACT.Copy).then_inc(h2T_ev, 1)
            act.wait_ge(rt_dve, 1)
            act.activation(rt[:, 1], rt[:, 0], ACT.Exp).then_inc(rt_act, 1)
            act.wait_ge(rt_dve, 2)
            act.activation(rs1[:, 0], rs1[:, 11], ACT.Exp).then_inc(rt_act, 1)

            act.wait_ge(tab_done, 1)
            pairs = act.value_load(tab[0:1, TABLE:TABLE + 1], min_val=NE // 2, max_val=MAX_PAIRS)
            act.sem_inc(ye_ev0, 1)
            act.sem_inc(ye_out[0], 16)
            act.sem_inc(ye_out[1], 16)
            with act.Fori(0, pairs) as jp:
                for q in range(2):
                    act.wait_ge(a_pe, 2 * jp + (q + 1))
                    act.wait_ge(hid_done, 2 * jp + (q + 1))
                    act.activation(sil[:, q].rearrange("p f n -> p (f n)"), psum[:, 2 + q, 0:FC * TS],
                                   ACT.Silu).then_inc(sil_done, 1)
                    act.wait_ge(e2_in[q], 16 * jp + 16)
                    act.wait_ge(ye_pe, 4 * jp + (2 * q + 4))
                    for n in range(2):
                        cols = slice(512 * n, 512 * n + 512)
                        act.activation(e2Hi[:, :, cols], e2[:, q, :, cols], ACT.Copy).then_inc(hi_done, 1)
                    act.wait_ge(ye_pe, 4 * jp + (2 * q + 5))
                    act.wait_ge(ye_out[q], 16 * jp + 16)
                    act.activation(yev[:, q, 0:512], psum[0:TS, 6, :], ACT.Copy).then_inc(ye_ev0, 1)
                    act.wait_ge(ye_ev0, 2 * jp + (q + 2))
                    act.wait_ge(ye_ev1, 2 * jp + (q + 2))
                    act.dma_start(y_rows[bass.ds((2 * jp + q) * TS, TS), :], yev[:, q, :]).then_inc(ye_out[q], 16)
            def first_choice(tt):
                n = P if tt < TILES else NS
                act.wait_ge(yg_in[tt], 32)
                act.activation(ya[0:n, tt], ya[0:n, tt], ACT.Copy, scale=cw[0:n, 0, tt:tt + 1]).then_inc(ya_done, 1)

            first_choice(0)
            for tt in range(TILES + 2):
                if tt:
                    a = tt - 1
                    n = P if a < TILES else NS
                    act.wait_ge(f_mix, a + 1)
                    if a:
                        act.wait_ge(f_sq, a)
                    act.activation(junk3[0:n, :], x2[0:n, a, :], ACT.Square,
                                   accum_out=stat[0:n, a:a + 1]).then_inc(f_sq, 1)
                if tt < TILES:
                    first_choice(tt + 1)
                if tt:
                    act.wait_ge(ms_done, a + 3)
                    act.activation(rstd[0:n, a:a + 1], stat[0:n, a:a + 1], ACT.Sqrt).then_inc(sqrt_done, 1)
                    act.wait_ge(rec_done, a + 3)
                    act.activation(x2[0:n, a, :], x2[0:n, a, :], ACT.Copy, scale=rstd[0:n, a:a + 1]).then_inc(xn_done, 1)

        @block.vector
        def _(dve):
            local = [0]

            def own(ins):
                local[0] += 1
                ins.then_inc(dve_local, 1)
                dve.wait_ge(dve_local, local[0])

            own(dve.memset(stat[:, :], 1.0))
            dve.sem_inc(ada_ev, 2)
            dve.sem_inc(mrow_done, 2)
            dve.wait_ge(first_T, 1)
            dve.tensor_copy(small[:, 0:88], psum[:, 0, 0:88]).then_inc(first_ev, 1)
            dve.wait_ge(first_T, 2)
            dve.tensor_copy(cT[:, :, :], psum[:, 1, 0:128].rearrange("p (k n) -> p k n", n=16)[:, :, 0:9])\
               .then_inc(first_ev, 1)
            dve.wait_ge(first_T, 3)
            dve.tensor_copy(stT[:, :, :], psum[:, 2, 0:128].rearrange("p (k n) -> p k n", n=16)).then_inc(first_ev, 1)
            dve.wait_ge(first_ev, 3)
            def split_lo(slot, count):
                dve.wait_ge(hi_done, count)
                dve.tensor_tensor(wlo[:, slot], wraw[:, slot], whi[:, slot].bitcast(F32), ALU.subtract)\
                   .then_inc(lo_done, 1)

            for i in range(ADA_FIRST // RING):
                for h in range(2):
                    dve.wait_ge(ada_pe, 4 * i + 2 * h + 2)
                    dve.tensor_copy(mrow[:, h, :], psum[0:9, 4 + h, 0:2 * P]).then_inc(mrow_done, 1)
                for h in range(2):
                    dve.wait_ge(mT_pe, 2 * i + h + 1)
                    n = 4 * i + 2 * h
                    dve.tensor_tensor(modT[:, n:n + 2, :],
                                      psum[:, 6 + h, 0:32].rearrange("p (k n) -> p k n", n=16)[:, :, 0:9],
                                      small[:, n:n + 2].unsqueeze(2).to_broadcast([P, 2, 9]),
                                      ALU.add).then_inc(ada_ev, 1)
                if i == 0:
                    dve.wait_ge(sq_done, TILES + 1)
                    dve.tensor_scalar(stat[:, :], stat[:, :], 1.0 / D, EPS, ALU.mult, ALU.add).then_inc(ms_done, 1)
                    dve.wait_ge(sqrt_done, 1)
                    dve.reciprocal(rstd[:, :], rstd[:, :]).then_inc(rec_done, 1)
            dve.wait_ge(ada_ev, 2 + ADA_FIRST // 2)
            own(dve.tensor_scalar(A1[:, :, :], modT[:, KC:2 * KC, :], 1.0, None, ALU.add))
            own(dve.tensor_tensor(A1[:, :, :], A1[:, :, :], small[:, 48:56].unsqueeze(2).to_broadcast([P, KC, 9]),
                                  ALU.mult))
            dve.sem_inc(rec_done, 1)
            def modulate(tt):
                if tt > TILES:
                    return
                s = tt % 2
                dve.wait_ge(xT_pe, tt + 1)
                if tt >= 2:
                    dve.wait_ge(hlo_done, tt - 1)
                if tt < TILES:
                    for k in range(KC // 2):
                        ins = dve.tensor_scalar(hraw[:, s, k, :], psum[:, 2 * s, P * k:P * k + P],
                                                A1[:, k, 0:1], modT[:, k, 0:1], ALU.mult, ALU.add)
                    ins.then_inc(hraw_done, 1)
                else:
                    for k in range(0, KC, 4):
                        src = psum[:, 2 * s + k // 4, :].rearrange("p (k n) -> p k n", n=P)[:, :, 0:NS]\
                            .rearrange("p k (b q) -> p k b q", q=DEC_T)
                        dst = hraw[:, s, k:k + 4, 0:NS].rearrange("p k (b q) -> p k b q", q=DEC_T)
                        shape = [P, 4, DEC_B, DEC_T]
                        own(dve.tensor_tensor(dst, src, A1[:, k:k + 4, 1:9].unsqueeze(3).to_broadcast(shape), ALU.mult))
                        own(dve.tensor_tensor(dst, dst, modT[:, k:k + 4, 1:9].unsqueeze(3).to_broadcast(shape),
                                              ALU.add))
                    dve.sem_inc(hraw_done, 1)

            modulate(0)
            for tt in range(TILES + 1):
                s, n = tt % 2, P if tt < TILES else NS
                modulate(tt + 1)
                dve.wait_ge(hraw_done, tt + 1)
                dve.wait_ge(hraw_act, min(tt + 1, TILES))
                dve.wait_ge(hhi_done, tt + 1)
                dve.tensor_tensor(hLo[:, :, P * tt:P * tt + n], hraw[:, s, :, 0:n],
                                  hHi[:, :, P * tt:P * tt + n].bitcast(F32), ALU.subtract).then_inc(hlo_done, 1)
                if 1 <= tt <= LEAD:
                    split_lo((tt - 1) % RING, tt)

            def rope_add(G):
                m, t = divmod(G, 2)
                c, j = divmod(m, 9)
                g, kv = divmod(j, 3)
                R = 4 * (m // 3) + 2 * kv + t
                dve.wait_ge(rot_done, 2 * R + 2)
                if c >= 2:
                    dve.wait_ge(s_pe, UNITS * (c - 1))
                    dve.wait_ge(kn_pe, 2 * GROUPS * (c - 1))
                    dve.wait_ge(qb_done, 3 * GROUPS * (c - 1))
                dve.tensor_tensor((kT if kv else qT)[:, c % 2, g, HALF * t:HALF * t + HALF], t1[:, t, :],
                                  shb[:, t, :], ALU.add).then_inc(rope_done, 1)

            def conv(f, part):
                w = [small[:, 64 + KC * j + f:65 + KC * j + f] for j in range(3)]

                def tap(dst, src, j):
                    own(dve.scalar_tensor_tensor(dst, src, w[j], dst, ALU.mult, ALU.add))

                if part == 0:
                    if f >= 1:
                        dve.wait_ge(yb_done, 2 * f)
                    own(dve.tensor_scalar(yv[:, 0:SEQ], cu[:, 0:SEQ], w[2], None, ALU.mult))
                    tap(yv[:, P:SEQ], cu[:, 0:SEQ - P], 1)
                    return
                if part == 1:
                    conv_prompt(tap)
                    return

                own(dve.tensor_copy(ext[:, :, 0:2], stT[:, f, :].rearrange("p (b r) -> p b r", r=2)))
                own(dve.tensor_copy(ext[:, :, 2:6], cu[:, SEQ:NT].rearrange("p (b q) -> p b q", q=DEC_T)))
                ysv = yv[:, SEQ:NT].rearrange("p (b q) -> p b q", q=DEC_T)
                own(dve.tensor_scalar(ysv, ext[:, :, 2:6], w[2], None, ALU.mult))
                tap(ysv, ext[:, :, 1:5], 1)
                tap(ysv, ext[:, :, 0:4], 0)
                dve.tensor_copy(last2[:, f, 0:2], cu[:, 383:512:128]).then_inc(cu_done, 1)
                dve.tensor_copy(last2[:, f, 2:18].rearrange("p (b r) -> p b r", r=2), ext[:, :, 4:6])\
                   .then_inc(cu_done, 1)

            def conv_prompt(tap):
                tap(yv[:, 32:P], cu[:, 3 * P:SEQ - 32], 1)
                tap(yv[:, 1:32], cu[:, SEQ - 32:SEQ - 1], 1)
                tap(yv[:, 2 * P:SEQ], cu[:, 0:2 * P], 0)
                y2 = yv[:, 0:2 * P].rearrange("p (a n) -> p a n", n=P)
                c2 = cu[:, 2 * P:SEQ].rearrange("p (a n) -> p a n", n=P)
                tap(y2[:, :, 32:P], c2[:, :, 0:P - 32], 0)
                tap(y2[:, :, 1:32], c2[:, :, P - 32:P - 1], 0)

            SWAP = [i + 8 if i < 8 else i - 8 if i < 16 else i for i in range(32)]
            for G in range(2 * C0):
                m, t = divmod(G, 2)
                step = step_of(G)
                if misc_use(G, 0):
                    c, j = divmod(m - 2, 9)
                    g = j // 3
                    n = GROUPS * c + g
                    if kind(m - 2) == "k":
                        dve.wait_ge(kn_pe, 2 * n + 1)
                        if n >= 1:
                            dve.wait_ge(kn_out, 16 * n)
                        dve.tensor_copy(Kns[:, n % 2], psum[0:NS, BANK_MISC, 0:P]).then_inc(misc_ev, 1)
                        dve.wait_ge(kt_pe, n + 1)
                        if n >= 2:
                            dve.wait_ge(k_out[n % 2], 64 * (n // 2))
                        dve.tensor_copy(Kst[:, n % 2].rearrange("p a n -> p (a n)"), psum[:, BANK_KV, :])\
                           .then_inc(kt_ev, 1)
                    else:
                        dve.wait_ge(kn_pe, 2 * n + 2)
                        dve.tensor_copy(Vn[NS * g:NS * g + NS, c, :], psum[NS * g:NS * g + NS, BANK_MISC, 0:P])\
                           .then_inc(misc_ev, 1)
                if t == 0 and m + LEAD < C0:
                    split_lo((m + LEAD) % RING, m + LEAD + 1)
                if t == 0:
                    u = unit_at(step - 2)
                    if u:
                        n, c, a, h = u
                        dve.wait_ge(pvb_pe, n + 1)
                        rows_h = slice(HD * h, HD * h + HD)
                        dve.tensor_copy(oT[rows_h, c, P * a:P * a + P], psum[rows_h, BANK_O, 0:P]).then_inc(o_ev, 1)
                    u = unit_at(step)
                    if u:
                        n, c, a, h = u
                        s = n % 2
                        if n == 0:
                            dve.wait_ge(rope_in, 48)
                        dve.wait_ge(s_pe, n + 1)
                        if n >= 2:
                            dve.wait_ge(ptb_pe, n - 1)
                            dve.wait_ge(s_exp, n - 1)
                        dve.tensor_tensor_reduce(out=pr[:, s], in0=score[:, 0:KEYS_P], in1=maskp[:, a].bitcast(BF16),
                                                 scale=1.0, scalar=NEG, op0=ALU.add, op1=ALU.max,
                                                 accum_out=nmx[:, s:s + 1]).then_inc(s_mx, 1)
                        dve.wait_ge(s_mx, n + 1)
                        dve.tensor_scalar(nb[:, s:s + 1], nmx[:, s:s + 1], -SCALE, None, ALU.mult).then_inc(s_nb, 1)
                else:
                    u = unit_at(step)
                    if u:
                        s = u[0] % 2
                        dve.wait_ge(s_exp, u[0] + 1)
                        own(dve.reciprocal(ri[:, s:s + 1], rs[:, s:s + 1]))
                        dve.tensor_scalar(pr[:, s], pr[:, s], ri[:, s:s + 1], None, ALU.mult).then_inc(p_done, 1)
                    u = unit_at(step - 1)
                    if u:
                        dve.wait_ge(ptb_pe, u[0] + 1)
                        if u[0] >= 1:
                            dve.wait_ge(pvb_pe, u[0])
                        dve.tensor_copy(pTb[:, :], psum[:, BANK_PT, 0:3 * P]).then_inc(ptb_ev, 1)
                    if misc_use(G, 1):
                        n = ADA_FIRST + m
                        dve.wait_ge(ada_pe, n + 1)
                        if m >= 2:
                            dve.wait_ge(mT_pe, ADA_FIRST // 2 + m - 1)
                        dve.tensor_copy(mrow[:, (m + 1) % 2, 0:P], psum[0:9, BANK_MISC, 0:P]).then_inc(misc_ev, 1)
                if misc_use(G, 2):
                    n = ADA_FIRST + m - 1
                    dve.wait_ge(mT_pe, ADA_FIRST // 2 + m)
                    dve.tensor_scalar(modT[:, n, :], psum[:, BANK_MISC, 0:9], small[:, n:n + 1], None,
                                      ALU.add).then_inc(misc_ev, 1)
                if G >= 1 and kind((G - 1) // 2) in "qk":
                    rope_add(G - 1)
                if kind(m) in "qk":
                    R = 4 * (m // 3) + 2 * (m % 3) + t
                    dve.wait_ge(bank_free[t], m + 1)
                    dve.stream_shuffle(shb[:, t, :], rb[:, t, :], SWAP).then_inc(shuf_done, 1)
                elif kind(m) == "c":
                    f = (m - A0) // 3
                    cols = slice(HALF * t, HALF * t + HALF)
                    dve.wait_ge(grp, G + 1)
                    if f >= 1:
                        dve.wait_ge(cu_done, 2 * f)
                    dve.tensor_tensor(cu[:, cols], psum[:, t, 0:HALF], u_sb[:, t, :], ALU.mult)\
                       .then_inc(bank_free[t], 1)
                    if t == 1:
                        dve.wait_ge(bank_free[0], m + 1)
                        dve.wait_ge(bank_free[1], m + 1)
                        conv(f, 0)
                elif kind(m) == "b":
                    f = (m - A0) // 3
                    conv(f, 1 + t)
                    for n in range(2) if t == 1 else ():
                        cols = slice(HALF * n, HALF * n + HALF)
                        dve.wait_ge(bank_free[n], m + 1)
                        dve.tensor_tensor(yb[:, f, cols], gb[:, n, :], yv[:, cols], ALU.mult).then_inc(yb_done, 1)

            for m in range(C0, C0 + LEAD):
                split_lo(m % RING, m + 1)

            def normalise(half):
                dve.wait_ge(ss_exp, half + 1)
                own(dve.reciprocal(sst[:, half, 3:4], sst[:, half, 2:3]))
                dve.tensor_scalar(ps_[:, half], ps_[:, half], sst[:, half, 3:4], None, ALU.mult).then_inc(ss_p, 1)

            for half in range(2):
                for n in range(1, 12 * AC, 2):
                    x = half * 12 * AC + n
                    g = (1, 2, 0)[n // AC % 3]
                    dve.wait_ge(ktr_pe, x + 1)
                    if x >= RING:
                        dve.wait_ge(ss_pe, x - RING + 1)
                    dve.tensor_copy(kTs[:, x % RING, 0:P * kv_tiles(g)], psum[:, 1, 0:P * kv_tiles(g)])\
                       .then_inc(ktr_dve, 1)
                    if half == 0 and n % 4 == 3 and n // 4 < KC:
                        dve.wait_ge(yo_hi, n // 4 + 1)
                        dve.tensor_tensor(ybLo[:, n // 4, :], yb[:, n // 4, :], ybHi[:, n // 4, :].bitcast(F32),
                                          ALU.subtract).then_inc(yo_lo, 1)
                    if half == 1 and n == 9:
                        normalise(0)
                dve.wait_ge(mask_in, 16)
                dve.wait_ge(ssn_pe, half + 1)
                dve.tensor_tensor_reduce(out=ps_[:, half], in0=score_s[half][:, 0:KEYS_S],
                                         in1=masks[:, half].bitcast(BF16), scale=1.0, scalar=NEG, op0=ALU.add,
                                         op1=ALU.max, accum_out=sst[:, half, 0:1]).then_inc(ss_mx, 1)
                dve.wait_ge(ss_mx, half + 1)
                dve.tensor_scalar(sst[:, half, 1:2], sst[:, half, 0:1], -SCALE, None, ALU.mult).then_inc(ss_nb, 1)
            dve.wait_ge(conv_out, 32)
            for half in range(2):
                for part in range(3 * half, 3 * half + 3):
                    dve.wait_ge(spt_pe, part + 1)
                    if part % 3 < 2:
                        n = 4 * (part % 3)
                        dve.tensor_copy(pTs[half][:, n:n + 4, :].rearrange("p t n -> p (t n)"),
                                        psum[:, part % 2, :]).then_inc(spt_ev, 1)
                    else:
                        dve.tensor_copy(pTs[half][:, 8, :], psum[:, part % 2, 0:P])
                        dve.tensor_copy(pTn[half][:, :], psum[0:GROUPS * NS, part % 2, P:2 * P]).then_inc(spt_ev, 1)
                if half == 0:
                    normalise(1)
                dve.wait_ge(orow_pe, half + 1)
                dve.tensor_copy(osm[half], psum[:, 2 + half, :]).then_inc(osm_done, 1)
                dve.wait_ge(so_pe, half + 1)
                for hh in range(2):
                    part = slice(HD * hh, HD * hh + HD)
                    src = psum[part, 4, 0:P].rearrange("p (k j n) -> p k j n", k=AC, j=4)[:, :, :, 4 * hh:4 * hh + 4]
                    dst = oT[part, :, SEQ + 16 * half:SEQ + 16 * half + 16].rearrange("p k (j q) -> p k j q", q=DEC_T)
                    dve.tensor_copy(dst, src).then_inc(so_ev, 1)

            dve.wait_ge(yo_hi, KC + 1)
            dve.tensor_tensor(oLo[:, :, :], oT[:, :, :], oHi[:, :, :].bitcast(F32), ALU.subtract).then_inc(yo_lo, 1)
            dve.sem_inc(g_m1, 2)
            dve.sem_inc(g_m2, 2)
            with dve.Fori(0, KC) as f:
                for j in range(RING):
                    split_lo((j + LEAD) % RING, 4 * f + (C0 + j + LEAD + 1))
                    for t in range(2):
                        if j == 1:
                            dve.wait_ge(bank_free[t], 4 * f + (C0 + 2))
                            dve.tensor_tensor(gm1[:, t, :], gsg[:, t, :], gyc[:, t, :], ALU.mult).then_inc(g_m1, 1)
                        if j == 3:
                            cols = slice(HALF * t, HALF * t + HALF)
                            dve.wait_ge(bank_free[t], 4 * f + (C0 + 4))
                            dve.tensor_tensor(gmx[:, t, :], gsg[:, t, :], gyc[:, t, :], ALU.mult).then_inc(g_m2, 1)
                            dve.wait_ge(g_m2, 2 * f + (t + 3))
                            dve.tensor_tensor(gmx[:, t, :], gmx[:, t, :], gm1[:, t, :], ALU.add).then_inc(g_mx, 1)
                            dve.wait_ge(g_mx, 2 * f + (t + 1))
                            hi = mixHi[:, bass.ds(f, 1), cols].rearrange("p k n -> p (k n)")
                            dve.tensor_scalar(hi, gmx[:, t, :], 1.0, None, ALU.mult).then_inc(g_hi, 1)
                            dve.wait_ge(g_hi, 2 * f + (t + 1))
                            dve.tensor_tensor(mixLo[:, bass.ds(f, 1), cols].rearrange("p k n -> p (k n)"),
                                              gmx[:, t, :], hi.bitcast(F32), ALU.subtract).then_inc(g_lo, 1)
            own(dve.tensor_scalar(A2[:, :, :], modT[:, 4 * KC:5 * KC, :], 1.0, None, ALU.add))
            own(dve.tensor_tensor(A2[:, :, :], A2[:, :, :], small[:, 56:64].unsqueeze(2).to_broadcast([P, KC, 9]),
                                  ALU.mult))
            def residual(f):
                if f == 0:
                    dve.wait_ge(xr_in, 16 * (4 * TILES + 1))
                dve.wait_ge(opT_pe, f + 1)
                if f == 0:
                    own(dve.memset(sqp[:, :, :], 1.0))
                cols = slice(P * f, P * f + P)
                dve.tensor_tensor(x2[:, 0:TILES, cols], psum[:, 2 + f % 2, :].rearrange("p (a n) -> p a n", n=P),
                                  x2[:, 0:TILES, cols], ALU.add).then_inc(x2_half, 1)
                dve.tensor_tensor(x2[0:NS, TILES, cols], psum[0:NS, 4, 0:P], x2[0:NS, TILES, cols], ALU.add)\
                   .then_inc(x2_done, 1)

            for m in range(D0, N_P):
                if m + LEAD < N_P:
                    split_lo((m + LEAD) % RING, m + LEAD + 1)
                f = m - D0
                gate = modT[:, 2 * KC + f, :]
                if f >= 2:
                    dve.wait_ge(opT_pe, f - 1)
                for t in range(2):
                    dve.wait_ge(grp, 2 * m + t + 1)
                    n = HALF if t == 0 else SEQ - HALF
                    ins = dve.tensor_scalar(op[:, f % 2, HALF * t:HALF * t + n], psum[:, t, 0:n], gate[:, 0:1], None,
                                            ALU.mult)
                    if t == 1:
                        ins.then_inc(op_half, 1)
                        ins = dve.tensor_tensor(op[:, f % 2, SEQ:NT].rearrange("p (b q) -> p b q", q=DEC_T),
                                                psum[:, t, n:HALF].rearrange("p (b q) -> p b q", q=DEC_T),
                                                gate[:, 1:9].unsqueeze(2).to_broadcast([P, DEC_B, DEC_T]), ALU.mult)
                    ins.then_inc(bank_free[t], 1)
                dve.wait_ge(bank_free[0], m + 1)
                dve.wait_ge(bank_free[1], m + 1)
                dve.wait_ge(op_half, f + 1)
                dve.sem_inc(op_done, 1)
                if f < 4:
                    prm = (A2[:, :, :], modT[:, 3 * KC:4 * KC, :])[f // 2]
                    if f >= 2:
                        dve.wait_ge(bcT_pe, f - 1)
                    if f % 2 == 0:
                        dve.tensor_copy(bcp[:, :, :], prm[:, :, 0:1].to_broadcast([P, KC, P])).then_inc(bc_done, 1)
                    else:
                        dve.tensor_copy(bcs[:, :, :].rearrange("p k (b q) -> p k b q", q=DEC_T),
                                        prm[:, :, 1:9].unsqueeze(3).to_broadcast([P, KC, DEC_B, DEC_T]))\
                           .then_inc(bc_done, 1)
                if 1 <= f < 5:
                    dve.wait_ge(bcT_pe, f)
                    rows_n = P if f % 2 else NS
                    dve.tensor_copy((tokt if f % 2 else toks)[:, (f - 1) // 2, :],
                                    psum[0:rows_n, 5:7, :].rearrange("p b n -> p (b n)")).then_inc(bcT_ev, 1)
                if f >= 1:
                    residual(f - 1)
            residual(KC - 1)
            own(dve.memset(ones_b[:, :], 1.0))
            own(dve.memset(lg[:, :, :], 0.0))
            dve.wait_ge(late_in, 128)
            own(dve.tensor_copy(tri_b[:, :], tri[:, :]))
            dve.wait_ge(ss2_done, (TILES + 1) * KC)
            own(dve.tensor_reduce(stat[:, 0:TILES + 1], sqp[:, :, :], AX.X, ALU.add))
            dve.tensor_scalar(stat[:, :], stat[:, :], 1.0 / D, EPS, ALU.mult, ALU.add).then_inc(ms_done, 1)
            dve.wait_ge(sqrt_done, 2)
            own(dve.reciprocal(rstd[:, :], rstd[:, :]))
            for tt in range(TILES + 1):
                n = P if tt < TILES else NS
                tab_ = tokt if tt < TILES else toks
                own(dve.scalar_tensor_tensor(h2[0:n, tt, :], x2[0:n, tt, :], rstd[0:n, tt:tt + 1], tab_[0:n, 0, :],
                                             ALU.mult, ALU.mult))
                dve.tensor_tensor(h2[0:n, tt, :], h2[0:n, tt, :], tab_[0:n, 1, :], ALU.add).then_inc(h2_done, 1)

            for tt in range(TILES + 1):
                n = P if tt < TILES else NS
                dve.wait_ge(lg_pe, tt + 1)
                if tt >= 2:
                    dve.wait_ge(lgT_pe, tt - 1)
                dve.tensor_copy(lgT[:, tt % 2, 0:n], psum[0:20, 5 + tt % 2, 0:n]).then_inc(lgT_ev, 1)
            dve.wait_ge(lgT_pe, TILES + 1)
            own(dve.tensor_tensor(lg[:, 0:TILES, :],
                                  psum[:, 4, 0:32 * TILES].rearrange("p (t n) -> p t n", n=32)[:, :, 0:20],
                                  br[:, :].unsqueeze(1).to_broadcast([P, TILES, 20]), ALU.add))
            own(dve.tensor_tensor(lg[0:NS, TILES, :], psum[0:NS, 4, 32 * TILES:32 * TILES + 20], br[0:NS, :], ALU.add))
            tok4 = [P, 5, 4]
            rev = cst[:, 0:4].unsqueeze(1).to_broadcast(tok4)

            def first_best(values, diff, best, mark, pick, key):
                own(dve.tensor_reduce(rs1[:, best], values, AX.X, ALU.max))
                own(dve.tensor_tensor(rt[:, diff], values, rs1[:, best].unsqueeze(2).to_broadcast(tok4), ALU.subtract))
                own(dve.tensor_scalar(rt[:, mark], rt[:, diff], 0.0, None, ALU.is_equal))
                own(dve.tensor_tensor(rt[:, mark], rt[:, mark], rev, ALU.mult))
                own(dve.tensor_reduce(rs1[:, key], rt[:, mark], AX.X, ALU.max))
                own(dve.tensor_tensor(rt[:, pick], rt[:, mark], rs1[:, key].unsqueeze(2).to_broadcast(tok4),
                                      ALU.is_equal))

            first_best(lg[:, :, 0:4], 0, 3, 2, 3, 4)
            dve.sem_inc(rt_dve, 1)
            prod = onehot[:, 3].rearrange("p t (g e) -> p t g e", g=4)
            tok16 = [P, 5, 4, 4]
            own(dve.tensor_tensor(prod, lg[:, :, 4:20].rearrange("p t (g e) -> p t g e", g=4),
                                  rt[:, 3].unsqueeze(3).to_broadcast(tok16), ALU.mult))
            own(dve.tensor_reduce(rt[:, 4], prod.rearrange("p t g e -> p t e g"), AX.X, ALU.add))
            first_best(rt[:, 4], 5, 7, 7, 8, 8)
            own(dve.scalar_tensor_tensor(rt[:, 9], rt[:, 8], -1.0e30, rt[:, 4], ALU.mult, ALU.add))
            first_best(rt[:, 9], 10, 9, 12, 13, 10)
            own(dve.tensor_tensor(rs1[:, 11], rs1[:, 9], rs1[:, 7], ALU.subtract))
            dve.sem_inc(rt_dve, 1)
            for r_ in range(2):
                own(dve.tensor_tensor(onehot[:, r_].rearrange("p t (g e) -> p t g e", g=4),
                                      rt[:, 3].unsqueeze(3).to_broadcast(tok16),
                                      rt[:, 8 if r_ == 0 else 13].unsqueeze(2).to_broadcast(tok16), ALU.mult))
            dve.tensor_tensor(chosen[:, :, :], onehot[:, 0], onehot[:, 1], ALU.add).then_inc(oh_done, 1)
            dve.wait_ge(pos_pe, 1)
            own(dve.tensor_tensor(cmp6[:, :, :], psum[:, 6, 0:16].unsqueeze(2).to_broadcast([P, NE, COUNT_STEPS]),
                                  cst[:, 8:8 + COUNT_STEPS].unsqueeze(1).to_broadcast([P, NE, COUNT_STEPS]), ALU.is_gt))
            own(dve.tensor_reduce(ends[:, 0], cmp6[:, :, :], AX.X, ALU.add))
            for n, sh in enumerate((1, 2, 4, 8)):
                own(dve.tensor_copy(ends[:, n + 1, 0:sh], ends[:, n, 0:sh]))
                own(dve.tensor_tensor(ends[:, n + 1, sh:NE], ends[:, n, sh:NE], ends[:, n, 0:NE - sh], ALU.add))
            own(dve.tensor_tensor(ends[:, 5], ends[:, 4], ends[:, 0], ALU.subtract))
            own(dve.tensor_tensor(ends[:, 5], ends[:, 5], cst[:, 64:64 + NE], ALU.add))
            before = psum[:, 5, 0:80].rearrange("p (t n) -> p t n", n=16)
            own(dve.scalar_tensor_tensor(onehot[:, 3], before, float(TS), ends[:, 5].unsqueeze(1).to_broadcast([P, 5, NE]),
                                         ALU.is_ge, ALU.mult))
            own(dve.tensor_tensor(onehot[:, 3], onehot[:, 3], cst[:, 80:80 + NE].unsqueeze(1).to_broadcast([P, 5, NE]),
                                  ALU.add))
            own(dve.scalar_tensor_tensor(onehot[:, 3], onehot[:, 3], float(TS), before, ALU.mult, ALU.add))
            for r_ in range(2):
                own(dve.tensor_tensor(onehot[:, 2], onehot[:, r_], onehot[:, 3], ALU.mult))
                own(dve.tensor_reduce(slotf[:, r_], onehot[:, 2], AX.X, ALU.add))
                own(dve.tensor_copy(sloti[:, r_], slotf[:, r_]))
            dve.sem_inc(slot_done, 1)
            shape = [1, TABLE, NE]
            own(dve.tensor_tensor(cmpt[:, :, :], ends[0:1, 4].unsqueeze(1).to_broadcast(shape),
                                  cst[0:1, 32:32 + TABLE].unsqueeze(2).to_broadcast(shape), ALU.is_le))
            own(dve.tensor_reduce(eidf[:, 0:TABLE], cmpt[:, :, :], AX.X, ALU.add))
            own(dve.tensor_scalar(eidf[:, 0:TABLE], eidf[:, 0:TABLE], float(NE - 1), None, ALU.min))
            own(dve.tensor_tensor(eidf[:, 0:NE], eidf[:, 0:NE], cst[0:1, 80:80 + NE], ALU.add))
            own(dve.tensor_copy(tab[:, 0:TABLE], eidf[:, 0:TABLE]))
            more = MAX_PAIRS - NE // 2
            own(dve.tensor_tensor(eidf[:, 32:32 + more], ends[0:1, 4, NE - 1:NE].to_broadcast([1, more]),
                                  cst[0:1, 16:16 + more], ALU.is_gt))
            own(dve.tensor_reduce(eidf[:, 47:48], eidf[:, 32:32 + more], AX.X, ALU.add))
            own(dve.tensor_scalar(eidf[:, 47:48], eidf[:, 47:48], float(NE // 2), None, ALU.add))
            own(dve.tensor_copy(tab[:, TABLE:TABLE + 1], eidf[:, 47:48]))
            dve.sem_inc(tab_done, 1)
            dve.wait_ge(ada_pe, ADA_ALL)
            dve.wait_ge(late_in, 128)
            dve.tensor_tensor(gate2[:, :], psum[0:9, 2:4, :].rearrange("p b n -> p (b n)"), gate2[:, :], ALU.add)\
               .then_inc(mrow_done, 1)
            dve.wait_ge(rt_act, 1)
            own(dve.tensor_reduce(rs1[:, 5], rt[:, 1], AX.X, ALU.add))
            own(dve.reciprocal(rs1[:, 6], rs1[:, 5]))
            dve.wait_ge(rt_act, 2)
            own(dve.tensor_scalar(rs1[:, 1], rs1[:, 0], 1.0, None, ALU.add))
            own(dve.reciprocal(rs1[:, 2], rs1[:, 1]))
            own(dve.tensor_tensor(cw[:, 0], rs1[:, 6], rs1[:, 2], ALU.mult))
            own(dve.tensor_tensor(cw[:, 1], cw[:, 0], rs1[:, 0], ALU.mult))

            pairs = dve.value_load(tab[0:1, TABLE:TABLE + 1], min_val=NE // 2, max_val=MAX_PAIRS)
            dve.sem_inc(hid_done, 2)
            dve.sem_inc(ye_ev1, 1)

            def rows_T_copy(slot):
                dve.tensor_copy(xgT[:, slot, 0:4, :].rearrange("p k n -> p (k n)"), psum[:, 0, 0:4 * TS])\
                   .then_inc(xgT_ev, 1)
                dve.tensor_copy(xgT[:, slot, 4:8, :].rearrange("p k n -> p (k n)"), psum[:, 1, 0:4 * TS])\
                   .then_inc(xgT_ev, 1)

            dve.wait_ge(xgT_pe, 2)
            rows_T_copy(0)
            dve.wait_ge(bcT_pe, 5)
            dve.tensor_copy(tokt[:, 2, :], psum[:, 6:8, :].rearrange("p b n -> p (b n)")).then_inc(bcT_ev, 1)
            dve.wait_ge(bcT_pe, 6)
            for n, bank in enumerate((3, 5)):
                dve.tensor_copy(toks[:, 2, 512 * n:512 * n + 512], psum[0:NS, bank, :]).then_inc(bcT_ev, 1)
            dve.wait_ge(bcT_ev, 7)
            with dve.Fori(0, pairs) as jp:
                for q in range(2):
                    for n in range(2):
                        cols = slice(512 * n, 512 * n + 512)
                        dve.wait_ge(hi_done, 4 * jp + (N_P + 2 * q + n + 1))
                        dve.tensor_tensor(e2Lo[:, q, :, cols], e2[:, q, :, cols], e2Hi[:, :, cols].bitcast(F32),
                                          ALU.subtract).then_inc(lo_done, 1)
                    dve.wait_ge(sil_done, 2 * jp + (q + 1))
                    dve.wait_ge(ab_pe, 2 * jp + (q + 3))
                    dve.wait_ge(ye_pe, 4 * jp + (2 * q + 4))
                    s_q = sil[:, q].rearrange("p f n -> p (f n)")
                    h_q = hid[:, q].rearrange("p f n -> p (f n)")
                    hi = hidHi[:, :, :].rearrange("p f n -> p (f n)")
                    dve.tensor_tensor(hi, s_q, psum[:, 4 + q, 0:FC * TS], ALU.mult).then_inc(hid_done, 1)
                    dve.tensor_tensor(h_q, s_q, psum[:, 4 + q, 0:FC * TS], ALU.mult).then_inc(g_hi, 1)
                    dve.wait_ge(hid_done, 2 * jp + (q + 3))
                    dve.wait_ge(g_hi, 2 * jp + (2 * KC + q + 1))
                    dve.tensor_tensor(hidLo[:, q].rearrange("p f n -> p (f n)"), h_q, hi.bitcast(F32),
                                      ALU.subtract).then_inc(g_lo, 1)
                    dve.wait_ge(xgT_pe, 2 * jp + (q + 3))
                    rows_T_copy(1 - q)
                    dve.wait_ge(ye_pe, 4 * jp + (2 * q + 6))
                    dve.wait_ge(ye_out[q], 16 * jp + 16)
                    dve.tensor_copy(yev[:, q, 512:1024], psum[0:TS, 7, :]).then_inc(ye_ev1, 1)

            dve.wait_ge(nf_in, 16)
            for tt in range(TILES + 2):
                a = tt - 1
                m = P if a < TILES else NS
                if tt <= TILES:
                    n = P if tt < TILES else NS
                    tab_ = tokt if tt < TILES else toks
                    dve.wait_ge(yg_in[tt], 32)
                    dve.wait_ge(ya_done, tt + 1)
                    own(dve.scalar_tensor_tensor(ya[0:n, tt], yb2[0:n, tt], cw[0:n, 1, tt:tt + 1], ya[0:n, tt],
                                                 ALU.mult, ALU.add))
                if tt:
                    dve.wait_ge(f_sq, a + 1)
                    dve.tensor_scalar(stat[0:m, a:a + 1], stat[0:m, a:a + 1], 1.0 / D, EPS, ALU.mult, ALU.add)\
                       .then_inc(ms_done, 1)
                if tt <= TILES:
                    own(dve.tensor_tensor(ya[0:n, tt], ya[0:n, tt], tab_[0:n, 2, :], ALU.mult))
                if tt:
                    dve.wait_ge(sqrt_done, a + 3)
                    dve.reciprocal(rstd[0:m, a:a + 1], rstd[0:m, a:a + 1]).then_inc(rec_done, 1)
                if tt <= TILES:
                    dve.tensor_tensor(x2[0:n, tt, :], x2[0:n, tt, :], ya[0:n, tt], ALU.add).then_inc(f_mix, 1)

        @block.gpsimd
        def _(pool):
            pool.memset(zrow[:, :], 0.0).then_inc(zrow_done, 1)
            pool.memset(QB[:, :, :, :, :], 0.0).then_inc(qb_zero, 1)
            pool.wait_ge(qb_zero, 1)
            prompt_v = [[prompt_kv[g][kv][0, 0].rearrange("(n b a) h d -> b n a (h d)", b=4, a=TILES)
                         for kv in range(2)] for g in range(GROUPS)]

            def store(g, kv, c, src, done):
                lo = 24 if g == 0 else 0
                for b in range(4):
                    pool.dma_start(prompt_v[g][kv][b][:, :, P * c:P * c + P], src[32 * b + lo:32 * b + 32])\
                        .then_inc(done, 16)

            rotated = 0
            for G in range(2 * B_P + 8):
                m, t = divmod(G, 2)
                if m < B_P and kind(m) in "qk":
                    R = 4 * (m // 3) + 2 * (m % 3) + t
                    cols = slice(HALF * t, HALF * t + HALF)
                    if R == 0:
                        pool.wait_ge(rope_in, 48)
                    pool.wait_ge(bank_free[t], m + 1)
                    if R >= 2:
                        pool.wait_ge(rope_done, R - 1)
                    pool.tensor_tensor(t1[:, t, :], rb[:, t, :], ropec[:, cols], ALU.mult).then_inc(rot_done, 1)
                    pool.wait_ge(shuf_done, R + 1)
                    pool.tensor_tensor(shb[:, t, :], shb[:, t, :], ropes[:, cols], ALU.mult)\
                        .then_inc(rot_done, 1)
                    rotated += 2
                if t == 0 and 1 <= m and m - 1 < B_P and kind(m - 1) in "qk":
                    c, j = divmod(m - 1, 9)
                    g, kv = divmod(j, 3)
                    pool.wait_ge(rope_done, 4 * ((m - 1) // 3) + 2 * kv + 2)
                    if kv == 0:
                        pool.wait_ge(rot_done, rotated)
                        for h in range(2):
                            part = slice(HD * h, HD * h + HD)
                            pool.tensor_copy(QB[part, g, c, :, 8 * c + 4 * h:8 * c + 4 * h + 4],
                                             qT[part, c % 2, g, SEQ:NT].rearrange("p (b q) -> p b q", q=DEC_T))\
                                .then_inc(qb_done, 1)
                            pool.wait_ge(qb_done, 3 * ((m - 1) // 3) + h + 1)
                    else:
                        pool.tensor_copy(kTn[:, g, c, :], kT[:, c % 2, g, SEQ:NT]).then_inc(qb_done, 1)
                if t == 1 and 2 <= m < B_P + 2 and kind(m - 2) in "kv":
                    c, j = divmod(m - 2, 9)
                    g = j // 3
                    n = GROUPS * c + g
                    if kind(m - 2) == "k":
                        pool.wait_ge(kt_ev, n + 1)
                        store(g, 0, c, Kst[:, n % 2], k_out[n % 2])
                        pool.wait_ge(misc_ev, MISC[G - 1, 0] + 1)
                        pool.dma_start(kn_rows[g, :, P * c:P * c + P], Kns[:, n % 2]).then_inc(kn_out, 16)
                    else:
                        pool.wait_ge(vt_ev, n + 1)
                        store(g, 1, c, Vt[:, c % 2, :, g, :], v_out[c % 2])
            pool.wait_ge(misc_ev, MISC_ALL)
            for g in range(GROUPS):
                pool.dma_start(vn_rows[g], Vn[NS * g:NS * g + NS].rearrange("p c n -> p (c n)")).then_inc(vn_out, 16)
            pool.wait_ge(vn_out, 16 * GROUPS)
            pool.wait_ge(kn_out, 16 * GROUPS * AC)
            for g in range(GROUPS):
                for kv, src in enumerate((kn_rows, vn_rows)):
                    dst = sample_kv[g][kv][0, :, WINDOWS[g] - DEC_T:].rearrange("b q h d -> b (q h d)")
                    pool.dma_start(dst, src[g].rearrange("(b q) n -> b (q n)", q=DEC_T)).then_inc(tail_out, 16)
            pool.wait_ge(lt_ev, 2)
            pool.dma_start(conv_p[0, 0], ltok[0:2, :]).then_inc(conv_out, 16)
            pool.dma_start(conv_s[0].rearrange("b r c -> (b r) c"), ltok[2:18, :]).then_inc(conv_out, 16)
            pool.wait_ge(conv_out, 32)
            pool.wait_ge(xz_out, 16 * (C0 - SHIFTS_AB))
            pool.wait_ge(slot_done, 1)
            pool.wait_ge(h2_done, TILES + 1)
            for r_ in range(2):
                for tt in range(TILES + 1):
                    n = P if tt < TILES else NS
                    pool.indirect_dma_start(x_rows, bass.IndirectOffsetOnAxis(sloti[0:n, r_, tt:tt + 1], 0),
                                            h2[0:n, tt, :], None).then_inc(disp_out, 16)
            pool.wait_ge(tab_done, 1)
            pairs = pool.value_load(tab[0:1, TABLE:TABLE + 1], min_val=NE // 2, max_val=MAX_PAIRS)
            for k in range(2):
                pool.wait_ge(ye_out[k], 16 * pairs + 16)
                pool.sem_inc(all_stored, 1)
            for tt in range(TILES + 1):
                n = P if tt < TILES else NS
                for r_, dst in enumerate((ya, yb2)):
                    pool.indirect_dma_start(dst[0:n, tt], None, y_rows,
                                            bass.IndirectOffsetOnAxis(sloti[0:n, r_, tt:tt + 1], 0))\
                        .then_inc(yg_in[tt], 16)
            pool.wait_ge(nf_in, 16)
            for tt in range(TILES + 1):
                n = P if tt < TILES else NS
                pool.wait_ge(xn_done, TILES + 2 + tt)
                pool.tensor_tensor(x2[0:n, tt, :], x2[0:n, tt, :], tokt[0:n, 0, :], ALU.mult).then_inc(f_y, 1)


_INS = ['x_prompt', 'x_sample', 'cache_k1', 'cache_v1', 'cache_k2', 'cache_v2', 'cache_k3', 'cache_v3', 'state_conv',
        'c_prompt', 'c_sample', 'norm1_g', 'norm2_g', 'normf_g', 'w_ada', 'b_ada', 'w_in', 'conv_w', 'w_conv_out',
        'w_attn_out', 'w_o', 'w_rg', 'b_rg', 'w_re', 'b_re', 'w1', 'w3', 'w2']


def _kv(b, rows):
    return (1, b, rows, HEADS, HD)


_OUTS = [(1, SEQ, D), (DEC_B, DEC_T, D)] \
    + [_kv(1, min(w, SEQ)) for w in WINDOWS for _ in range(2)] + [(1, 1, 2, D)] \
    + [_kv(DEC_B, w) for w in WINDOWS for _ in range(2)] + [(1, DEC_B, 2, D)]


def _constants():
    import numpy as np

    col = np.arange(SEQ)
    time = 16 * (col % 32) + 4 * (col // 32 % 4) + col // P
    pos = np.concatenate([time, 2048 + np.arange(NS) % DEC_T]).astype(np.float32)
    freq = np.power(np.float32(500000.0), -np.arange(ROT, dtype=np.float32) / np.float32(ROT)).astype(np.float32)
    ang = (pos[:, None] * freq[None, :]).astype(np.float32).astype(np.float64)
    ropec = np.ones((P, NT), np.float32)
    ropes = np.zeros((P, NT), np.float32)
    for h in range(2):
        for i in range(ROT):
            for s, sign in ((0, -1.0), (ROT, 1.0)):
                ropec[HD * h + s + i] = np.cos(ang[:, i])
                ropes[HD * h + s + i] = sign * np.sin(ang[:, i])
    off = np.float32(-1.0e30)
    maskp = np.full((P, TILES, KEYS_P), off, np.float32)
    for a in range(TILES):
        tq = time[P * a:P * a + P][:, None]
        back = tq - time[None, :]
        maskp[:, a, 0:SEQ][(back >= 0) & (back <= WINDOWS[0])] = 0
        back = tq - time[P * a:P * a + P][None, :]
        for g, dil in ((1, 4), (2, 16)):
            view = maskp[:, a, SEQ + P * (g - 1):SEQ + P * g]
            view[(back >= 0) & (back % dil == 0) & (back <= WINDOWS[g])] = 0
    masks = np.full((P, 2, KEYS_S), off, np.float32)
    part = np.arange(P)
    j, q = part // NS, part % DEC_T
    row = np.arange(P)
    for half in range(2):
        m = masks[:, half]
        for r in range(DEC_T):
            m[q == r, P * r:P * r + P] = 0
            m[q == r, 4 * P + P * r:4 * P + P * r + P] = 0
        m[:, 8 * P:9 * P][row[None, :] >= q[:, None]] = 0
        new = np.arange(NS)
        own = (new // DEC_T)[None, :] == 4 * half + j[:, None]
        for g in range(GROUPS):
            ok = own & ((new % DEC_T)[None, :] <= q[:, None] if g == 0 else (new % DEC_T)[None, :] == q[:, None])
            m[:, 9 * P + NS * g:9 * P + NS * g + NS][ok] = 0
    small = np.zeros((P, 96), np.float32)
    small[:, 0:4] = [4, 3, 2, 1]
    small[:, 8:8 + COUNT_STEPS] = TS * np.arange(1, COUNT_STEPS + 1)
    small[:, 16:32] = 2 * np.arange(16)
    small[:, 32:32 + TABLE] = np.arange(TABLE) - NE
    small[:, 64:64 + NE] = NE - 1 - np.arange(NE)
    small[:, 80:80 + NE] = np.arange(NE)
    bf = lambda a: (np.ascontiguousarray(a).view(np.uint32) >> 16).astype(np.uint16)
    sel = np.zeros((9, P + NS), np.float32)
    sel[0, 0:P] = 1
    sel[1 + np.arange(NS) // DEC_T, P + np.arange(NS)] = 1
    return {
        "k_ident": np.eye(P, dtype=np.float32), "k_tri": np.triu(np.ones((P, P), np.float32), 1), "k_sel": sel,
        "k_small": small, "k_ropec": ropec, "k_ropes": ropes, "k_maskp": bf(maskp), "k_masks": bf(masks),
    }


def kernel(**inputs):
    import numpy as _np
    import concourse.bacc as _bacc
    from concourse import mybir as _mybir
    from concourse.bass_utils import run_bass_kernel_spmd as _run

    nc = _bacc.Bacc("TRN2", target_bir_lowering=False, num_devices=1)
    arrays, args = {}, []
    given = {name: _np.ascontiguousarray(inputs[name]) for name in _INS}
    for name, a in {**given, **_constants()}.items():
        arrays[f"in_{name}_dram"] = a
        args.append(nc.dram_tensor(f"in_{name}_dram", a.shape, _mybir.dt.from_np(a.dtype), kind="ExternalInput").ap())
    for i, shape in enumerate(_OUTS):
        args.append(nc.dram_tensor(f"out_{i}_dram", shape, _mybir.dt.float32, kind="ExternalOutput").ap())
    _build(nc, *args)
    r = _run(nc, [arrays], core_ids=[0])
    return tuple(r.results[0][f"out_{i}_dram"] for i in range(len(_OUTS)))
```
